# Optimizing a Trainium2 kernel written in Bass

```python
import math
import jax, jax.numpy as jnp
from jax import lax
import numpy as np

D_MODEL = 1024
BATCH = 1
SEQ = 512
DEPTH = 2
DEC_BATCH = 8
DEC_SEQ = 4
PAST_LEN = 1024
PAGE_SIZE = 128

N_META = 16
CHUNK = 128
M_HEADS = 4
M_DK = 128
M_DV = 128
F_HEADS = 8
F_DH = 64
R_HEADS = 4
R_DK = 128
R_DV = 128
ROPE_BASE = 10000.0
LRU_WIDTH = 512
LRU_BLOCKS = 8
LRU_BDIM = LRU_WIDTH // LRU_BLOCKS
LRU_C = 8.0
CONV_W = 4
D_FF = ((8 * D_MODEL // 3 + 255) // 256) * 256
EVEN_COLS = (M_HEADS * M_DK, M_HEADS * M_DK, M_HEADS * M_DV, M_HEADS * M_DV, M_HEADS, M_HEADS,
             F_HEADS * F_DH, F_HEADS * F_DH, F_HEADS * F_DH, F_HEADS)
ODD_COLS = (R_HEADS * R_DK, R_HEADS * R_DK, R_HEADS * R_DV, R_HEADS * R_DV, LRU_WIDTH, LRU_WIDTH)
MIX_EVEN = M_HEADS * M_DV + F_HEADS * F_DH
MIX_ODD = R_HEADS * R_DV + LRU_WIDTH
EPS = 1e-6

kernel_name = "hybrid_mlstm_fox_retnet_rglru_decode_step"

def _split(z, widths):
    idx = [int(i) for i in np.cumsum(widths)[:-1]]
    return jnp.split(z, idx, axis=-1)

def rmsnorm(x, g):
    xf = x.astype(jnp.float32)
    y = xf * lax.rsqrt(jnp.mean(xf * xf, axis=-1, keepdims=True) + EPS) * g.astype(jnp.float32)
    return y.astype(x.dtype)

def swiglu(x, wg, wu, wd):
    return (jax.nn.silu(x @ wg) * (x @ wu)) @ wd

def to_heads(t, n_heads):
    b, s, _ = t.shape
    return t.reshape(b, s, n_heads, -1).transpose(0, 2, 1, 3)

def from_heads(t):
    b, h, s, d = t.shape
    return t.transpose(0, 2, 1, 3).reshape(b, s, h * d)

def run_chunks(step, carry, seqs, lead):
    carry, out0 = step(carry, tuple(s[:, :, :lead] for s in seqs))
    rest = tuple(s[:, :, lead:] for s in seqs)
    n = rest[0].shape[2] // CHUNK
    blocks = tuple(jnp.moveaxis(s.reshape(s.shape[:2] + (n, CHUNK) + s.shape[3:]), 2, 0) for s in rest)
    carry, outs = lax.scan(step, carry, blocks)
    outs = jnp.moveaxis(outs, 0, 2)
    outs = outs.reshape(outs.shape[:2] + (n * CHUNK,) + outs.shape[4:])
    return carry, jnp.concatenate([out0, outs], axis=2)

def mlstm_chunk(carry, seqs):
    C, n, m = carry
    q, k, v, logi, logf = seqs
    L = q.shape[2]
    b = jnp.cumsum(logf, axis=-1)
    causal = jnp.tril(jnp.ones((L, L), dtype=bool))
    logD = jnp.where(causal, b[..., :, None] - b[..., None, :] + logi[..., None, :], -jnp.inf)
    m_inter = b + m[..., None]
    m_t = jnp.maximum(m_inter, jnp.max(logD, axis=-1))
    w_intra = jnp.einsum('bhtd,bhsd->bhts', q, k) * jnp.exp(logD - m_t[..., None])
    w_inter = jnp.exp(m_inter - m_t)
    num = jnp.einsum('bhts,bhsv->bhtv', w_intra, v) + w_inter[..., None] * jnp.einsum('bhtd,bhdv->bhtv', q, C)
    den = jnp.sum(w_intra, axis=-1) + w_inter * jnp.einsum('bhtd,bhd->bht', q, n)
    h = num / jnp.maximum(jnp.abs(den), jnp.exp(-m_t))[..., None]
    m_new = m_t[..., -1]
    w_src = jnp.exp(b[..., -1:] - b + logi - m_new[..., None])
    decay = jnp.exp(b[..., -1] + m - m_new)
    C_new = decay[..., None, None] * C + jnp.einsum('bhs,bhsd,bhsv->bhdv', w_src, k, v)
    n_new = decay[..., None] * n + jnp.einsum('bhs,bhsd->bhd', w_src, k)
    return (C_new, n_new, m_new), h

def _ret_log_gamma():
    return jnp.log1p(-jnp.exp2(-5.0 - jnp.arange(R_HEADS, dtype=jnp.float32)))

def retention_chunk(S, seqs):
    q, k, v = seqs
    L = q.shape[2]
    lg = _ret_log_gamma()
    t = jnp.arange(L, dtype=jnp.float32)
    diff = t[:, None] - t[None, :]
    D = jnp.exp(jnp.where(diff >= 0, diff[None] * lg[:, None, None], -jnp.inf))
    intra = jnp.einsum('bhts,bhsv->bhtv', jnp.einsum('bhtd,bhsd->bhts', q, k) * D, v)
    inter = jnp.einsum('bhtd,bhdv->bhtv', q, S) * jnp.exp((t + 1.0)[None, :] * lg[:, None])[None, :, :, None]
    w_src = jnp.exp((L - 1.0 - t)[None, :] * lg[:, None])
    S_new = jnp.exp(L * lg)[None, :, None, None] * S + jnp.einsum('bhsd,hs,bhsv->bhdv', k, w_src, v)
    return S_new, intra + inter

def rotary(x, pos):
    half = x.shape[-1] // 2
    freq = ROPE_BASE ** (-jnp.arange(half, dtype=jnp.float32) / half)
    ang = pos.astype(jnp.float32)[:, None] * freq[None, :]
    cos, sin = jnp.cos(ang), jnp.sin(ang)
    x1, x2 = x[..., :half], x[..., half:]
    return jnp.concatenate([x1 * cos - x2 * sin, x1 * sin + x2 * cos], axis=-1)

def fox_attend(q, Fq, tq, k, v, Fk, tk):
    s = jnp.einsum('bhqd,bhkd->bhqk', q, k) * (F_DH ** -0.5) + Fq[..., :, None] - Fk[..., None, :]
    s = jnp.where(tk[None, :] <= tq[:, None], s, -jnp.inf)
    return jnp.einsum('bhqk,bhkd->bhqd', jax.nn.softmax(s, axis=-1), v)

def fox_prompt(q, k, v, F):
    b, h, T, d = q.shape
    tk = jnp.arange(T)
    out0 = fox_attend(q[:, :, :N_META], F[:, :, :N_META], tk[:N_META], k, v, F, tk)
    n = (T - N_META) // CHUNK
    qb = jnp.moveaxis(q[:, :, N_META:].reshape(b, h, n, CHUNK, d), 2, 0)
    Fb = jnp.moveaxis(F[:, :, N_META:].reshape(b, h, n, CHUNK), 2, 0)
    tb = tk[N_META:].reshape(n, CHUNK)
    outs = lax.map(lambda a: fox_attend(a[0], a[1], a[2], k, v, F, tk), (qb, Fb, tb))
    outs = jnp.moveaxis(outs, 0, 2).reshape(b, h, n * CHUNK, d)
    return jnp.concatenate([out0, outs], axis=2)

def mixer_even(xn, w_in, b_mi, b_mf, b_ff, w_out, m_state, fox_past, is_prompt):
    f32 = jnp.float32
    B, T, _ = xn.shape
    mq, mk, mv, mo, mi, mf, fq, fk, fv, ff = _split(xn @ w_in, EVEN_COLS)
    q = to_heads(mq, M_HEADS).astype(f32)
    k = to_heads(mk, M_HEADS).astype(f32) * (M_DK ** -0.5)
    v = to_heads(mv, M_HEADS).astype(f32)
    logi = (mi.astype(f32) + b_mi.astype(f32)).transpose(0, 2, 1)
    logf = jax.nn.log_sigmoid(mf.astype(f32) + b_mf.astype(f32)).transpose(0, 2, 1)
    seqs = (q, k, v, logi, logf)
    if is_prompt:
        m_new, hm = run_chunks(mlstm_chunk, m_state, seqs, N_META)
    else:
        m_new, hm = mlstm_chunk(m_state, seqs)
    hm = jax.nn.sigmoid(mo.astype(f32)) * from_heads(hm)
    fk_rows = fk.reshape(B, T, F_HEADS, F_DH)
    fv_rows = fv.reshape(B, T, F_HEADS, F_DH)
    lf_rows = jax.nn.log_sigmoid(ff.astype(f32) + b_ff.astype(f32))
    qf = to_heads(fq, F_HEADS).astype(f32)
    if is_prompt:
        kf = fk_rows.astype(f32).transpose(0, 2, 1, 3)
        vf = fv_rows.astype(f32).transpose(0, 2, 1, 3)
        F = jnp.cumsum(lf_rows, axis=1).transpose(0, 2, 1)
        hf = fox_prompt(qf, kf, vf, F)
    else:
        cache_k, cache_v, cache_lf, page_table = fox_past
        past = page_table.shape[1] * PAGE_SIZE
        gather = lambda c: c[page_table].reshape((B, past) + c.shape[2:]).astype(f32)
        kf = jnp.concatenate([gather(cache_k), fk_rows.astype(f32)], axis=1).transpose(0, 2, 1, 3)
        vf = jnp.concatenate([gather(cache_v), fv_rows.astype(f32)], axis=1).transpose(0, 2, 1, 3)
        F = jnp.cumsum(jnp.concatenate([gather(cache_lf), lf_rows], axis=1), axis=1).transpose(0, 2, 1)
        tk = jnp.arange(past + T)
        hf = fox_attend(qf, F[:, :, past:], tk[past:], kf, vf, F, tk)
    out = jnp.concatenate([hm, from_heads(hf)], axis=-1).astype(xn.dtype) @ w_out
    return out, m_new, (fk_rows, fv_rows, lf_rows)

def _lin_combine(c1, c2):
    a1, b1 = c1
    a2, b2 = c2
    return a1 * a2, a2 * b1 + b2

def mixer_odd(xn, pos, w_in, ret_ln_g, conv_w, conv_b, lru_wa, lru_ba, lru_wx, lru_bx, lru_lambda, w_out,
              S, h0, conv_buf, is_prompt):
    f32 = jnp.float32
    B, T, _ = xn.shape
    rq, rk, rv, rg, lx, lgate = _split(xn @ w_in, ODD_COLS)
    q = rotary(to_heads(rq, R_HEADS).astype(f32), pos)
    k = rotary(to_heads(rk, R_HEADS).astype(f32), pos) * (R_DK ** -0.5)
    v = to_heads(rv, R_HEADS).astype(f32)
    if is_prompt:
        S_new, hr = run_chunks(retention_chunk, S, (q, k, v), N_META)
    else:
        S_new, hr = retention_chunk(S, (q, k, v))
    mu = jnp.mean(hr, axis=-1, keepdims=True)
    var = jnp.mean(jnp.square(hr - mu), axis=-1, keepdims=True)
    hr = (hr - mu) * lax.rsqrt(var + EPS) * ret_ln_g.astype(f32)[None, :, None, :]
    hr = jax.nn.silu(rg.astype(f32)) * from_heads(hr)
    u = jnp.concatenate([conv_buf.astype(f32), lx.astype(f32)], axis=1)
    xc = conv_b.astype(f32) + sum(conv_w[j].astype(f32) * u[:, j:j + T] for j in range(CONV_W))
    xb = xc.reshape(B, T, LRU_BLOCKS, LRU_BDIM)
    r = jax.nn.sigmoid(jnp.einsum('btgi,gij->btgj', xb, lru_wa.astype(f32)).reshape(B, T, LRU_WIDTH) + lru_ba.astype(f32))
    ig = jax.nn.sigmoid(jnp.einsum('btgi,gij->btgj', xb, lru_wx.astype(f32)).reshape(B, T, LRU_WIDTH) + lru_bx.astype(f32))
    log_a = -LRU_C * r * jax.nn.softplus(-lru_lambda.astype(f32))
    a = jnp.exp(log_a)
    bx = jnp.sqrt(-jnp.expm1(2.0 * log_a)) * (ig * xc)
    bx = bx.at[:, 0].add(a[:, 0] * h0)
    _, hs = lax.associative_scan(_lin_combine, (a, bx), axis=1)
    hl = hs * jax.nn.gelu(lgate.astype(f32))
    out = jnp.concatenate([hr, hl], axis=-1).astype(xn.dtype) @ w_out
    return out, S_new, hs[:, -1], u[:, -(CONV_W - 1):]

def setup_inputs(seed: int = 0) -> dict:
    key = jax.random.key(seed)
    ks = jax.random.split(key, 40)
    f32 = jnp.float32
    nrm = lambda i, shape, s=1.0: jax.random.normal(ks[i], shape, f32) * s
    n_pages = PAST_LEN // PAGE_SIZE
    used = DEC_BATCH * n_pages
    n_phys = used + max(1, used // 4)
    perm = jax.random.permutation(ks[0], n_phys)
    page_table = perm[:used].reshape(DEC_BATCH, n_pages).astype(jnp.int32)
    lam_u = jax.random.uniform(ks[30], (LRU_WIDTH,), f32, minval=0.9, maxval=0.999)
    lam_a = lam_u ** (1.0 / LRU_C)
    return {
        "x_prompt": nrm(1, (BATCH, SEQ, D_MODEL)),
        "x_sample": nrm(2, (DEC_BATCH, DEC_SEQ, D_MODEL)),
        "cache_fox_k": nrm(3, (n_phys, PAGE_SIZE, F_HEADS, F_DH)),
        "cache_fox_v": nrm(4, (n_phys, PAGE_SIZE, F_HEADS, F_DH)),
        "cache_fox_logf": jax.nn.log_sigmoid(4.0 + nrm(5, (n_phys, PAGE_SIZE, F_HEADS))),
        "state_mlstm_C": nrm(6, (DEC_BATCH, M_HEADS, M_DK, M_DV), 0.5),
        "state_mlstm_n": nrm(7, (DEC_BATCH, M_HEADS, M_DK), 0.5),
        "state_mlstm_m": nrm(8, (DEC_BATCH, M_HEADS)),
        "state_ret_S": nrm(9, (DEC_BATCH, R_HEADS, R_DK, R_DV), 0.5),
        "state_lru_h": nrm(10, (DEC_BATCH, LRU_WIDTH), 0.5),
        "state_lru_conv": nrm(11, (DEC_BATCH, CONV_W - 1, LRU_WIDTH)),
        "page_table": page_table,
        "meta_tokens": nrm(12, (N_META, D_MODEL)),
        "w_in_even": nrm(13, (D_MODEL, sum(EVEN_COLS)), D_MODEL ** -0.5),
        "b_mlstm_i": nrm(14, (M_HEADS,), 0.1),
        "b_mlstm_f": jnp.linspace(3.0, 6.0, M_HEADS, dtype=f32) + nrm(15, (M_HEADS,), 0.1),
        "b_fox_f": jnp.linspace(2.0, 6.0, F_HEADS, dtype=f32) + nrm(16, (F_HEADS,), 0.1),
        "w_out_even": nrm(17, (MIX_EVEN, D_MODEL), MIX_EVEN ** -0.5),
        "w_in_odd": nrm(18, (D_MODEL, sum(ODD_COLS)), D_MODEL ** -0.5),
        "ret_ln_g": 1.0 + nrm(19, (R_HEADS, R_DV), 0.02),
        "conv_w": nrm(20, (CONV_W, LRU_WIDTH), CONV_W ** -0.5),
        "conv_b": nrm(21, (LRU_WIDTH,), 0.02),
        "lru_wa": nrm(22, (LRU_BLOCKS, LRU_BDIM, LRU_BDIM), LRU_BDIM ** -0.5),
        "lru_ba": nrm(23, (LRU_WIDTH,), 0.02),
        "lru_wx": nrm(24, (LRU_BLOCKS, LRU_BDIM, LRU_BDIM), LRU_BDIM ** -0.5),
        "lru_bx": nrm(25, (LRU_WIDTH,), 0.02),
        "lru_lambda": jnp.log(lam_a) - jnp.log1p(-lam_a),
        "w_out_odd": nrm(26, (MIX_ODD, D_MODEL), MIX_ODD ** -0.5),
        "norm_g": 1.0 + nrm(27, (DEPTH, 4, D_MODEL), 0.02),
        "ffn_wg": nrm(28, (DEPTH, D_MODEL, D_FF), D_MODEL ** -0.5),
        "ffn_wu": nrm(29, (DEPTH, D_MODEL, D_FF), D_MODEL ** -0.5),
        "ffn_wd": nrm(31, (DEPTH, D_FF, D_MODEL), D_FF ** -0.5),
    }

def reference(x_prompt, x_sample, cache_fox_k, cache_fox_v, cache_fox_logf, state_mlstm_C, state_mlstm_n,
              state_mlstm_m, state_ret_S, state_lru_h, state_lru_conv, page_table, meta_tokens, w_in_even,
              b_mlstm_i, b_mlstm_f, b_fox_f, w_out_even, w_in_odd, ret_ln_g, conv_w, conv_b, lru_wa, lru_ba,
              lru_wx, lru_bx, lru_lambda, w_out_odd, norm_g, ffn_wg, ffn_wu, ffn_wd):
    f32 = jnp.float32

    def trunk(h, pos, m_state, fox_past, S, h0, cbuf, is_prompt):
        fox_rows = None
        for layer in range(DEPTH):
            xn = rmsnorm(h, norm_g[layer, 0])
            if layer % 2 == 0:
                mix, m_state, fox_rows = mixer_even(xn, w_in_even, b_mlstm_i, b_mlstm_f, b_fox_f, w_out_even,
                                                    m_state, fox_past, is_prompt)
            else:
                mix, S, h0, cbuf = mixer_odd(xn, pos, w_in_odd, ret_ln_g, conv_w, conv_b, lru_wa, lru_ba,
                                             lru_wx, lru_bx, lru_lambda, w_out_odd, S, h0, cbuf, is_prompt)
            h = h + rmsnorm(mix, norm_g[layer, 1])
            ff = swiglu(rmsnorm(h, norm_g[layer, 2]), ffn_wg[layer], ffn_wu[layer], ffn_wd[layer])
            h = h + rmsnorm(ff, norm_g[layer, 3])
        return h, m_state, fox_rows, S, h0, cbuf

    B = x_prompt.shape[0]
    T = x_prompt.shape[1] + N_META
    hp = jnp.concatenate([jnp.broadcast_to(meta_tokens.astype(x_prompt.dtype)[None], (B, N_META, D_MODEL)),
                          x_prompt], axis=1)
    m0 = (jnp.zeros((B, M_HEADS, M_DK, M_DV), f32), jnp.zeros((B, M_HEADS, M_DK), f32),
          jnp.zeros((B, M_HEADS), f32))
    hp, (pC, pn, pm), (pk, pv, plf), pS, ph, pcb = trunk(
        hp, jnp.arange(T), m0, None, jnp.zeros((B, R_HEADS, R_DK, R_DV), f32),
        jnp.zeros((B, LRU_WIDTH), f32), jnp.zeros((B, CONV_W - 1, LRU_WIDTH), f32), True)
    y_prompt = hp[:, N_META:]

    past = page_table.shape[1] * PAGE_SIZE
    pos_s = past + jnp.arange(x_sample.shape[1])
    ms = (state_mlstm_C.astype(f32), state_mlstm_n.astype(f32), state_mlstm_m.astype(f32))
    y_sample, (sC, sn, sm), (sk, sv, slf), sS, sh, scb = trunk(
        x_sample, pos_s, ms, (cache_fox_k, cache_fox_v, cache_fox_logf, page_table),
        state_ret_S.astype(f32), state_lru_h.astype(f32), state_lru_conv, False)

    return (y_prompt, y_sample, pk, pv, plf, sk, sv, slf, pC, pn, pm, sC, sn, sm, pS, sS, ph, sh, pcb, scb)


_drawn_inputs = setup_inputs


def setup_inputs(seed=0):
    import zlib

    import numpy as np

    out = dict(_drawn_inputs(seed))
    spreads = {}
    factors = {'ret_ln_g': 6.14, 'lru_ba': 8.0, 'lru_bx': 8.0}
    for name, (base, spread) in spreads.items():
        noise = np.random.default_rng([zlib.crc32(name.encode()), seed]).standard_normal(out[name].shape)
        drawn = base * np.exp(spread * noise) if base else spread * noise
        out[name] = __import__('jax').numpy.asarray(drawn.astype(out[name].dtype))
    for name, factor in factors.items():
        out[name] = (out[name] * factor).astype(out[name].dtype)
    return out
```

```python
from contextlib import ExitStack

import numpy as np

import concourse.bass as bass
from concourse import mybir

F32 = mybir.dt.float32
F32R = mybir.dt.float32r
I32 = mybir.dt.int32
ALU = mybir.AluOpType
ACT = mybir.ActivationFunctionType
AX_X = mybir.AxisListType.X

D = 1024
KC = D // 128
META, SEQ = 16, 512
TP = META + SEQ
NB, TS = 8, 4
NS = NB * TS
T = TP + NS
HALF = T // 2
MH = 4
FH, FD = 8, 64
FF = 2816
FC = FF // 128
PAGES, PAGE = 8, 128
PAST = PAGES * PAGE
LW = 512
NPHYS = 80
EPS = 1e-6
NEG = -1e30
QK_SCALE = 128.0 ** -0.5
FOX_SCALE = FD ** -0.5
BLK = [(0, 128), (128, 128), (256, 128), (384, 128), (512, 16), (TP, NS)]
SB = 5
RANGES = [(0, 256), (256, T)]


def constants():
    f = np.float32
    c = {}
    i = np.arange(128)
    c["ident"] = np.eye(128, dtype=f)
    c["ones"] = np.ones((128, 128), f)
    c["tri_ts"] = np.where(i[None, :] <= i[:, None], 0, NEG).astype(f)
    c["tri_st"] = (i[:, None] <= i[None, :]).astype(f)
    swap = np.zeros((128, 128), f)
    swap[i[:64] + 64, i[:64]] = -1
    swap[i[:64], i[:64] + 64] = 1
    c["swap"] = swap
    small = np.zeros((128, 16 + 4 + 64), f)
    small[:, 0:16] = np.eye(4, dtype=f).reshape(1, 16)
    q = i % 4
    small[:, 16:20] = np.where(np.arange(4)[None, :] <= q[:, None], 0, NEG)
    for g in range(2):
        own = np.repeat(np.arange(8) == 0, 4)
        for p in range(128):
            own = np.repeat(np.arange(8) == 4 * g + p // 32, 4)
            small[p, 20 + 32 * g:52 + 32 * g] = own
    c["small"] = small
    s = np.arange(32)
    sm = np.zeros((32, 40), f)
    sm[:, 0:32] = (s[:, None] // 4 == s[None, :] // 4) & (s[:, None] <= s[None, :])
    sm[:, 32:40] = s[:, None] // 4 == np.arange(8)[None, :]
    c["smask"] = sm
    pos = np.concatenate([np.arange(TP), np.tile(PAST + np.arange(TS), NB)]).astype(f)
    freq = f(10000.0) ** (-np.arange(64, dtype=f) / f(64))
    ang = freq[:, None] * pos[None, :]
    c["rope"] = np.stack([np.tile(np.cos(ang), (2, 1)), np.tile(np.sin(ang), (2, 1))], 1).astype(f)
    lg = np.log1p(-np.exp2(-5.0 - np.arange(4, dtype=f))).astype(np.float64)
    t = np.arange(TP)
    rel = t[None, :] - i[:, None]
    dec = np.zeros((128, 4, TP), f)
    dsm = np.zeros((128, 4, NS + NS + 6), f)
    for h in range(4):
        dec[:, h, :TP] = np.where(rel >= 0, np.exp(np.minimum(rel, TP) * 1.0 * lg[h]), 0)
        srel = s[None, :] - s[:, None]
        dsm[:32, h, :NS] = sm[:, 0:32] * np.exp(np.maximum(srel, 0) * lg[h])
        dsm[:, h, NS:2 * NS] = np.exp((s % 4 + 1) * lg[h])[None, :]
        for b, (t0, n) in enumerate(BLK):
            last = TP - 1 - t0 - i if b < SB else 3 - i % 4
            dsm[:, h, 2 * NS + b] = np.where(i < n, np.exp(np.maximum(last, 0) * lg[h]), 0)
    c["decay"] = dec
    c["decay_small"] = dsm
    return c


CONST_SHAPES = {k: v.shape for k, v in constants().items()}
GAMMA4 = [float(np.exp(4 * np.log1p(-np.exp2(-5.0 - h)))) for h in range(4)]


def hybrid_decoder(nc, io):
    ctx = ExitStack()
    sems = {}

    def sem(name):
        sems[name] = sems.get(name, 0) + 1
        return ctx.enter_context(nc.semaphore(f"{name}_{sems[name]}"))

    names = {}

    def place(stack, name, shape, dt=F32, side="left"):
        names[name] = names.get(name, 0) + 1
        return stack.enter_context(nc.sbuf_tensor(f"{name}_{names[name]}", shape, dt, side=side))

    def sb(name, shape, dt=F32):
        return place(ctx, name, shape, dt)

    V, A, G, PE = nc.vector, nc.scalar, nc.gpsimd, nc.tensor

    h = sb("h", [128, KC, T])
    ring = sb("ring", [128, 2, FC * 128])
    ident = sb("ident", [128, 128])
    ones = sb("ones", [128, 128])
    tri_ts = sb("tri_ts", [128, 128])
    tri_st = sb("tri_st", [128, 128])
    swap = sb("swap", [128, 128])
    small = sb("small", [128, 84])
    smask = sb("smask", [32, 40])
    cols = sb("cols", [128, 100])
    rstd = sb("rstd", [128, T])
    psum = ctx.enter_context(nc.psum_tensor("psum", [128, 8 * 512], F32))
    banks = [psum[:, i * 512:(i + 1) * 512] for i in range(8)]
    dsm = sb("dsm", [128, MH, 70])
    page_ids = sb("page_ids", [1, NB * PAGES], I32)

    onecol = small[:, 0:16].rearrange("p (h j) -> p h j", h=4)
    newmask = small[:, 16:20]
    bmask = small[:, 20:84].rearrange("p (g c) -> p g c", g=2)

    def head_row(heads, hd, m=128):
        return ident[0:heads, hd:hd + 1].to_broadcast([heads, m])

    def gain(layer, n, k):
        c = (layer * 4 + n) * 8 + k
        return cols[:, c:c + 1]

    CONVW, CONVB, LBA, LBX, LLAM, LNG = 64, 80, 84, 88, 92, 96

    w_full = [sem("w_full_even"), sem("w_full_odd")]
    high_done = [sem("w_high_done") for _ in range(2)]
    low_done = [sem("w_low_done") for _ in range(2)]
    tile_full = [sem("tile_full") for _ in range(4)]
    tile_free = [sem("tile_free") for _ in range(4)]
    silu_done = [sem("silu_done") for _ in range(2)]
    hid_split = [sem("hidden_split") for _ in range(2)]
    k_done = [sem("k_transposed") for _ in range(PAGES)]
    sent, split_n, full_n, free_n, silus = [0], [0], [1] * 4, [1] * 4, [1]
    with nc.Block() as block:
        @block.vector
        def _(dve):
            for s in tile_full + tile_free + silu_done + hid_split + k_done:
                dve.sem_inc(s, 1)

    def w_view(w):
        return w.rearrange("(k p) n -> p k n", p=128)

    def plain_unit(w, col):
        v = w_view(w)
        return lambda slot, u: [(ring[:, slot, 0:KC * 256].rearrange("p (k n) -> p k n", k=KC),
                                 v[:, :, bass.ds(u * 256 + col, 256)])]

    def down_unit(w):
        v = w_view(w)
        return lambda slot, u: [(ring[:, slot, :].rearrange("p (k n) -> p k n", k=FC),
                                 v[:, :, bass.ds(u * 128, 128)])]

    def gate_up_unit(wg, wu):
        g, u_ = w_view(wg), w_view(wu)

        def src(slot, u):
            dst = ring[:, slot, 0:2 * KC * 128].rearrange("p (a k n) -> p a k n", a=2, k=KC)
            return [(dst[:, 0], g[:, :, bass.ds(u * 128, 128)]), (dst[:, 1], u_[:, :, bass.ds(u * 128, 128)])]
        return src

    def send(sp, unit, slot, u):
        for dst, src in unit(slot, u):
            sp.dma_start(dst, src).then_inc(w_full[slot], 16)

    def prefetch(sp, unit):
        for slot in range(2):
            send(sp, unit, slot, slot)

    def project(unit, loads, iters, kc, x, dst, first, pieces, then=None, silu=None, beside=None):
        whole = kc == KC
        kp = kc if whole else kc // 2
        high, low = pieces
        wbase, s0, full0, free0, silu0 = sent[0], split_n[0], list(full_n), list(free_n), silus[0]
        per = 16 * loads

        def raw(slot, p):
            if silu is not None or not whole:
                return ring[:, slot, p * kp * 128:(p + 1) * kp * 128].rearrange("p (k n) -> p k n", k=kp)
            return ring[:, slot, 0:2 * kp * 128].rearrange("p (k a n) -> p k a n", k=kp, a=2)[:, :, p]

        def part(a, p):
            return a[:, p, 0:kp * 128].rearrange("p (k n) -> p k n", k=kp)

        def tile_of(slot, p):
            return 2 * slot + (p if whole else 1)

        def two_on(i, q):
            return (i, 1, q) if q < 2 else (i + 1, 0, q - 2)

        def turns(eng, turn):
            with eng.Fori(0, iters - 1) as i:
                turn(i, True)
            turn(iters - 1, False)

        with nc.Block() as block:
            @block.sync
            def _(sp):
                with sp.Fori(0, iters - 1) as i:
                    for slot in range(2):
                        for p in range(2):
                            sp.wait_ge(low_done[p], i * 2 + (s0 + slot + 1))
                        send(sp, unit, slot, i * 2 + (2 + slot))
                for slot in range(2):
                    for p in range(2):
                        sp.wait_ge(low_done[p], s0 + 2 * (iters - 1) + slot + 1)
                    if then is not None:
                        send(sp, then, slot, slot)

            @block.tensor
            def _(pe):
                with pe.Fori(0, iters) as i:
                    for slot in range(2):
                        for p in range(2):
                            tl = tile_of(slot, p)
                            pe.wait_ge(low_done[p], i * 2 + (s0 + slot + 1))
                            if silu is not None and p == 0:
                                pe.wait_ge(silu_done[slot], i + silu0)
                            elif whole or p == 0:
                                pe.wait_ge(tile_free[tl], i + free0[tl])
                            w_high, w_low = part(high, p), part(low, p)
                            for k in range(kp):
                                kk = k if whole else p * kp + k
                                x_high, x_low = x(kk)
                                for w, m, end in ((w_high, x_high, 0), (w_high, x_low, 0), (w_low, x_high, 1)):
                                    for half in range(2):
                                        last = nc.tensor.matmul(
                                            banks[2 * tl + half][:, 0:HALF], w[:, k, :],
                                            m[:, half * HALF:(half + 1) * HALF],
                                            start=(kk == 0 and w is w_high and m is x_high),
                                            stop=(kk == kc - 1 and end == 1))
                            last.then_inc(tile_full[2 * slot + p], 1)

            @block.scalar
            def _(act):
                def split_high(i, slot, p):
                    if p == 0:
                        act.wait_ge(w_full[slot], i * per + (wbase + per))
                    if slot:
                        act.wait_ge(tile_full[p], i + (full0[p] + 1))
                    else:
                        act.wait_ge(tile_full[2 + p], i + full0[2 + p])
                    nc.scalar.copy(part(high, p), raw(slot, p)).then_inc(high_done[p], 1)

                def turn(i, more):
                    for q in range(4):
                        if q < 2 or more:
                            split_high(*two_on(i, q))
                        slot = q // 2
                        if silu is None or q % 2:
                            continue
                        act.wait_ge(tile_full[2 * slot], i + (full0[2 * slot] + 1))
                        act.wait_ge(hid_split[slot], i + silu0)
                        for half in range(2):
                            g = nc.scalar.activation(silu[:, slot, half * HALF:(half + 1) * HALF],
                                                     banks[4 * slot + half][:, 0:HALF], ACT.Silu)
                        g.then_inc(silu_done[slot], 1)

                split_high(0, 0, 0)
                split_high(0, 0, 1)
                turns(act, turn)

            @block.vector
            def _(dve):
                def split_low(i, slot, p):
                    dve.wait_ge(high_done[p], i * 2 + (s0 + slot + 1))
                    nc.vector.tensor_tensor(part(low, p), raw(slot, p), part(high, p).bitcast(F32),
                                            ALU.subtract).then_inc(low_done[p], 1)

                def turn(i, more):
                    for q in range(4):
                        slot, p = q // 2, q % 2
                        tl = tile_of(slot, p)
                        if silu is not None and p:
                            dve.wait_ge(silu_done[slot], i + (silu0 + 1))
                            dve.wait_ge(tile_full[tl], i + (full0[tl] + 1))
                            for half in range(2):
                                c = nc.vector.tensor_tensor(silu[:, slot, half * HALF:(half + 1) * HALF],
                                                            silu[:, slot, half * HALF:(half + 1) * HALF],
                                                            banks[2 * tl + half][:, 0:HALF], ALU.mult)
                            c.then_inc(tile_free[tl], 1)
                        elif silu is None and (whole or p):
                            dve.wait_ge(tile_full[tl], i + (full0[tl] + 1))
                            step, at = (4, first + q) if whole else (2, first + slot)
                            for half in range(2):
                                c = nc.vector.tensor_copy(
                                    dst[:, bass.ds(i * step + at, 1), half * HALF:(half + 1) * HALF]
                                    .rearrange("p a t -> p (a t)"), banks[2 * tl + half][:, 0:HALF])
                            c.then_inc(tile_free[tl], 1)
                        if q < 2 or more:
                            split_low(*two_on(i, q))

                split_low(0, 0, 0)
                split_low(0, 0, 1)
                turns(dve, turn)

            @block.gpsimd
            def _(pool):
                if beside is not None:
                    beside(pool)
                if silu is None:
                    return
                with pool.Fori(0, iters) as i:
                    for slot in range(2):
                        pool.wait_ge(tile_free[2 * slot + 1], i + (free0[2 * slot + 1] + 1))
                        hh, hl = (a[:, bass.ds(i * 2 + slot, 1), :].rearrange("p a t -> p (a t)") for a in dst)
                        nc.gpsimd.tensor_copy(hh, silu[:, slot, :])
                        nc.gpsimd.drain()
                        nc.gpsimd.tensor_tensor(hl, silu[:, slot, :], hh.bitcast(F32),
                                                ALU.subtract).then_inc(hid_split[slot], 1)
        sent[0] += per * iters
        split_n[0] += 2 * iters
        for slot in range(2):
            for p in range(2):
                tl = 2 * slot + p
                full_n[tl] += iters
                if silu is None and (whole or p) or silu is not None and p:
                    free_n[tl] += iters
        if silu is not None:
            silus[0] += iters

    def put_pieces(stack):
        return [place(stack, f"w_{x}", [128, 2, FC // 2 * 128], F32R) for x in ("high", "low")]

    def put_split(stack, name, chunks, side):
        return [place(stack, f"{name}_{x}", [128, chunks, T], F32R, side) for x in ("high", "low")]

    tr_full, tr_free, tr_n = [sem("tr_full_v"), sem("tr_full_a")], [sem("tr_free_v"), sem("tr_free_a")], [0, 0]

    def transposes(jobs, sync=None):
        full, free, n0 = tr_full, tr_free, list(tr_n)
        with nc.Block() as block:
            if sync is not None:
                block.sync(sync)

            @block.tensor
            def _(pe):
                for j, (ins, _) in enumerate(jobs):
                    if j >= 8:
                        pe.wait_ge(free[j % 2], n0[j % 2] + (j - 8) // 2 + 1)
                    for src, col in ins:
                        k, m = src.shape[0], src.shape[-1]
                        last = nc.tensor.matmul(banks[j % 8][0:m, col:col + k], src, ident[0:k, 0:k],
                                                start=True, stop=True, is_transpose=True)
                    last.then_inc(full[j % 2], 1)

            @block.vector
            def _(dve):
                for j in range(0, len(jobs), 2):
                    dve.wait_ge(full[0], n0[0] + j // 2 + 1)
                    jobs[j][1](lambda d, s: nc.vector.tensor_copy(d, s), banks[j % 8]).then_inc(free[0], 1)

            @block.scalar
            def _(act):
                for j in range(1, len(jobs), 2):
                    act.wait_ge(full[1], n0[1] + j // 2 + 1)
                    jobs[j][1](lambda d, s: nc.scalar.copy(d, s), banks[j % 8]).then_inc(free[1], 1)

        tr_n[0] += (len(jobs) + 1) // 2
        tr_n[1] += len(jobs) // 2

    n_sq, n_sum, n_var, n_rstd, n_y, n_high = (sem(x) for x in (
        "sq_done", "sum_done", "inv_var", "rstd_done", "normed", "normed_high"))
    norms = [0, 0]

    def rmsnorm(src, layer, n, sq, dst=None, beside=None):
        m, highs = norms
        norms[0] += 1
        norms[1] += dst is not None
        with nc.Block() as block:
            if beside is not None:
                block.sync(beside)

            @block.scalar
            def _(act):
                for k in range(KC):
                    nc.scalar.activation(sq[:, k, :], src[:, k, :], ACT.Square).then_inc(n_sq, 1)
                act.wait_ge(n_var, m + 1)
                nc.scalar.activation(rstd[:, :], rstd[:, :], ACT.Sqrt).then_inc(n_rstd, 1)
                if dst is None:
                    return
                for k in range(KC):
                    act.wait_ge(n_y, KC * m + k + 1)
                    nc.scalar.copy(dst[0][:, k, :], sq[:, k, :]).then_inc(n_high, 1)

            @block.tensor
            def _(pe):
                for k in range(KC):
                    pe.wait_ge(n_sq, KC * m + k + 1)
                    for half in range(2):
                        last = nc.tensor.matmul(banks[half][:, 0:HALF], ones[:, :],
                                                sq[:, k, half * HALF:(half + 1) * HALF],
                                                start=(k == 0), stop=(k == KC - 1))
                last.then_inc(n_sum, 1)

            def add_or_split(eng, ne, k):
                if dst is None:
                    ne.tensor_tensor(h[:, k, :], h[:, k, :], sq[:, k, :], ALU.add)
                else:
                    eng.wait_ge(n_high, KC * highs + k + 1)
                    ne.tensor_tensor(dst[1][:, k, :], sq[:, k, :], dst[0][:, k, :].bitcast(F32), ALU.subtract)

            @block.vector
            def _(dve):
                dve.wait_ge(n_sum, m + 1)
                for half in range(2):
                    nc.vector.tensor_scalar(rstd[:, half * HALF:(half + 1) * HALF], banks[half][:, 0:HALF],
                                            1.0 / D, EPS, ALU.mult, ALU.add)
                nc.vector.drain()
                nc.vector.reciprocal(rstd[:, :], rstd[:, :]).then_inc(n_var, 1)
                dve.wait_ge(n_rstd, m + 1)
                for k in range(KC):
                    nc.vector.scalar_tensor_tensor(out=sq[:, k, :], in0=src[:, k, :], scalar=gain(layer, n, k),
                                                   in1=rstd[:, :], op0=ALU.mult, op1=ALU.mult).then_inc(n_y, 1)
                for k in range(1, KC, 2):
                    nc.vector.drain()
                    add_or_split(dve, nc.vector, k)

            @block.gpsimd
            def _(pool):
                for k in range(0, KC, 2):
                    pool.wait_ge(n_y, KC * m + k + 1)
                    add_or_split(pool, nc.gpsimd, k)

    even_a, even_b = plain_unit(io["w_in_even"], 0), plain_unit(io["w_in_even"], 2048 + 8)
    out_even, odd = plain_unit(io["w_out_even"], 0), plain_unit(io["w_in_odd"], 0)
    out_odd = plain_unit(io["w_out_odd"], 0)
    up = [gate_up_unit(io["ffn_wg"][l], io["ffn_wu"][l]) for l in range(2)]
    down = [down_unit(io["ffn_wd"][l]) for l in range(2)]

    left = ExitStack()
    xt = place(left, "tokens_in", [128, 6, D])
    params = rstd[0:100, 0:128]
    s_in, s_const = sem("x_loaded"), sem("const_loaded")
    xp, xs = io["x_prompt"][0], io["x_sample"].rearrange("b t d -> (b t) d")
    with nc.Block() as block:
        @block.sync
        def _(sp):
            sp.dma_start(ident[:, :], io["c_ident"]).then_inc(s_const, 16)
            sp.dma_start(page_ids[:, :], io["page_table"].rearrange("(a b) p -> a (b p)", a=1)).then_inc(s_const, 16)
            sp.dma_start(xt[0:META, 0, :], io["meta_tokens"]).then_inc(s_in, 16)
            sp.dma_start(xt[META:128, 0, :], xp[0:128 - META]).then_inc(s_in, 16)
            for b in range(1, SB):
                t0, n = BLK[b]
                sp.dma_start(xt[0:n, b, :], xp[t0 - META:t0 - META + n]).then_inc(s_in, 16)
            sp.dma_start(xt[0:NS, SB, :], xs).then_inc(s_in, 16)
            prefetch(sp, even_a)
            sp.wait_ge(s_in, 16 * 7)

        @block.scalar
        def _(act):
            for dst, name in ((ones, "ones"), (tri_ts, "tri_ts"), (tri_st, "tri_st"), (swap, "swap"),
                              (small, "small"), (smask, "smask")):
                act.dma_start(dst[:, :], io["c_" + name]).then_inc(s_const, 16)
            act.dma_start(dsm[:, :, :], io["c_decay_small"]).then_inc(s_const, 16)
            for r0, n, src in ((0, 64, io["norm_g"].rearrange("l n (k p) -> (l n k) p", p=128)),
                               (CONVW, 16, io["conv_w"].rearrange("j (k p) -> (j k) p", p=128)),
                               (CONVB, 4, io["conv_b"].rearrange("(k p) -> k p", p=128)),
                               (LBA, 4, io["lru_ba"].rearrange("(k p) -> k p", p=128)),
                               (LBX, 4, io["lru_bx"].rearrange("(k p) -> k p", p=128)),
                               (LLAM, 4, io["lru_lambda"].rearrange("(k p) -> k p", p=128)),
                               (LNG, 4, io["ret_ln_g"])):
                act.dma_start(params[r0:r0 + n, :], src).then_inc(s_const, 16)
            act.wait_ge(s_const, 16 * 16)

    jobs = [([(params, 0)], lambda cp, bank: cp(cols[:, :], bank[:, 0:100]))]
    for b, (t0, n) in enumerate(BLK):
        for kk in range(0, KC, 4):
            jobs.append(([(xt[0:n, b, (kk + j) * 128:(kk + j + 1) * 128], j * 128) for j in range(4)],
                         lambda cp, bank, kk=kk, t0=t0, n=n: cp(
                             h[:, kk:kk + 4, t0:t0 + n],
                             bank[:, :].rearrange("p (j t) -> p j t", j=4)[:, :, 0:n])))
    transposes(jobs)

    lf_past = nc.dram_tensor("lf_past", (NB, FH, PAST), F32, kind="Internal").ap()
    lf_new = nc.dram_tensor("lf_new", (FH, NS), F32, kind="Internal").ap()

    def page_numbers(b, engine=mybir.EngineType.SP):
        _, pages = nc.values_load_multi_w_load_instructions(
            page_ids[0:1, bass.ds(b * PAGES, PAGES)], engines=[engine], min_val=0, max_val=NPHYS - 1)
        return pages

    left.close()
    left, right = ExitStack(), ExitStack()
    proj = place(right, "projected", [128, 7 * 4 * T], side="right")
    pieces = put_pieces(left)
    xn = put_split(left, "normed", KC, "left")
    lf_pages = place(left, "lf_pages", [NB * PAGES, PAGE * FH])
    lf_heads = place(left, "lf_heads", [NB * PAGES, PAGE * FH])
    lf_rows = nc.dram_tensor("lf_rows", (NB * PAGES, PAGE * FH), F32, kind="Internal").ap()
    s_lg, s_lf, s_lh, s_ls = sem("lf_gathered"), sem("lf_loaded"), sem("lf_by_head"), sem("lf_stored")

    def gather_lf(pool):
        with pool.Fori(0, NB) as b:
            for i, page in enumerate(page_numbers(b, mybir.EngineType.Pool)):
                pool.dma_start(lf_rows[bass.ds(b * PAGES + i, 1), :],
                               io["cache_fox_logf"].rearrange("n t h -> n (t h)")[bass.ds(page, 1), :]).then_inc(s_lg, 16)
        pool.wait_ge(s_lg, 16 * NB * PAGES)
        pool.dma_start(lf_pages[:, :], lf_rows).then_inc(s_lf, 16)
        pool.wait_ge(s_lf, 16)
        nc.gpsimd.tensor_copy(lf_heads[:, :].rearrange("p (h t) -> p h t", h=FH),
                              lf_pages[:, :].rearrange("p (t h) -> p h t", h=FH)).then_inc(s_lh, 1)
        pool.wait_ge(s_lh, 1)
        for b in range(NB):
            pool.dma_start(lf_past[b].rearrange("h (p t) -> p h t", p=PAGES),
                           lf_heads[b * PAGES:(b + 1) * PAGES, :].rearrange("p (h t) -> p h t", h=FH)).then_inc(s_ls, 16)
        pool.wait_ge(s_ls, 16 * NB)

    with ExitStack() as scratch_:
        rmsnorm(h, 0, 0, place(scratch_, "squares", [128, KC, T]), xn)
    chunk = lambda a: lambda k: (a[0][:, k, :], a[1][:, k, :])
    Pt = proj[:, :].rearrange("p (k t) -> p k t", k=28)
    P = proj[:, :].rearrange("p (a k t) -> p a k t", a=7, k=4)
    project(even_a, 1, 4, KC, chunk(xn), Pt, 0, pieces, then=even_b, beside=gather_lf)
    project(even_b, 1, 3, KC, chunk(xn), Pt, 16, pieces, then=out_even)
    mq, mk, mv, mo, fq, fk, fv = (P[:, a] for a in range(7))

    keep = place(right, "gate_rows", [72, T], side="right")
    R, CS = keep[:, :], rstd[0:72, :]
    mrow = place(right, "m_rows", [4, 2, T], side="right")
    negM, expm = mrow[:, 0, :], mrow[:, 1, :]
    winter = place(right, "w_inter", [4, NS], side="right")
    st4 = place(right, "by_head_and_sequence", [4, 4 * NB], side="right")
    m0, dec4, mnew = st4[:, 0:NB], st4[:, NB:2 * NB], st4[:, 2 * NB:3 * NB]
    mnew_p = st4[:, 3 * NB:3 * NB + 1]
    gbias = place(right, "gate_bias", [128, 1], side="right")
    TR = place(right, "gate_columns", [128, 6, 72], side="right")
    gates = ExitStack()
    wg = place(gates, "gate_weights", [128, KC, 96])
    row_ = place(gates, "gate_scratch", [96, 6, T])
    row = [row_[:, i, :] for i in range(6)]
    wg_high, wg_low = (a[:, 0, 0:KC * 96].rearrange("p (k c) -> p k c", k=KC) for a in pieces)
    s_gh, s_gl0 = sem("gate_w_high"), sem("gate_w_low")
    s_gw, s_wz, s_gp, s_ga, s_gv, s_gs = (sem(x) for x in
                                          ("gate_w", "gate_w_zero", "gate_logits", "gate_act", "gate_vec", "gate_out"))
    with nc.Block() as block:
        @block.sync
        def _(sp):
            sp.wait_ge(s_wz, 1)
            wv = w_view(io["w_in_even"])
            with nc.allow_non_contiguous_dma(reason="16 gate columns"):
                for dst, col, n in ((0, 2048, 4), (32, 2052, 4), (64, 3592, 8)):
                    sp.dma_start(wg[:, :, dst:dst + n], wv[:, :, col:col + n]).then_inc(s_gw, 16)
                for dst, src in ((0, "b_mlstm_i"), (32, "b_mlstm_f"), (64, "b_fox_f")):
                    n = io[src].shape[0]
                    sp.dma_start(gbias[dst:dst + n, :], io[src].rearrange("(a b) -> a b", b=1)).then_inc(s_gw, 16)
                sp.dma_start(m0, io["state_mlstm_m"].rearrange("b h -> h b")).then_inc(s_gw, 16)
            sp.wait_ge(s_gw, 16 * 7)

        @block.gpsimd
        def _(pool):
            nc.gpsimd.memset(wg[:, :, :], 0.0)
            nc.gpsimd.memset(gbias[:, :], 0.0)
            nc.gpsimd.drain()
            nc.gpsimd.memset(keep[:, :], 0.0).then_inc(s_wz, 1)

        @block.tensor
        def _(pe):
            pe.wait_ge(s_gl0, 1)
            for k in range(KC):
                for n, (w, x) in enumerate(((wg_high, xn[0]), (wg_high, xn[1]), (wg_low, xn[0]))):
                    for half in range(2):
                        last = nc.tensor.matmul(banks[half][0:96, 0:HALF], w[:, k, :],
                                                x[:, k, half * HALF:(half + 1) * HALF],
                                                start=(k == 0 and n == 0), stop=(k == KC - 1 and n == 2))
            last.then_inc(s_gp, 1)

        x, ax, lf = row[0][0:96, :], row[1][0:96, :], row[2][0:96, :]

        @block.scalar
        def _(act):
            act.wait_ge(s_gw, 16 * 7)
            nc.scalar.copy(wg_high, wg[:, :, :]).then_inc(s_gh, 1)
            nc.scalar.mul(mk[:, :, :], mk[:, :, :], QK_SCALE)
            act.wait_ge(s_gv, 1)
            nc.scalar.activation(ax, x, ACT.Abs)
            nc.scalar.drain()
            nc.scalar.activation(ax, ax, ACT.Exp, scale=-1.0).then_inc(s_ga, 1)
            act.wait_ge(s_gv, 2)
            nc.scalar.activation(ax, ax, ACT.Ln).then_inc(s_ga, 1)
            act.wait_ge(s_gv, 3)
            nc.scalar.activation(expm, expm, ACT.Exp)
            nc.scalar.activation(winter[:, :], winter[:, :], ACT.Exp)
            nc.scalar.activation(dec4, dec4, ACT.Exp)
            nc.scalar.activation(R[32:36, :], R[32:36, :], ACT.Exp)

        @block.vector
        def _(dve):
            v = nc.vector
            dve.wait_ge(s_gh, 1)
            v.tensor_tensor(wg_low, wg[:, :, :], wg_high.bitcast(F32), ALU.subtract).then_inc(s_gl0, 1)
            dve.wait_ge(s_gp, 1)
            for half in range(2):
                c = slice(half * HALF, (half + 1) * HALF)
                last = v.tensor_scalar(x[:, c], banks[half][0:96, 0:HALF], gbias[0:96, :], None, ALU.add)
            v.memset(row[4][0:72, :], 1.0)
            v.drain()
            v.tensor_scalar(lf, x, 0.0, None, ALU.min).then_inc(s_gv, 1)
            dve.wait_ge(s_ga, 1)
            v.tensor_scalar(ax, ax, 1.0, None, ALU.add).then_inc(s_gv, 1)
            dve.wait_ge(s_ga, 2)
            v.tensor_tensor(lf, lf, ax, ALU.subtract)
            v.drain()
            v.tensor_copy(R[64:72, :], lf[64:72, :])
            v.tensor_tensor_scan(CS[:, 0:TP], row[4][0:72, 0:TP], lf[0:72, 0:TP], 0.0, ALU.mult, ALU.add)
            cs, ls = (a[0:72, TP:T].rearrange("p (b t) -> p b t", t=TS) for a in (CS, lf))
            v.tensor_copy(cs[:, :, 0], ls[:, :, 0])
            for t in range(1, TS):
                v.drain()
                v.tensor_tensor(cs[:, :, t], cs[:, :, t - 1], ls[:, :, t], ALU.add)
            v.drain()
            cf = row[5][0:4, :]
            v.tensor_copy(cf, CS[32:36, :])
            v.drain()
            g, M = R[0:4, :], row[3][0:4, :]
            v.tensor_tensor(g, x[0:4, :], cf, ALU.subtract)
            v.drain()
            v.tensor_tensor_scan(M[:, 0:TP], g[:, 0:TP], g[:, 0:TP], 0.0, ALU.max, ALU.max)
            ms, gs = (a[:, TP:T].rearrange("p (b t) -> p b t", t=TS) for a in (M, g))
            v.tensor_tensor(ms[:, :, 0], gs[:, :, 0], m0, ALU.max)
            for t in range(1, TS):
                v.drain()
                v.tensor_tensor(ms[:, :, t], ms[:, :, t - 1], gs[:, :, t], ALU.max)
            v.drain()
            v.tensor_scalar(negM, M, -1.0, None, ALU.mult)
            v.tensor_tensor(expm, cf, M, ALU.add)
            cfs = cf[:, TP:T].rearrange("p (b t) -> p b t", t=TS)
            v.tensor_tensor(mnew, cfs[:, :, TS - 1], ms[:, :, TS - 1], ALU.add)
            v.tensor_tensor(mnew_p, cf[:, TP - 1:TP], M[:, TP - 1:TP], ALU.add)
            wi = winter[:, :].rearrange("p (b t) -> p b t", t=TS)
            for t in range(TS):
                v.tensor_tensor(wi[:, :, t], m0, ms[:, :, t], ALU.subtract)
            v.tensor_tensor(dec4, m0, ms[:, :, TS - 1], ALU.subtract)
            src = row[4][0:4, :]
            v.tensor_scalar(src[:, 0:TP], g[:, 0:TP], M[:, TP - 1:TP], None, ALU.subtract)
            ss = src[:, TP:T].rearrange("p (b t) -> p b t", t=TS)
            for t in range(TS):
                v.tensor_tensor(ss[:, :, t], gs[:, :, t], ms[:, :, TS - 1], ALU.subtract)
            v.drain()
            v.tensor_scalar(expm, expm, -1.0, None, ALU.mult)
            v.drain()
            v.tensor_copy(R[32:36, :], src).then_inc(s_gv, 1)

    gates.close()
    left.close()
    left = ExitStack()

    def place_mixer():
        global_ = place(left, "mixed", [128, KC, T])
        inner = ExitStack()
        states = place(inner, "states", [128, NB * MH * 128])
        return global_, inner, states, place(inner, "token_major", [128, 4, 6, 512])

    xn, inner, states, tok = place_mixer()
    TK = {"mk": tok[:, 0], "mv": tok[:, 1], "fk": tok[:, 2], "fv": tok[:, 3]}

    def token_major(pairs):
        jobs = []
        for dst, src in pairs:
            for b, (t0, n) in enumerate(BLK):
                jobs.append(([(src[:, c, t0:t0 + n], c * 128) for c in range(4)],
                             lambda cp, bank, dst=dst, b=b, n=n: cp(dst[0:n, b, :], bank[0:n, :])))
        return jobs

    jobs = token_major([(TK["mk"], mk), (TK["mv"], mv), (TK["fk"], fk), (TK["fv"], fv)])
    for b, (t0, n) in enumerate(BLK):
        jobs.append(([(R[:, t0:t0 + n], 0)],
                     lambda cp, bank, b=b, n=n: cp(TR[0:n, b, :], bank[0:n, 0:72])))
    Cst = states[:, :].rearrange("p (s v) -> p s v", v=128)
    cp = place(right, "cp", [128, MH, 129], side="right")
    nrow = cp[0:32, 0, 0:128]
    nst = place(right, "nst", [128, NB * MH], side="right")
    decs = place(right, "decs", [128, MH * NB], side="right")
    mwbuf = place(right, "mwbuf", [NS, 2, NB], side="right")
    nrows = place(right, "nrows", [32, 2, 128], side="right")
    s_state = sem("mlstm_state")

    def load_mlstm_state(sp):
        for b in range(NB):
            sp.dma_start(Cst[:, b * MH:(b + 1) * MH, :],
                         io["state_mlstm_C"][b].rearrange("h k v -> k h v")).then_inc(s_state, 16)
        sp.dma_start(nrow, io["state_mlstm_n"].rearrange("b h k -> (b h) k")).then_inc(s_state, 16)
        sp.wait_ge(s_state, 16 * 9)
    transposes(jobs, load_mlstm_state)

    s_kv = sem("kv_stored")

    def store_kv(sp):
        for name, a in (("fox_k", TK["fk"]), ("fox_v", TK["fv"])):
            p = io["p_" + name][0].rearrange("t h d -> t (h d)")
            sp.dma_start(p[0:512].rearrange("(b p) n -> p b n", p=128), a[:, 0:4, :]).then_inc(s_kv, 16)
            sp.dma_start(p[512:TP], a[0:16, 4, :]).then_inc(s_kv, 16)
            sp.dma_start(io["s_" + name].rearrange("b t h d -> (b t) (h d)"), a[0:NS, SB, :]).then_inc(s_kv, 16)
        p = io["p_fox_logf"][0]
        sp.dma_start(p[0:512].rearrange("(b p) n -> p b n", p=128), TR[:, 0:4, 64:72]).then_inc(s_kv, 16)
        sp.dma_start(p[512:TP], TR[0:16, 4, 64:72]).then_inc(s_kv, 16)
        sp.dma_start(io["s_fox_logf"].rearrange("b t h -> (b t) h"), TR[0:NS, SB, 64:72]).then_inc(s_kv, 16)
        with nc.allow_non_contiguous_dma(reason="36 numbers"):
            sp.dma_start(io["p_mlstm_m"].rearrange("b h -> h b"), mnew_p).then_inc(s_kv, 16)
            sp.dma_start(io["s_mlstm_m"].rearrange("b h -> h b"), mnew).then_inc(s_kv, 16)

    flat = lambda a: a.rearrange("p k t -> p (k t)")

    def scratch(x, y):
        return ([a[:, 0:1400] for a in (x, y)],
                [(x, y)[j % 2][:, 1400 + 304 * (j // 2):1704 + 304 * (j // 2)] for j in range(4)])

    qs = place(right, "qs", [128, MH, NS], side="right")
    nq = place(right, "nq", [128, MH, NS], side="right")
    TILES = [[(0, 0, 256), (1, 128, 128)],
             [(0, 256, 272), (1, 256, 272), (2, 256, 272), (3, 384, 144), (4, 512, 16), (SB, TP, NS)]]
    EOFF = [0, 528, 928, 1200, 1344, 1360]
    ALL = [(hd, r, tile) for hd in range(MH) for r in range(2) for tile in TILES[r]]

    d_bc, d_e, d_x = sem("m_rows"), sem("exponents"), sem("decays")
    d_s, d_w, d_wu, d_numc = (sem(x) for x in ("scores", "weights", "weights_used", "num_copied"))

    def decayed_attention(q, k, vt, state, bufs, mlstm, decay=None, decay_s=None):
        n_tiles = len(ALL)
        w0, c0_ = (0, 0) if mlstm else (len(ALL), 2 * MH)
        ebuf, wbuf = bufs

        with nc.Block() as block:
            @block.tensor
            def _(pe):
                def rows_of_max(hd):
                    if hd:
                        pe.wait_ge(d_e, hd)
                    for r, (c0, c1) in enumerate(RANGES):
                        at = banks[0][:, 256:512] if r == 0 else banks[1][:, 0:c1 - c0]
                        last = nc.tensor.matmul(at, head_row(4, hd), negM[:, c0:c1], start=True, stop=True)
                    last.then_inc(d_bc, 1)

                def score(i):
                    hd, r, (b, t0, w) = ALL[i]
                    if i >= 2:
                        pe.wait_ge(d_w, w0 + i - 1)
                    s0, n = BLK[b]
                    nc.tensor.matmul(banks[2 + i % 2][0:n, 0:w], k[:, hd, s0:s0 + n], q[:, hd, t0:t0 + w],
                                     start=True, stop=True).then_inc(d_s, 1)

                if mlstm:
                    rows_of_max(0)
                score(0)
                for i, (hd, r, (b, t0, w)) in enumerate(ALL):
                    if i + 1 < n_tiles:
                        score(i + 1)
                    if mlstm and i + 1 < n_tiles and i % 8 == 5 and hd + 1 < MH:
                        rows_of_max(hd + 1)
                    n = BLK[b][1]
                    c0 = t0 - RANGES[r][0]
                    first = b == 0
                    final = b == (1 if r == 0 else SB)
                    if first and hd:
                        pe.wait_ge(d_numc, c0_ + (hd - 1) * 2 + r + 1)
                    pe.wait_ge(d_w, w0 + i + 1)
                    stop = final and b != SB
                    if mlstm:
                        nc.tensor.matmul(banks[6 + r][0:4, c0:c0 + w], onecol[0:n, hd, :], wbuf[i % 4][0:n, 0:w],
                                         start=(first and hd == 0), stop=(stop and hd == MH - 1), skip_group_check=True)
                    last = nc.tensor.matmul(banks[4 + r][:, c0:c0 + w], vt[0:n, b, hd * 128:(hd + 1) * 128],
                                            wbuf[i % 4][0:n, 0:w], start=first, stop=stop, skip_group_check=True)
                    if b != SB:
                        last.then_inc(d_wu, 1)
                        continue
                    if mlstm:
                        nc.tensor.matmul(banks[7][0:4, c0:c0 + w], onecol[:, hd, :], nq[:, hd, :],
                                         start=False, stop=(hd == MH - 1), skip_group_check=True)
                    for bb in range(NB):
                        last = nc.tensor.matmul(banks[5][:, c0 + bb * TS:c0 + (bb + 1) * TS],
                                                state[:, bb * MH + hd, :], qs[:, hd, bb * TS:(bb + 1) * TS],
                                                start=False, stop=(bb == NB - 1), skip_group_check=True)
                    last.then_inc(d_wu, 1)

            @block.scalar
            def _(act):
                for hd in range(MH):
                    if mlstm:
                        act.wait_ge(d_e, hd + 1)
                        nc.scalar.activation(ebuf[hd % 2][:, 0:1344], ebuf[hd % 2][:, 0:1344], ACT.Exp)
                        nc.scalar.activation(ebuf[hd % 2][0:16, 1344:1360], ebuf[hd % 2][0:16, 1344:1360], ACT.Exp)
                        nc.scalar.activation(ebuf[hd % 2][0:32, 1360:1392], ebuf[hd % 2][0:32, 1360:1392],
                                             ACT.Exp).then_inc(d_x, 1)
                    if hd:
                        for r, (c0, c1) in enumerate(RANGES):
                            act.wait_ge(d_wu, w0 + 8 * (hd - 1) + (2, 8)[r])
                            nc.scalar.copy(xn[:, hd - 1, c0:c1], banks[4 + r][:, 0:c1 - c0]).then_inc(d_numc, 1)
                for r, (c0, c1) in enumerate(RANGES):
                    act.wait_ge(d_wu, w0 + 8 * (MH - 1) + (2, 8)[r])
                    nc.scalar.copy(xn[:, MH - 1, c0:c1], banks[4 + r][:, 0:c1 - c0]).then_inc(d_numc, 1)

            @block.vector
            def _(dve):
                v = nc.vector

                def exponents(hd):
                    dve.wait_ge(d_bc, hd + 1)
                    v.drain()
                    for b, (s0, n) in enumerate(BLK):
                        w = 528 - 128 * b if b < SB else NS
                        for lo, hi, bank, at in ((0, 256, 0, 256), (256, T, 1, -256)):
                            a, z = max(s0, lo), min(s0 + w, hi)
                            if a >= z:
                                continue
                            last = v.tensor_scalar(ebuf[hd % 2][0:n, EOFF[b] + a - s0:EOFF[b] + z - s0],
                                                   banks[bank][0:n, a + at:z + at], TR[0:n, b, hd:hd + 1], 0.0,
                                                   ALU.add, ALU.min)
                    last.then_inc(d_e, 1)

                if mlstm:
                    exponents(0)
                for i, (hd, r, (b, t0, w)) in enumerate(ALL):
                    s0, n = BLK[b]
                    if mlstm and i % 8 == 0:
                        dve.wait_ge(d_x, hd + 1)
                    if mlstm:
                        dec = ebuf[hd % 2][0:n, EOFF[b] + t0 - s0:EOFF[b] + t0 - s0 + w]
                        diag = t0 == s0
                        if diag:
                            wd = min(w, n)
                            mask = smask[0:NS, 0:NS] if b == SB else tri_st[0:n, 0:wd]
                            v.tensor_tensor(dec[:, 0:wd], dec[:, 0:wd], mask, ALU.mult)
                            v.drain()
                    else:
                        dec = decay_s[0:n, hd, 0:NS] if b == SB else decay[0:n, hd, t0 - s0:t0 - s0 + w]
                    dve.wait_ge(d_s, w0 + i + 1)
                    if i >= 4:
                        dve.wait_ge(d_wu, w0 + i - 3)
                    v.tensor_tensor(wbuf[i % 4][0:n, 0:w], banks[2 + i % 2][0:n, 0:w], dec, ALU.mult).then_inc(d_w, 1)
                    if mlstm and i % 8 == 6 and hd + 1 < MH:
                        exponents(hd + 1)

    s_prep = sem("state_rows")
    s_prep2 = sem("state_cols")
    with nc.Block() as block:
        @block.tensor
        def _(pe):
            for hd in range(MH):
                nc.tensor.matmul(banks[0][:, hd * NS:(hd + 1) * NS], head_row(4, hd), winter[:, :],
                                 start=True, stop=True)
            nc.tensor.matmul(banks[1][:, 0:32], nrow, ident[0:32, 0:32], start=True, stop=True,
                             is_transpose=True)
            for hd in range(MH):
                last = nc.tensor.matmul(banks[2][:, hd * NB:(hd + 1) * NB], head_row(4, hd), dec4,
                                        start=True, stop=True)
            last.then_inc(s_prep, 1)

        @block.vector
        def _(dve):
            v = nc.vector
            dve.wait_ge(s_prep, 1)
            v.tensor_copy(nst[:, :], banks[1][:, 0:32])
            v.tensor_copy(decs[:, :], banks[2][:, 0:32])
            for hd in range(MH):
                v.tensor_tensor(qs[:, hd, :], mq[:, hd, TP:T], banks[0][:, hd * NS:(hd + 1) * NS], ALU.mult)
            v.drain()
            for hd in range(MH):
                n = nst[:, :].rearrange("p (b h) -> p b h", h=MH)[:, :, hd:hd + 1].to_broadcast([128, NB, TS])
                v.tensor_tensor(nq[:, hd, :].rearrange("p (b t) -> p b t", t=TS),
                                qs[:, hd, :].rearrange("p (b t) -> p b t", t=TS), n, ALU.mult)

        @block.sync
        def _(sp):
            store_kv(sp)

    bufs = scratch(flat(mv), flat(fv))
    decayed_attention(mq, mk, TK["mv"], Cst, bufs, True)

    s_den, s_dbc, s_dbu, s_hm, s_sig = (sem(x) for x in ("den", "den_rows", "den_rows_used", "normalised", "sigmoid"))
    den = negM
    with nc.Block() as block:
        @block.vector
        def _(dve):
            v = nc.vector
            for r, (c0, c1) in enumerate(RANGES):
                v.tensor_copy(den[:, c0:c1], banks[6 + r][0:4, 0:c1 - c0])
            v.drain()
            v.scalar_tensor_tensor(out=den, in0=den, scalar=-1.0, in1=den, op0=ALU.mult, op1=ALU.max)
            v.drain()
            v.tensor_tensor(den, den, expm, ALU.max)
            v.drain()
            v.reciprocal(den, den).then_inc(s_den, 1)
            for i in range(2 * MH):
                hd, (c0, c1) = i // 2, RANGES[i % 2]
                dve.wait_ge(s_dbc, i + 1)
                v.tensor_tensor(xn[:, hd, c0:c1], xn[:, hd, c0:c1], banks[i % 4][:, 0:c1 - c0],
                                ALU.mult).then_inc(s_dbu, 1)

        @block.tensor
        def _(pe):
            pe.wait_ge(s_den, 1)
            for i in range(2 * MH):
                hd, (c0, c1) = i // 2, RANGES[i % 2]
                if i >= 4:
                    pe.wait_ge(s_dbu, i - 3)
                nc.tensor.matmul(banks[i % 4][:, 0:c1 - c0], head_row(4, hd), den[:, c0:c1],
                                 start=True, stop=True).then_inc(s_dbc, 1)

        @block.scalar
        def _(act):
            for hd in range(MH):
                nc.scalar.activation(mo[:, hd, :], mo[:, hd, :], ACT.Sigmoid).then_inc(s_sig, 1)

        @block.gpsimd
        def _(pool):
            for hd in range(MH):
                pool.wait_ge(s_sig, hd + 1)
                pool.wait_ge(s_dbu, 2 * hd + 2)
                nc.gpsimd.tensor_tensor(xn[:, hd, :], xn[:, hd, :], mo[:, hd, :], ALU.mult)

    u_v, u_u = sem("weighted_v"), sem("updates")

    def state_update(kt, vt, state, weight, decay, normaliser, bufs):
        u0 = 0 if normaliser else MH
        ebuf, _ = bufs
        nv = 129 if normaliser else 128
        vw = [e[:, 0:5 * 129].rearrange("p (b v) -> p b v", b=5) for e in ebuf]
        vm = [e[0:NS, 0:1024].rearrange("p (b v) -> p b v", b=NB) for e in vmbuf]
        own = smask[:, 32:40]

        with nc.Block() as block:
            @block.vector
            def _(dve):
                v = nc.vector

                def sources(hd):
                    for b in range(SB):
                        n = BLK[b][1]
                        v.tensor_scalar(vw[hd % 2][0:n, b, 0:128], vt[0:n, b, hd * 128:(hd + 1) * 128],
                                        weight(n, b, hd), None, ALU.mult)
                        v.tensor_copy(vw[hd % 2][0:n, b, 128:129], weight(n, b, hd))
                    mw = mwbuf[:, hd % 2, :]
                    v.tensor_scalar(mw, own, weight(NS, SB, hd), None, ALU.mult)
                    v.drain()
                    for b in range(NB):
                        last = v.tensor_scalar(vm[hd % 2][:, b, :], vt[0:NS, SB, hd * 128:(hd + 1) * 128],
                                               mw[:, b:b + 1], None, ALU.mult)
                    last.then_inc(u_v, 1)

                sources(0)
                for hd in range(MH):
                    if hd + 1 < MH:
                        sources(hd + 1)
                    dve.wait_ge(u_u, u0 + hd + 1)
                    p = hd % 2
                    v.tensor_copy(cp[:, hd, 0:nv], banks[4 * p][:, 0:nv])
                    d = decay(hd)
                    for b in range(NB):
                        s = state[:, b * MH + hd, :]
                        v.scalar_tensor_tensor(out=s, in0=s, scalar=d if isinstance(d, float) else d[:, b:b + 1],
                                               in1=banks[4 * p + 1 + b // 4][:, (b % 4) * 128:(b % 4 + 1) * 128],
                                               op0=ALU.mult, op1=ALU.add)
                    if normaliser:
                        n = nst[:, :].rearrange("p (b h) -> p b h", h=MH)[:, :, hd]
                        v.tensor_tensor(n, n, d, ALU.mult)
                        v.drain()
                        v.tensor_tensor(n, n, banks[4 * p + 3][:, 0:NB], ALU.add)

            @block.tensor
            def _(pe):
                for hd in range(MH):
                    p = hd % 2
                    pe.wait_ge(u_v, u0 + hd + 1)
                    for b in range(SB):
                        n = BLK[b][1]
                        nc.tensor.matmul(banks[4 * p][:, 0:nv], kt[0:n, b, hd * 128:(hd + 1) * 128],
                                         vw[p][0:n, b, 0:nv], start=(b == 0), stop=(b == SB - 1))
                    ks = kt[0:NS, SB, hd * 128:(hd + 1) * 128]
                    for half in range(2):
                        last = nc.tensor.matmul(banks[4 * p + 1 + half][:, :], ks,
                                                vm[p][:, 4 * half:4 * half + 4, :].rearrange("p b v -> p (b v)"),
                                                start=True, stop=True)
                    if normaliser:
                        last = nc.tensor.matmul(banks[4 * p + 3][:, 0:NB], ks, mwbuf[:, p, :], start=True, stop=True)
                    last.then_inc(u_u, 1)

    vmbuf = [flat(mk)[0:NS, 0:1024], flat(mk)[0:NS, 1024:2048]]
    decs_b = decs[:, :].rearrange("p (h b) -> p h b", h=MH)
    state_update(TK["mk"], TK["mv"], Cst, lambda n, b, hd: TR[0:n, b, 32 + hd:33 + hd],
                 lambda hd: decs_b[:, hd, :], True, bufs)

    s_st, s_nt, s_nr = sem("state_stored"), sem("norm_rows"), sem("norm_rows_copied")
    with nc.Block() as block:
        @block.tensor
        def _(pe):
            nc.tensor.matmul(banks[0][0:32, 0:128], nst[:, :], ident[:, :], start=True, stop=True, is_transpose=True)
            nc.tensor.matmul(banks[1][0:4, 0:128], cp[:, :, 128], ident[:, :], start=True, stop=True,
                             is_transpose=True).then_inc(s_nt, 1)

        @block.vector
        def _(dve):
            dve.wait_ge(s_nt, 1)
            nc.vector.tensor_copy(nrows[0:32, 0, :], banks[0][0:32, 0:128])
            nc.vector.tensor_copy(nrows[0:4, 1, :], banks[1][0:4, 0:128]).then_inc(s_nr, 1)

        @block.sync
        def _(sp):
            for b in range(NB):
                sp.dma_start(io["s_mlstm_C"][b].rearrange("h k v -> k h v"),
                             Cst[:, b * MH:(b + 1) * MH, :]).then_inc(s_st, 16)
            sp.dma_start(io["p_mlstm_C"][0].rearrange("h k v -> k h v"), cp[:, :, 0:128]).then_inc(s_st, 16)
            sp.wait_ge(s_nr, 1)
            sp.dma_start(io["s_mlstm_n"].rearrange("b h k -> (b h) k"), nrows[0:32, 0, :]).then_inc(s_st, 16)
            sp.dma_start(io["p_mlstm_n"][0], nrows[0:4, 1, :]).then_inc(s_st, 16)
            sp.wait_ge(s_st, 16 * 11)
            sp.wait_ge(s_kv, 16 * 11)

    F8 = flat(mq)[0:FH, 0:T]
    pbuf = [flat(mk)[:, 528 * i:528 * (i + 1)] for i in range(2)]
    ptb = [flat(mv)[:, 640 * i:640 * (i + 1)].rearrange("p (b t) -> p b t", b=5) for i in range(2)]
    fst = place(right, "fst", [128, 2, 4], side="right")
    UNITS = [(c, i, e) for c in range(4) for i in range(SB) for e in range(2)]
    s_f8, s_s, s_m, s_x, s_pn, s_pt, s_ptc, s_pv, s_out = (
        sem(x) for x in ("minus_F", "scores", "row_max", "exps", "probs", "probs_T", "probs_T_copied", "pv", "out_copied"))
    with nc.Block() as block:
        @block.tensor
        def _(pe):
            def score(n):
                c, i, e = UNITS[n]
                t0, r = BLK[i]
                if n >= 2:
                    pe.wait_ge(s_x, n - 1)
                at = 1024 * (n % 2)
                p = slice(64 * e, 64 * e + 64)
                spans = [(0, min(512, t0 + r))] + ([(512, TP)] if i == SB - 1 else [])
                for s0, s1 in spans:
                    diag = s1 > t0
                    nc.tensor.matmul(psum[0:r, at + s0:at + s1], fq[p, c, t0:t0 + r], fk[p, c, s0:s1],
                                     start=True, stop=False)
                    last = nc.tensor.matmul(psum[0:r, at + s0:at + s1], head_row(FH, 2 * c + e, r), F8[:, s0:s1],
                                            start=False, stop=not diag)
                    if diag:
                        last = nc.tensor.matmul(psum[0:r, at + t0:at + t0 + r], ident[0:r, 0:r], tri_ts[0:r, 0:r],
                                                start=False, stop=True)
                last.then_inc(s_s, 1)

            def pv(n):
                c, i, e = UNITS[n]
                u, r = n // 2, BLK[i][1]
                pe.wait_ge(s_ptc, n + 1)
                if e == 0 and u >= 2:
                    pe.wait_ge(s_out, u - 1)
                for j in range(i + 1):
                    nj = BLK[j][1]
                    last = nc.tensor.matmul(banks[6 + u % 2][64 * e:64 * e + 64, 0:r],
                                            TK["fv"][0:nj, j, (2 * c + e) * 64:(2 * c + e + 1) * 64],
                                            ptb[n % 2][0:nj, j, 0:r], start=(j == 0), stop=(j == i))
                last.then_inc(s_pv, 1)

            pe.wait_ge(s_f8, 1)
            score(0)
            for n, (c, i, e) in enumerate(UNITS):
                r = BLK[i][1]
                if n + 1 < len(UNITS):
                    score(n + 1)
                pe.wait_ge(s_pn, n + 1)
                if n >= 2:
                    pe.wait_ge(s_ptc, n - 1)
                for j in range(i + 1):
                    nj = BLK[j][1]
                    last = nc.tensor.matmul(banks[4 + n % 2][0:nj, j * r:(j + 1) * r],
                                            pbuf[n % 2][0:r, 128 * j:128 * j + nj], ident[0:r, 0:r],
                                            start=True, stop=True, is_transpose=True)
                last.then_inc(s_pt, 1)
                if n:
                    pv(n - 1)
            pv(len(UNITS) - 1)

        @block.vector
        def _(dve):
            v = nc.vector
            v.tensor_scalar(F8, CS[64:72, :], -1.0 / FOX_SCALE, None, ALU.mult).then_inc(s_f8, 1)

            def normalise(n):
                c, i, e = UNITS[n]
                r, w = BLK[i][1], BLK[i][0] + BLK[i][1]
                st = fst[0:r, n % 2, :]
                dve.wait_ge(s_x, n + 1)
                v.reciprocal(st[:, 3:4], st[:, 2:3])
                v.drain()
                v.tensor_scalar(pbuf[n % 2][0:r, 0:w], pbuf[n % 2][0:r, 0:w], st[:, 3:4], None,
                                ALU.mult).then_inc(s_pn, 1)

            for n, (c, i, e) in enumerate(UNITS):
                r, w = BLK[i][1], BLK[i][0] + BLK[i][1]
                st = fst[0:r, n % 2, :]
                dve.wait_ge(s_s, n + 1)
                v.reduce_max(st[:, 0:1], psum[0:r, 1024 * (n % 2):1024 * (n % 2) + w], AX_X)
                v.drain()
                v.tensor_scalar(st[:, 1:2], st[:, 0:1], -FOX_SCALE, None, ALU.mult).then_inc(s_m, 1)
                if n:
                    normalise(n - 1)
            normalise(len(UNITS) - 1)

        @block.scalar
        def _(act):
            def copy_T(n):
                c, i, e = UNITS[n]
                r = BLK[i][1]
                act.wait_ge(s_pt, n + 1)
                if n >= 2:
                    act.wait_ge(s_pv, n - 1)
                full = min(i + 1, 4)
                src = banks[4 + n % 2][:, 0:full * r].rearrange("p (j t) -> p j t", t=r)
                last = nc.scalar.copy(ptb[n % 2][:, 0:full, 0:r], src)
                if i == SB - 1:
                    last = nc.scalar.copy(ptb[n % 2][0:16, 4, 0:r], banks[4 + n % 2][0:16, 4 * r:5 * r])
                last.then_inc(s_ptc, 1)

            def copy_out(u):
                c, i, _ = UNITS[2 * u]
                t0, r = BLK[i]
                act.wait_ge(s_pv, 2 * u + 2)
                nc.scalar.copy(xn[:, 4 + c, t0:t0 + r], banks[6 + u % 2][:, 0:r]).then_inc(s_out, 1)

            for n, (c, i, e) in enumerate(UNITS):
                r, w = BLK[i][1], BLK[i][0] + BLK[i][1]
                act.wait_ge(s_m, n + 1)
                if n >= 2:
                    act.wait_ge(s_pt, n - 1)
                st = fst[0:r, n % 2, :]
                nc.scalar.activation(pbuf[n % 2][0:r, 0:w], psum[0:r, 1024 * (n % 2):1024 * (n % 2) + w], ACT.Exp,
                                     bias=st[:, 1:2], scale=FOX_SCALE, accum_out=st[:, 2:3]).then_inc(s_x, 1)
                if n:
                    copy_T(n - 1)
                if n % 2 and n >= 3:
                    copy_out((n - 3) // 2)
            copy_T(len(UNITS) - 1)
            copy_out(len(UNITS) // 2 - 1)

        s_ln = sem("new_lf_stored")

        @block.sync
        def _(sp):
            sp.dma_start(lf_new, CS[64:72, TP:T]).then_inc(s_ln, 16)
            sp.wait_ge(s_ln, 16)

    tokf = tok[:, :, :, :].rearrange("p a b c -> p (a b c)")
    kpage = tokf[:, 0:4096].rearrange("p (g n) -> p g n", g=PAGES)
    vpage = [tokf[:, 4096:8192], proj[:, 0:4096]]
    KT = states[:, :].rearrange("p (f c s) -> p f c s", f=2, c=4)
    rest = proj[:, 2 * 4 * T:4 * 4 * T]
    Frow, S = rest[:, 0:PAST + TS], rest[:, 1028:1028 + PAST + TS]
    PT = rest[:, 2056:2056 + 9 * 128].rearrange("p (g n) -> p g n", g=9)
    Qbd = rest[:, 3208:3208 + 512].rearrange("p (c b n) -> p c b n", c=4, b=4)
    Pn = rest[:, 3720:3720 + 32]
    cache_k = io["cache_fox_k"].rearrange("n t h d -> n t (h d)")
    cache_v = io["cache_fox_v"].rearrange("n t h d -> n t (h d)")
    k_full = [sem("k_full") for _ in range(PAGES)]
    v_full, v_used = [sem("v_full") for _ in range(2)], [sem("v_used") for _ in range(2)]
    s_F, s_q0, s_q, s_sc = sem("F_loaded"), sem("q_zeroed"), sem("q_spread"), sem("past_scores")
    s_kc = [sem("kT_by_vector"), sem("kT_by_scalar")]

    def load_v(sp, b, slot):
        for pg, page in enumerate(page_numbers(b)):
            sp.dma_start(vpage[slot][:, pg * 512:(pg + 1) * 512],
                         cache_v[bass.ds(page, 1), :, :].rearrange("a t n -> (a t) n")).then_inc(v_full[slot], 16)

    s_m2, s_x2, s_p2, s_t2, s_t2c, s_o2, s_o2c = (sem(x) for x in (
        "past_max", "past_exps", "past_probs", "past_probs_T", "past_probs_T_copied", "past_out", "past_out_scaled"))
    for g in range(2):
        with nc.Block() as block:
            @block.sync
            def _(sp):
                for b4 in range(4):
                    b = 4 * g + b4
                    sp.dma_start(Frow[32 * b4:32 * b4 + 32, 0:PAST],
                                 lf_past[b].unsqueeze(1).to_broadcast([FH, TS, PAST])).then_inc(s_F, 16)
                    sp.dma_start(Frow[32 * b4:32 * b4 + 32, PAST:PAST + TS],
                                 lf_new[:, b * TS:(b + 1) * TS].unsqueeze(1).to_broadcast([FH, TS, TS])).then_inc(s_F, 16)
                with sp.Fori(0, 4) as b4:
                    for pg, page in enumerate(page_numbers(b4 + 4 * g)):
                        sp.wait_ge(k_done[pg], b4 + (4 * g + 1))
                        sp.dma_start(kpage[:, pg, :], cache_k[bass.ds(page, 1), :, :]
                                     .rearrange("a t n -> (a t) n")).then_inc(k_full[pg], 16)
                for slot in range(2):
                    load_v(sp, 4 * g + slot, slot)

            @block.gpsimd
            def _(pool):
                nc.gpsimd.memset(rest[:, 3208:3208 + 512], 0.0).then_inc(s_q0, 1)

            @block.tensor
            def _(pe):
                def scores(b4, f):
                    for e in range(2):
                        pe.wait_ge(s_kc[e], g * 16 + (b4 * 8 + f * 4 + 4) // 2)
                    for c in range(4):
                        last = nc.tensor.matmul(psum[32 * b4:32 * b4 + 32, 512 * f:512 * f + 512], Qbd[:, c, b4, :],
                                                KT[:, f, c, :], start=(c == 0), stop=(c == 3))
                    last.then_inc(s_sc, 1)

                for j in range(4 * PAGES):
                    b4, pg = j // PAGES, j % PAGES
                    pe.wait_ge(k_full[pg], 16 * (4 * g + b4 + 1))
                    if j >= 4:
                        pe.wait_ge(s_kc[j % 2], g * 16 + (j - 4) // 2 + 1)
                    for c in range(4):
                        last = nc.tensor.matmul(banks[4 + j % 4][:, c * 128:(c + 1) * 128],
                                                kpage[:, pg, c * 128:(c + 1) * 128], ident[:, :],
                                                start=True, stop=True, is_transpose=True)
                    last.then_inc(k_done[pg], 1)
                    if j == 0:
                        pe.wait_ge(s_q, g + 1)
                    if j % 4 == 1 and j >= 4:
                        scores((j // 4 - 1) // 2, (j // 4 - 1) % 2)
                scores(3, 1)
                for b4 in range(4):
                    t0 = TP + (4 * g + b4) * TS
                    for c in range(4):
                        nc.tensor.matmul(banks[2][32 * b4:32 * b4 + 32, 0:TS], Qbd[:, c, b4, :], fk[:, c, t0:t0 + TS],
                                         start=(c == 0), stop=(c == 3))

            def kt_copy(eng, copy, e):
                for j in range(e, 4 * PAGES, 2):
                    b4, pg = j // PAGES, j % PAGES
                    f = pg // 4
                    eng.wait_ge(k_done[pg], 4 * g + b4 + 2)
                    if b4:
                        eng.wait_ge(s_sc, g * 8 + 2 * (b4 - 1) + f + 1)
                    copy(KT[:, f, :, (pg % 4) * 128:(pg % 4 + 1) * 128],
                         banks[4 + j % 4].rearrange("p (c s) -> p c s", c=4)).then_inc(s_kc[e], 1)

            @block.vector
            def _(dve):
                v = nc.vector
                dve.wait_ge(s_q0, g + 1)
                for c in range(4):
                    for e in range(2):
                        last = v.tensor_copy(Qbd[64 * e:64 * e + 64, c, :, (2 * c + e) * TS:(2 * c + e + 1) * TS],
                                             fq[64 * e:64 * e + 64, c, TP + 16 * g:TP + 16 * g + 16]
                                             .rearrange("p (b q) -> p b q", b=4))
                last.then_inc(s_q, 1)
                v.memset(S[:, 0:PAST], 1.0)
                dve.wait_ge(s_F, 128 * (g + 1))
                v.drain()
                v.tensor_tensor_scan(Frow[:, 0:PAST], S[:, 0:PAST], Frow[:, 0:PAST], 0.0, ALU.mult, ALU.add)
                v.drain()
                v.tensor_scalar(Frow[:, PAST:], Frow[:, PAST:], Frow[:, PAST - 1:PAST], None, ALU.add)
                kt_copy(dve, lambda d, s: v.tensor_copy(d, s), 0)

            @block.scalar
            def _(act):
                kt_copy(act, lambda d, s: nc.scalar.copy(d, s), 1)

        st = fst[:, 0, :]
        with nc.Block() as block:
            @block.vector
            def _(dve):
                v = nc.vector
                v.scalar_tensor_tensor(out=S, in0=psum[:, 0:PAST + TS], scalar=FOX_SCALE, in1=Frow,
                                       op0=ALU.mult, op1=ALU.subtract)
                v.drain()
                v.tensor_tensor(S[:, PAST:], S[:, PAST:], newmask, ALU.add)
                v.drain()
                v.reduce_max(st[:, 0:1], S, AX_X)
                v.drain()
                v.tensor_scalar(st[:, 1:2], st[:, 0:1], -1.0, None, ALU.mult).then_inc(s_m2, 1)
                dve.wait_ge(s_x2, g + 1)
                v.reciprocal(st[:, 3:4], st[:, 2:3])
                v.tensor_tensor(Pn.rearrange("p (b t) -> p b t", b=NB),
                                S[:, PAST:].unsqueeze(1).to_broadcast([128, NB, TS]),
                                bmask[:, g, :].rearrange("p (b t) -> p b t", b=NB), ALU.mult).then_inc(s_p2, 1)
                for i in range(2):
                    dve.wait_ge(s_t2, 3 * g + i + 1)
                    v.tensor_copy(PT[:, 4 * i:4 * i + 4, :], banks[4 + i].rearrange("p (g n) -> p g n", g=4))
                dve.wait_ge(s_t2, 3 * g + 3)
                v.tensor_copy(PT[0:NS, 8, :], banks[6][0:NS, 0:128]).then_inc(s_t2c, 1)
                dve.wait_ge(v_used[1], 2 * g + 2)
                v.tensor_scalar(S[:, 0:512], banks[3], st[:, 3:4], None, ALU.mult).then_inc(s_o2c, 1)
                dve.wait_ge(s_o2, g + 1)
                acc = banks[7].rearrange("p (c b n) -> p c b n", b=4, c=4)
                for c in range(4):
                    for e in range(2):
                        v.tensor_copy(xn[64 * e:64 * e + 64, 4 + c, TP + 16 * g:TP + 16 * g + 16]
                                      .rearrange("p (b q) -> p b q", b=4),
                                      acc[64 * e:64 * e + 64, c, :, (2 * c + e) * TS:(2 * c + e + 1) * TS])

            @block.scalar
            def _(act):
                act.wait_ge(s_m2, g + 1)
                nc.scalar.activation(S, S, ACT.Exp, bias=st[:, 1:2], scale=1.0, accum_out=st[:, 2:3]).then_inc(s_x2, 1)

            @block.tensor
            def _(pe):
                pe.wait_ge(s_p2, g + 1)
                for i in range(2):
                    for j in range(4):
                        last = nc.tensor.matmul(banks[4 + i][:, j * 128:(j + 1) * 128],
                                                S[:, (4 * i + j) * 128:(4 * i + j + 1) * 128], ident[:, :],
                                                start=True, stop=True, is_transpose=True)
                    last.then_inc(s_t2, 1)
                nc.tensor.matmul(banks[6][0:NS, 0:128], Pn, ident[:, :], start=True, stop=True,
                                 is_transpose=True).then_inc(s_t2, 1)
                pe.wait_ge(s_t2c, g + 1)
                for b4 in range(4):
                    slot = b4 % 2
                    pe.wait_ge(v_full[slot], 128 * (2 * g + b4 // 2 + 1))
                    at, own = banks[3][32 * b4:32 * b4 + 32, :], slice(b4 * 32, b4 * 32 + 32)
                    for pg in range(PAGES):
                        nc.tensor.matmul(at, PT[:, pg, own], vpage[slot][:, pg * 512:(pg + 1) * 512],
                                         start=(pg == 0), stop=False)
                    nc.tensor.matmul(at, PT[0:NS, 8, own], TK["fv"][0:NS, SB, :],
                                     start=False, stop=True).then_inc(v_used[slot], 1)
                pe.wait_ge(s_o2c, g + 1)
                for c in range(4):
                    last = nc.tensor.matmul(banks[7][:, c * 128:(c + 1) * 128], S[:, c * 128:(c + 1) * 128], ident[:, :],
                                            start=True, stop=True, is_transpose=True)
                last.then_inc(s_o2, 1)

            @block.sync
            def _(sp):
                for b4 in range(2, 4):
                    slot = b4 % 2
                    sp.wait_ge(v_used[slot], 2 * g + 1)
                    load_v(sp, 4 * g + b4, slot)

    s_mh = sem("mixed_high")
    closed = [0]

    def close_layer(layer, units):
        nonlocal left, right, pieces
        m, closed[0] = closed[0], closed[0] + 1
        inner.close()
        right.close()
        right = ExitStack()
        x = put_split(right, "mixed", KC, "right")
        with nc.Block() as block:
            @block.scalar
            def _(act):
                for k in range(KC):
                    nc.scalar.copy(x[0][:, k, :], xn[:, k, :]).then_inc(s_mh, 1)

            @block.vector
            def _(dve):
                for k in range(0, KC):
                    dve.wait_ge(s_mh, KC * m + k + 1)
                    nc.vector.tensor_tensor(x[1][:, k, :], xn[:, k, :], x[0][:, k, :].bitcast(F32), ALU.subtract)
        left.close()
        left = ExitStack()
        pieces = put_pieces(left)
        inner_ = ExitStack()
        o = place(inner_, "projected_out", [128, KC, T])
        squares = place(inner_, "squares", [128, KC, T])
        project(units[0], 1, 2, KC, chunk(x), o, 0, pieces, then=up[layer])
        rmsnorm(o, layer, 1, squares)
        rmsnorm(h, layer, 2, squares, x)
        inner_.close()
        inner_ = ExitStack()
        hid = put_split(inner_, "hidden", FC, "left")
        silu = ExitStack()
        project(up[layer], 2, FC // 2, KC, chunk(x), hid, 0, pieces, then=down[layer],
                silu=place(silu, "silu", [128, 2, T]))
        silu.close()
        right.close()
        right = ExitStack()
        o = place(right, "ffn_out", [128, KC, T], side="right")
        project(down[layer], 1, 4, FC, chunk(hid), o, 0, pieces, then=units[1])
        inner_.close()
        squares = place(inner_, "squares", [128, KC, T])
        rmsnorm(o, layer, 3, squares)
        inner_.close()
        right.close()
        right = ExitStack()

    close_layer(0, (out_even, odd))

    s_odd, s_rope = sem("odd_constants"), sem("rope_loaded")
    proj = place(right, "projected", [128, 7 * 4 * T], side="right")
    cp, mwbuf, qs, lam, fin = (place(right, n, shape, side="right") for n, shape in (
        ("cp", [128, MH, 129]), ("mwbuf", [NS, 2, NB]), ("qs", [128, MH, NS]), ("lam", [128, 4, 4]),
        ("fin", [128, 2, 32])))
    xn = put_split(left, "normed", KC, "left")
    rope = proj[:, 6 * 4 * T:6 * 4 * T + 2 * T].rearrange("p (a t) -> p a t", a=2)

    def load_rope(sp):
        sp.dma_start(rope, io["c_rope"]).then_inc(s_rope, 16)
        sp.wait_ge(s_rope, 16)

    with ExitStack() as scratch_:
        rmsnorm(h, 1, 0, place(scratch_, "squares", [128, KC, T]), xn, load_rope)
    Pt = proj[:, :].rearrange("p (k t) -> p k t", k=28)
    P = proj[:, :].rearrange("p (a k t) -> p a k t", a=7, k=4)
    project(odd, 1, 6, KC, chunk(xn), Pt, 0, pieces, then=out_odd)
    rq, rk, rv, rg, lx, lgate = (P[:, a] for a in range(6))
    left.close()
    left = ExitStack()
    xn, inner, states, tok = place_mixer()
    tokf = tok[:, :, :, :].rearrange("p a b c -> p (a b c)")
    TK = {"mk": tok[:, 0], "mv": tok[:, 1]}
    Cst = states[:, :].rearrange("p (s v) -> p s v", v=128)
    dtab = tokf[:, 6144:6144 + MH * TP].rearrange("p (h t) -> p h t", h=MH)

    s_ks, s_sw, s_xc, s_xs = sem("k_scaled"), sem("swapped"), sem("times_cos"), sem("times_sin")
    s_st2, s_ro = sem("ret_state"), sem("rotated")
    rtmp = [tokf[:, T * i:T * (i + 1)] for i in range(2)]
    RX = [a[:, hd, :] for a in (rq, rk) for hd in range(MH)]
    with nc.Block() as block:
        @block.sync
        def _(sp):
            for b in range(NB):
                sp.dma_start(Cst[:, b * MH:(b + 1) * MH, :],
                             io["state_ret_S"][b].rearrange("h k v -> k h v")).then_inc(s_st2, 16)
            sp.dma_start(dtab, io["c_decay"]).then_inc(s_odd, 16)
            sp.wait_ge(s_odd, 16)
            sp.wait_ge(s_st2, 16 * 8)

        @block.scalar
        def _(act):
            nc.scalar.mul(rk[:, :, :], rk[:, :, :], QK_SCALE).then_inc(s_ks, 1)

        @block.tensor
        def _(pe):
            for i, x in enumerate(RX):
                if i == MH:
                    pe.wait_ge(s_ks, 1)
                if i >= 4:
                    pe.wait_ge(s_xs, i - 3)
                for half in range(2):
                    last = nc.tensor.matmul(banks[2 * (i % 4) + half][:, 0:HALF], swap[:, :],
                                            x[:, half * HALF:(half + 1) * HALF], start=True, stop=True)
                last.then_inc(s_sw, 1)

        @block.gpsimd
        def _(pool):
            for i, x in enumerate(RX):
                pool.wait_ge(s_sw, i + 1)
                nc.gpsimd.tensor_tensor(x, x, rope[:, 0, :], ALU.mult).then_inc(s_xc, 1)

        @block.vector
        def _(dve):
            for i, x in enumerate(RX):
                dve.wait_ge(s_sw, i + 1)
                nc.vector.drain()
                for half in range(2):
                    last = nc.vector.tensor_tensor(rtmp[i % 2][:, half * HALF:(half + 1) * HALF],
                                                   banks[2 * (i % 4) + half][:, 0:HALF],
                                                   rope[:, 1, half * HALF:(half + 1) * HALF], ALU.mult)
                last.then_inc(s_xs, 1)
                nc.vector.drain()
                dve.wait_ge(s_xc, i + 1)
                nc.vector.tensor_tensor(x, x, rtmp[i % 2], ALU.add)
            for hd in range(MH):
                nc.vector.tensor_tensor(qs[:, hd, :], rq[:, hd, TP:T], dsm[:, hd, NS:2 * NS], ALU.mult)

    transposes(token_major([(TK["mk"], rk), (TK["mv"], rv)]))
    bufs = scratch(flat(rv), tokf[:, 9216:12288])
    decayed_attention(rq, rk, TK["mv"], Cst, bufs, False, dtab, dsm[:, :, 0:NS])
    vmbuf = [flat(rk)[0:NS, 0:1024], flat(rk)[0:NS, 1024:2048]]
    state_update(TK["mk"], TK["mv"], Cst, lambda n, b, hd: dsm[0:n, hd, 2 * NS + b:2 * NS + b + 1],
                 lambda hd: GAMMA4[hd], False, bufs)

    s_mu, s_hc, s_sq, s_var, s_iv, s_sd, s_bc, s_hn, s_sg = (sem(x) for x in (
        "head_sum", "centred", "head_sq", "head_var", "inv_var_rows", "rstd_rows", "rstd_bc", "head_normed", "silu_gate"))
    s_rs = sem("ret_stored")
    vrow = rstd[0:4, :]
    sqh = [flat(rq)[:, T * i:T * (i + 1)] for i in range(4)]
    with nc.Block() as block:
        @block.sync
        def _(sp):
            for b in range(NB):
                sp.dma_start(io["s_ret_S"][b].rearrange("h k v -> k h v"),
                             Cst[:, b * MH:(b + 1) * MH, :]).then_inc(s_rs, 16)
            sp.dma_start(io["p_ret_S"][0].rearrange("h k v -> k h v"), cp[:, :, 0:128]).then_inc(s_rs, 16)
            sp.wait_ge(s_rs, 16 * 9)

        @block.tensor
        def _(pe):
            def variance(hd):
                pe.wait_ge(s_sq, hd + 1)
                for half in range(2):
                    last = nc.tensor.matmul(banks[4 + half][0:4, 0:HALF], onecol[:, hd, :],
                                            sqh[hd][:, half * HALF:(half + 1) * HALF],
                                            start=(hd == 0), stop=(hd == MH - 1))
                return last

            for hd in range(MH):
                if hd >= 2:
                    pe.wait_ge(s_hc, hd - 1)
                for half in range(2):
                    last = nc.tensor.matmul(banks[2 * (hd % 2) + half][:, 0:HALF], ones[:, :],
                                            xn[:, hd, half * HALF:(half + 1) * HALF], start=True, stop=True)
                last.then_inc(s_mu, 1)
                if hd:
                    variance(hd - 1)
            variance(MH - 1).then_inc(s_var, 1)
            pe.wait_ge(s_sd, 1)
            for hd in range(MH):
                if hd >= 2:
                    pe.wait_ge(s_hn, hd - 1)
                for half in range(2):
                    last = nc.tensor.matmul(banks[2 * (hd % 2) + half][:, 0:HALF], head_row(4, hd),
                                            vrow[:, half * HALF:(half + 1) * HALF], start=True, stop=True)
                last.then_inc(s_bc, 1)

        @block.vector
        def _(dve):
            v = nc.vector
            for hd in range(MH):
                dve.wait_ge(s_mu, hd + 1)
                for half in range(2):
                    c = slice(half * HALF, (half + 1) * HALF)
                    last = v.scalar_tensor_tensor(out=xn[:, hd, c], in0=banks[2 * (hd % 2) + half][:, 0:HALF],
                                                  scalar=-1.0 / 128, in1=xn[:, hd, c], op0=ALU.mult, op1=ALU.add)
                last.then_inc(s_hc, 1)
            dve.wait_ge(s_var, 1)
            for half in range(2):
                v.tensor_scalar(vrow[:, half * HALF:(half + 1) * HALF], banks[4 + half][0:4, 0:HALF],
                                1.0 / 128, EPS, ALU.mult, ALU.add)
            v.drain()
            v.reciprocal(vrow, vrow).then_inc(s_iv, 1)
            for hd in range(MH):
                dve.wait_ge(s_bc, hd + 1)
                for half in range(2):
                    c = slice(half * HALF, (half + 1) * HALF)
                    last = v.scalar_tensor_tensor(out=xn[:, hd, c], in0=xn[:, hd, c], scalar=cols[:, LNG + hd:LNG + hd + 1],
                                                  in1=banks[2 * (hd % 2) + half][:, 0:HALF], op0=ALU.mult, op1=ALU.mult)
                last.then_inc(s_hn, 1)

        @block.scalar
        def _(act):
            for hd in range(MH):
                act.wait_ge(s_hc, hd + 1)
                nc.scalar.activation(sqh[hd], xn[:, hd, :], ACT.Square).then_inc(s_sq, 1)
            act.wait_ge(s_iv, 1)
            nc.scalar.activation(vrow, vrow, ACT.Sqrt).then_inc(s_sd, 1)
            nc.scalar.activation(rg[:, :, :], rg[:, :, :], ACT.Silu).then_inc(s_sg, 1)

        @block.gpsimd
        def _(pool):
            pool.wait_ge(s_sg, 1)
            for hd in range(MH):
                pool.wait_ge(s_hn, hd + 1)
                nc.gpsimd.tensor_tensor(xn[:, hd, :], xn[:, hd, :], rg[:, hd, :], ALU.mult)

    conv_in = flat(rq)[0:24, 0:512]
    h0_in = flat(rq)[0:32, 512:640]
    wab = proj[:, 6 * 4 * T:6 * 4 * T + 1024].rearrange("p (a c j) -> p a c j", a=2, c=4)
    sub = lambda i: tokf[:, 2240 * i + 256:2240 * (i + 1) + 256].rearrange("p (c t) -> p c t", c=4)
    us = tokf[:, 0:224].rearrange("p (c b u) -> p c b u", c=4, b=NB)
    h0 = tokf[:, 224:256]
    xc, ga, gi, gt = (sub(i) for i in range(4))
    hs = flat(rk).rearrange("p (c t) -> p c t", c=4)
    s_li, s_lz = sem("lru_loaded"), sem("lru_zeroed")
    fin2 = flat(rv)[:, 1400:1400 + 4 * 27].rearrange("p (c n) -> p c n", c=4)
    with nc.Block() as block:
        @block.gpsimd
        def _(pool):
            nc.gpsimd.memset(wab[:, :, :, :], 0.0).then_inc(s_lz, 1)

        @block.sync
        def _(sp):
            sp.dma_start(conv_in, io["state_lru_conv"].rearrange("b j n -> (b j) n")).then_inc(s_li, 16)
            sp.dma_start(h0_in, io["state_lru_h"].rearrange("b (k p) -> (b k) p", p=128)).then_inc(s_li, 16)
            sp.wait_ge(s_lz, 1)
            for a, name in enumerate(("lru_wa", "lru_wx")):
                for e in range(2):
                    sp.dma_start(wab[64 * e:64 * e + 64, a, :, 64 * e:64 * e + 64],
                                 io[name].rearrange("(c e) i j -> e i c j", e=2)[e]).then_inc(s_li, 16)
            sp.wait_ge(s_li, 16 * 6)

    jobs = [([(conv_in[:, c * 128:(c + 1) * 128], 0)],
             lambda cp_, bank, c=c: cp_(us[:, c, :, 0:3], bank[:, 0:24].rearrange("p (b j) -> p b j", j=3)))
            for c in range(4)]
    jobs.append(([(h0_in, 0)], lambda cp_, bank: cp_(h0, bank[:, 0:32])))
    transposes(jobs)

    s_xcd, s_gl, s_gs, s_lm = sem("conv_done"), sem("gate_logits"), sem("gates"), sem("lambda_steps")
    with nc.Block() as block:
        @block.vector
        def _(dve):
            v = nc.vector
            for c in range(4):
                v.tensor_copy(us[:, c, :, 3:7], lx[:, c, TP:T].rearrange("p (b t) -> p b t", t=TS))
            v.drain()
            for c in range(4):
                w = [cols[:, CONVW + 4 * j + c:CONVW + 4 * j + c + 1] for j in range(4)]
                xs_ = xc[:, c, TP:T].rearrange("p (b t) -> p b t", t=TS)
                v.tensor_scalar(xc[:, c, 0:TP], lx[:, c, 0:TP], w[3], cols[:, CONVB + c:CONVB + c + 1], ALU.mult, ALU.add)
                v.tensor_scalar(xs_, us[:, c, :, 3:7], w[3], cols[:, CONVB + c:CONVB + c + 1], ALU.mult, ALU.add)
                for j in range(3):
                    v.drain()
                    d = 3 - j
                    v.scalar_tensor_tensor(out=xc[:, c, d:TP], in0=lx[:, c, 0:TP - d], scalar=w[j],
                                           in1=xc[:, c, d:TP], op0=ALU.mult, op1=ALU.add)
                    last = v.scalar_tensor_tensor(out=xs_, in0=us[:, c, :, j:j + 4], scalar=w[j], in1=xs_,
                                                  op0=ALU.mult, op1=ALU.add)
                last.then_inc(s_xcd, 1)
            dve.wait_ge(s_lm, 1)
            v.tensor_scalar(lam[:, 1, :], lam[:, 1, :], 1.0, None, ALU.add).then_inc(s_lm, 1)
            v.tensor_scalar(lam[:, 2, :], cols[:, LLAM:LLAM + 4], -1.0, 0.0, ALU.mult, ALU.max)
            v.drain()
            dve.wait_ge(s_lm, 3)
            v.tensor_tensor(lam[:, 1, :], lam[:, 1, :], lam[:, 2, :], ALU.add)
            v.drain()
            v.tensor_scalar(lam[:, 2, :], lam[:, 1, :], 8.0, None, ALU.mult)
            v.tensor_scalar(lam[:, 3, :], lam[:, 1, :], -8.0, None, ALU.mult)

        @block.tensor
        def _(pe):
            for c in range(4):
                pe.wait_ge(s_xcd, c + 1)
                for a in range(2):
                    i = 2 * c + a
                    if i >= 4:
                        pe.wait_ge(s_gs, i - 3)
                    for half in range(2):
                        last = nc.tensor.matmul(banks[2 * (i % 4) + half][:, 0:HALF], wab[:, a, c, :],
                                                xc[:, c, half * HALF:(half + 1) * HALF], start=True, stop=True)
                    last.then_inc(s_gl, 1)

        @block.scalar
        def _(act):
            nc.scalar.activation(lam[:, 0, :], cols[:, LLAM:LLAM + 4], ACT.Abs)
            nc.scalar.drain()
            nc.scalar.activation(lam[:, 1, :], lam[:, 0, :], ACT.Exp, scale=-1.0).then_inc(s_lm, 1)
            for i in range(8):
                c, a = i // 2, i % 2
                act.wait_ge(s_gl, i + 1)
                for half in range(2):
                    last = nc.scalar.activation((ga, gi)[a][:, c, half * HALF:(half + 1) * HALF],
                                                banks[2 * (i % 4) + half][:, 0:HALF], ACT.Sigmoid,
                                                bias=cols[:, (LBA, LBX)[a] + c:(LBA, LBX)[a] + c + 1])
                last.then_inc(s_gs, 1)
            act.wait_ge(s_lm, 2)
            nc.scalar.activation(lam[:, 1, :], lam[:, 1, :], ACT.Ln).then_inc(s_lm, 1)

    s_a, s_q, s_r, s_b, s_h, s_ge, s_ap = (sem(x) for x in (
        "decay_done", "one_minus_a2", "root_done", "input_gated", "recurrence", "gelu_done", "a_squared"))
    a2 = [flat(rq)[:, T * i:T * (i + 1)] for i in range(4)]
    with nc.Block() as block:
        @block.scalar
        def _(act):
            for c in range(4):
                nc.scalar.activation(gt[:, c, :], ga[:, c, :], ACT.Tanh, scale=lam[:, 2, c:c + 1])
                nc.scalar.drain()
                nc.scalar.activation(ga[:, c, :], ga[:, c, :], ACT.Exp, scale=lam[:, 3, c:c + 1]).then_inc(s_a, 1)
            for c in range(4):
                act.wait_ge(s_q, c + 1)
                nc.scalar.activation(gt[:, c, :], gt[:, c, :], ACT.Sqrt).then_inc(s_r, 1)
            nc.scalar.activation(lgate[:, :, :], lgate[:, :, :], ACT.Gelu_apprx_tanh).then_inc(s_ge, 1)

        @block.gpsimd
        def _(pool):
            for c in range(4):
                nc.gpsimd.tensor_tensor(gi[:, c, :], gi[:, c, :], xc[:, c, :], ALU.mult).then_inc(s_b, 1)
            pool.wait_ge(s_ge, 1)
            for c in range(4):
                pool.wait_ge(s_h, c + 1)
                nc.gpsimd.tensor_tensor(xn[:, 4 + c, :], hs[:, c, :], lgate[:, c, :], ALU.mult)

        @block.vector
        def _(dve):
            v = nc.vector
            for c in range(4):
                dve.wait_ge(s_a, c + 1)
                v.tensor_tensor(a2[c], ga[:, c, :], ga[:, c, :], ALU.mult)
                v.drain()
                v.scalar_tensor_tensor(out=gt[:, c, :], in0=a2[c], scalar=1.0, in1=gt[:, c, :],
                                       op0=ALU.add, op1=ALU.mult).then_inc(s_q, 1)
            for c in range(4):
                dve.wait_ge(s_r, c + 1)
                dve.wait_ge(s_b, c + 1)
                v.tensor_tensor(gi[:, c, :], gi[:, c, :], gt[:, c, :], ALU.mult)
                v.drain()
                v.tensor_tensor_scan(hs[:, c, 0:TP], ga[:, c, 0:TP], gi[:, c, 0:TP], 0.0, ALU.mult, ALU.add)
                a_, b_, h_ = (t[:, c, TP:T].rearrange("p (b t) -> p b t", t=TS) for t in (ga, gi, hs))
                prev = h0.rearrange("p (b k) -> p b k", k=4)[:, :, c]
                for t in range(TS):
                    v.tensor_tensor(h_[:, :, t], a_[:, :, t], prev, ALU.mult)
                    v.drain()
                    last = v.tensor_tensor(h_[:, :, t], h_[:, :, t], b_[:, :, t], ALU.add)
                    if t + 1 < TS:
                        v.drain()
                    prev = h_[:, :, t]
                last.then_inc(s_h, 1)
            v.drain()
            v.tensor_copy(fin[:, 0, 0:4], hs[:, :, TP - 1])
            for c in range(4):
                v.tensor_copy(fin[:, 1, c * NB:(c + 1) * NB], hs[:, c, TP:T].rearrange("p (b t) -> p b t", t=TS)[:, :, TS - 1])
                v.tensor_copy(fin2[:, c, 0:3], lx[:, c, TP - 3:TP])
                v.tensor_copy(fin2[:, c, 3:27].rearrange("p (b j) -> p b j", j=3), us[:, c, :, 4:7])

    orow = flat(rv)[0:32, 0:2 * 128]
    crow = [flat(rv)[0:24, 256 + 512 * i:256 + 512 * (i + 1)] for i in range(2)]
    jobs = [([(fin[:, 0, 0:4], 0)], lambda cp_, bank: cp_(orow[0:4, 0:128], bank[0:4, 0:128])),
            ([(fin[:, 1, :], 0)], lambda cp_, bank: cp_(orow[0:32, 128:256], bank[0:32, 0:128])),
            ([(fin2[:, c, 0:3], c * 128) for c in range(4)], lambda cp_, bank: cp_(crow[0][0:3, :], bank[0:3, :])),
            ([(fin2[:, c, 3:27], c * 128) for c in range(4)], lambda cp_, bank: cp_(crow[1][0:24, :], bank[0:24, :]))]
    transposes(jobs)
    s_lo = sem("lru_stored")
    with nc.Block() as block:
        @block.sync
        def _(sp):
            sp.dma_start(io["p_lru_h"].rearrange("b (k p) -> (b k) p", p=128), orow[0:4, 0:128]).then_inc(s_lo, 16)
            for c in range(4):
                sp.dma_start(io["s_lru_h"][:, c * 128:(c + 1) * 128], orow[c * NB:(c + 1) * NB, 128:256]).then_inc(s_lo, 16)
            sp.dma_start(io["p_lru_conv"][0], crow[0][0:3, :]).then_inc(s_lo, 16)
            sp.dma_start(io["s_lru_conv"].rearrange("b j n -> (b j) n"), crow[1][0:24, :]).then_inc(s_lo, 16)
            sp.wait_ge(s_lo, 16 * 7)

    close_layer(1, (out_odd, None))

    yt = place(left, "tokens_out", [128, 6, D])
    jobs = []
    for b, (t0, n) in enumerate(BLK):
        for kk in range(0, KC, 4):
            jobs.append(([(h[:, kk + j, t0:t0 + n], j * 128) for j in range(4)],
                         lambda cp_, bank, kk=kk, b=b, n=n: cp_(yt[0:n, b, kk * 128:(kk + 4) * 128], bank[0:n, :])))
    transposes(jobs)
    s_y = sem("y_stored")
    with nc.Block() as block:
        @block.sync
        def _(sp):
            yp = io["y_prompt"][0]
            sp.dma_start(yp[0:128 - META], yt[META:128, 0, :]).then_inc(s_y, 16)
            sp.dma_start(yp[128 - META:512 - META].rearrange("(b p) n -> p b n", p=128), yt[:, 1:4, :]).then_inc(s_y, 16)
            sp.dma_start(yp[512 - META:SEQ], yt[0:16, 4, :]).then_inc(s_y, 16)
            sp.dma_start(io["y_sample"].rearrange("b t d -> (b t) d"), yt[0:NS, SB, :]).then_inc(s_y, 16)
            sp.wait_ge(s_y, 64)
    left.close()
    ctx.close()


_OUTS = [("y_prompt", (1, SEQ, D)), ("y_sample", (NB, TS, D)),
         ("p_fox_k", (1, TP, FH, FD)), ("p_fox_v", (1, TP, FH, FD)), ("p_fox_logf", (1, TP, FH)),
         ("s_fox_k", (NB, TS, FH, FD)), ("s_fox_v", (NB, TS, FH, FD)), ("s_fox_logf", (NB, TS, FH)),
         ("p_mlstm_C", (1, MH, 128, 128)), ("p_mlstm_n", (1, MH, 128)), ("p_mlstm_m", (1, MH)),
         ("s_mlstm_C", (NB, MH, 128, 128)), ("s_mlstm_n", (NB, MH, 128)), ("s_mlstm_m", (NB, MH)),
         ("p_ret_S", (1, MH, 128, 128)), ("s_ret_S", (NB, MH, 128, 128)),
         ("p_lru_h", (1, LW)), ("s_lru_h", (NB, LW)), ("p_lru_conv", (1, 3, LW)), ("s_lru_conv", (NB, 3, LW))]


def kernel(**inputs):
    import concourse.bacc as bacc
    from concourse.bass_utils import run_bass_kernel_spmd

    nc = bacc.Bacc("TRN2", target_bir_lowering=False, num_devices=1)
    arrays, io = {}, {}
    for name, a in list(inputs.items()) + [("c_" + k, v) for k, v in constants().items()]:
        a = np.ascontiguousarray(a)
        arrays["in_" + name] = a
        io[name] = nc.dram_tensor("in_" + name, a.shape, mybir.dt.from_np(a.dtype), kind="ExternalInput").ap()
    for name, shape in _OUTS:
        io[name] = nc.dram_tensor("out_" + name, shape, F32, kind="ExternalOutput").ap()
    hybrid_decoder(nc, io)
    r = run_bass_kernel_spmd(nc, [arrays], core_ids=[0])
    return tuple(r.results[0]["out_" + name] for name, _ in _OUTS)
```

```python
from contextlib import ExitStack

import numpy as np

import concourse.bass as bass
from concourse import mybir

F32 = mybir.dt.float32
F32R = mybir.dt.float32r
I32 = mybir.dt.int32
ALU = mybir.AluOpType
ACT = mybir.ActivationFunctionType
AX_X = mybir.AxisListType.X

D = 1024
KC = D // 128
META, SEQ = 16, 512
TP = META + SEQ
NB, TS = 8, 4
NS = NB * TS
T = TP + NS
HALF = T // 2
MH = 4
FH, FD = 8, 64
VW = FD + FH
FF = 2816
FC = FF // 128
PAGES, PAGE = 8, 128
PAST = PAGES * PAGE
LW = 512
NPHYS = 80
EPS = 1e-6
NEG = -1e30
QK_SCALE = 128.0 ** -0.5
FOX_SCALE = FD ** -0.5
BLK = [(0, 128), (128, 128), (256, 128), (384, 128), (512, 16), (TP, NS)]
SB = 5
RANGES = [(0, 256), (256, T)]


def constants():
    f = np.float32
    c = {}
    i = np.arange(128)
    c["ident"] = np.eye(128, dtype=f)
    c["ones"] = np.ones((128, 128), f)
    c["tri_ts"] = np.where(i[None, :] <= i[:, None], 0, NEG).astype(f)
    c["tri_st"] = (i[:, None] <= i[None, :]).astype(f)
    swap = np.zeros((128, 128), f)
    swap[i[:64] + 64, i[:64]] = -1
    swap[i[:64], i[:64] + 64] = 1
    c["swap"] = swap
    small = np.zeros((128, 16 + 4 + 64), f)
    small[:, 0:16] = np.eye(4, dtype=f).reshape(1, 16)
    q = i % 4
    small[:, 16:20] = np.where(np.arange(4)[None, :] <= q[:, None], 0, NEG)
    for g in range(2):
        own = np.repeat(np.arange(8) == 0, 4)
        for p in range(128):
            own = np.repeat(np.arange(8) == 4 * g + p // 32, 4)
            small[p, 20 + 32 * g:52 + 32 * g] = own
    c["small"] = small
    s = np.arange(32)
    sm = np.zeros((32, 40), f)
    sm[:, 0:32] = (s[:, None] // 4 == s[None, :] // 4) & (s[:, None] <= s[None, :])
    sm[:, 32:40] = s[:, None] // 4 == np.arange(8)[None, :]
    c["smask"] = sm
    pos = np.concatenate([np.arange(TP), np.tile(PAST + np.arange(TS), NB)]).astype(f)
    freq = f(10000.0) ** (-np.arange(64, dtype=f) / f(64))
    ang = freq[:, None] * pos[None, :]
    c["rope"] = np.stack([np.tile(np.cos(ang), (2, 1)), np.tile(np.sin(ang), (2, 1))], 1).astype(f)
    lg = np.log1p(-np.exp2(-5.0 - np.arange(4, dtype=f))).astype(np.float64)
    t = np.arange(TP)
    rel = t[None, :] - i[:, None]
    dec = np.zeros((128, 4, TP), f)
    dsm = np.zeros((128, 4, NS + NS + 6), f)
    for h in range(4):
        dec[:, h, :TP] = np.where(rel >= 0, np.exp(np.minimum(rel, TP) * 1.0 * lg[h]), 0)
        srel = s[None, :] - s[:, None]
        dsm[:32, h, :NS] = sm[:, 0:32] * np.exp(np.maximum(srel, 0) * lg[h])
        dsm[:, h, NS:2 * NS] = np.exp((s % 4 + 1) * lg[h])[None, :]
        for b, (t0, n) in enumerate(BLK):
            last = TP - 1 - t0 - i if b < SB else 3 - i % 4
            dsm[:, h, 2 * NS + b] = np.where(i < n, np.exp(np.maximum(last, 0) * lg[h]), 0)
    c["decay"] = dec
    c["decay_small"] = dsm
    return c


CONST_SHAPES = {k: v.shape for k, v in constants().items()}
GAMMA4 = [float(np.exp(4 * np.log1p(-np.exp2(-5.0 - h)))) for h in range(4)]


def hybrid_decoder(nc, io):
    ctx = ExitStack()
    sems = {}

    def sem(name):
        sems[name] = sems.get(name, 0) + 1
        return ctx.enter_context(nc.semaphore(f"{name}_{sems[name]}"))

    names = {}

    def place(stack, name, shape, dt=F32, side="left"):
        names[name] = names.get(name, 0) + 1
        return stack.enter_context(nc.sbuf_tensor(f"{name}_{names[name]}", shape, dt, side=side))

    def sb(name, shape, dt=F32):
        return place(ctx, name, shape, dt)

    V, A, G, PE = nc.vector, nc.scalar, nc.gpsimd, nc.tensor

    h = sb("h", [128, KC, T])
    ring = sb("ring", [128, 2, FC * 128])
    ident = sb("ident", [128, 128])
    ones = sb("ones", [128, 128])
    tri_ts = sb("tri_ts", [128, 128])
    tri_st = sb("tri_st", [128, 128])
    swap = sb("swap", [128, 128])
    small = sb("small", [128, 84])
    smask = sb("smask", [32, 40])
    cols = sb("cols", [128, 100])
    rstd = sb("rstd", [128, T])
    eps = sb("eps", [128, 2])
    psum = ctx.enter_context(nc.psum_tensor("psum", [128, 8 * 512], F32))
    banks = [psum[:, i * 512:(i + 1) * 512] for i in range(8)]
    dsm = sb("dsm", [128, MH, 70])
    page_ids = sb("page_ids", [1, NB * PAGES], I32)

    onecol = small[:, 0:16].rearrange("p (h j) -> p h j", h=4)
    newmask = small[:, 16:20]
    bmask = small[:, 20:84].rearrange("p (g c) -> p g c", g=2)

    def head_row(heads, hd, m=128):
        return ident[0:heads, hd:hd + 1].to_broadcast([heads, m])

    def gain(layer, n, k):
        c = (layer * 4 + n) * 8 + k
        return cols[:, c:c + 1]

    CONVW, CONVB, LBA, LBX, LLAM, LNG = 64, 80, 84, 88, 92, 96

    w_full = [sem("w_full_even"), sem("w_full_odd")]
    high_done = [sem("w_high_done") for _ in range(2)]
    low_done = [sem("w_low_done") for _ in range(2)]
    tile_full = [sem("tile_full") for _ in range(4)]
    tile_free = [sem("tile_free") for _ in range(4)]
    silu_done = [sem("silu_done") for _ in range(2)]
    hid_split = [sem("hidden_split") for _ in range(2)]
    k_done = [sem("k_transposed") for _ in range(PAGES)]
    sent, split_n, full_n, free_n, silus = [0], [0], [1] * 4, [1] * 4, [1]
    with nc.Block() as block:
        @block.vector
        def _(dve):
            for s in tile_full + tile_free + hid_split + k_done:
                dve.sem_inc(s, 1)
            nc.vector.memset(eps[:, :], EPS)

    def w_view(w):
        return w.rearrange("(k p) n -> p k n", p=128)

    def plain_unit(w, col):
        v = w_view(w)
        return lambda slot, u: [(ring[:, slot, 0:KC * 256].rearrange("p (k n) -> p k n", k=KC),
                                 v[:, :, bass.ds(u * 256 + col, 256)])]

    def down_unit(w):
        v = w_view(w)
        return lambda slot, u: [(ring[:, slot, :].rearrange("p (k n) -> p k n", k=FC),
                                 v[:, :, bass.ds(u * 128, 128)])]

    def gate_up_unit(wg, wu):
        g, u_ = w_view(wg), w_view(wu)

        def src(slot, u):
            dst = ring[:, slot, 0:2 * KC * 128].rearrange("p (a k n) -> p a k n", a=2, k=KC)
            return [(dst[:, 0], g[:, :, bass.ds(u * 128, 128)]), (dst[:, 1], u_[:, :, bass.ds(u * 128, 128)])]
        return src

    def send(sp, unit, slot, u):
        for dst, src in unit(slot, u):
            sp.dma_start(dst, src).then_inc(w_full[slot], 16)

    def prefetch(sp, unit):
        for slot in range(2):
            send(sp, unit, slot, slot)

    def splitters(loads, kc, pieces, gate_up=False):
        whole = kc == KC
        kp = kc if whole else kc // 2
        high, low = pieces
        wbase, s0, full0 = sent[0], split_n[0], list(full_n)
        per = 16 * loads

        def raw(slot, p):
            if gate_up or not whole:
                return ring[:, slot, p * kp * 128:(p + 1) * kp * 128].rearrange("p (k n) -> p k n", k=kp)
            return ring[:, slot, 0:2 * kp * 128].rearrange("p (k a n) -> p k a n", k=kp, a=2)[:, :, p]

        def part(a, p):
            return a[:, p, 0:kp * 128].rearrange("p (k n) -> p k n", k=kp)

        def split_high(act, i, slot, p):
            if p == 0:
                act.wait_ge(w_full[slot], i * per + (wbase + per))
            if slot:
                act.wait_ge(tile_full[p], i + (full0[p] + 1))
            else:
                act.wait_ge(tile_full[2 + p], i + full0[2 + p])
            nc.scalar.copy(part(high, p), raw(slot, p)).then_inc(high_done[p], 1)

        def split_low(dve, i, slot, p):
            dve.wait_ge(high_done[p], i * 2 + (s0 + slot + 1))
            nc.vector.tensor_tensor(part(low, p), raw(slot, p), part(high, p).bitcast(F32),
                                    ALU.subtract).then_inc(low_done[p], 1)

        return split_high, split_low, part

    def project(unit, loads, iters, kc, x, dst, first, pieces, then=None, silu=None, beside=None, normed=False,
                scaled=False, split=False, following=None,
                pe_first=None, act_first=None, dve_first=None, act_last=None, dve_last=None, dve_after=None, bank_free=None):
        whole = kc == KC
        kp = kc if whole else kc // 2
        high, low = pieces
        s0, full0, free0, silu0, root0 = split_n[0], list(full_n), list(free_n), silus[0], roots[0]
        per = 16 * loads
        split_high, split_low, part = splitters(loads, kc, pieces, silu is not None)
        scale = normed or scaled
        sent[0] += per * iters
        split_n[0] += 2 * iters
        for slot in range(2):
            for p in range(2):
                tl = 2 * slot + p
                full_n[tl] += iters
                if whole or p:
                    free_n[tl] += iters
        roots[0] += 2 * normed
        if silu is not None:
            silus[0] += iters
        next_high, next_low, _ = splitters(following[0], following[1], pieces, following[2]) if following else (None,) * 3

        def tile_of(slot, p):
            return 2 * slot + (p if whole else 1)

        def two_on(i, q):
            return (i, 1, q) if q < 2 else (i + 1, 0, q - 2)

        def turns(eng, turn):
            with eng.Fori(0, iters - 1) as i:
                turn(i, True)
            turn(iters - 1, False)

        with nc.Block() as block:
            @block.sync
            def _(sp):
                with sp.Fori(0, iters - 1) as i:
                    for slot in range(2):
                        for p in range(2):
                            sp.wait_ge(low_done[p], i * 2 + (s0 + slot + 1))
                        send(sp, unit, slot, i * 2 + (2 + slot))
                for slot in range(2):
                    for p in range(2):
                        sp.wait_ge(low_done[p], s0 + 2 * (iters - 1) + slot + 1)
                    if then is not None:
                        send(sp, then, slot, slot)

            @block.tensor
            def _(pe):
                if pe_first is not None:
                    pe_first(pe)
                with pe.Fori(0, iters) as i:
                    for slot in range(2):
                        for p in range(2):
                            tl = tile_of(slot, p)
                            pe.wait_ge(low_done[p], i * 2 + (s0 + slot + 1))
                            if whole or p == 0:
                                pe.wait_ge(tile_free[tl], i + free0[tl])
                            if normed and tl == 3:
                                pe.wait_ge(n_root2, root0 + 2)
                            if bank_free is not None and tl == 3:
                                pe.wait_ge(*bank_free)
                            w_high, w_low = part(high, p), part(low, p)
                            for k in range(kp):
                                kk = k if whole else p * kp + k
                                x_high, x_low = x(kk)
                                for w, m, end in ((w_high, x_high, 0), (w_high, x_low, 0), (w_low, x_high, 1)):
                                    for half in range(2):
                                        last = nc.tensor.matmul(
                                            banks[2 * tl + half][:, 0:HALF], w[:, k, :],
                                            m[:, half * HALF:(half + 1) * HALF],
                                            start=(kk == 0 and w is w_high and m is x_high),
                                            stop=(kk == kc - 1 and end == 1))
                            last.then_inc(tile_full[2 * slot + p], 1)

            @block.scalar
            def _(act):
                def turn(i, more):
                    for q in range(4):
                        if q < 2 or more:
                            split_high(act, *two_on(i, q))
                        if q < 2 and not more and act_last is not None:
                            act_last[q](act)
                        slot = q // 2
                        if silu is None or q % 2:
                            continue
                        act.wait_ge(tile_free[2 * slot], i + (free0[2 * slot] + 1))
                        nc.scalar.activation(silu[:, slot, :], silu[:, slot, :], ACT.Silu).then_inc(silu_done[slot], 1)

                if normed:
                    for half in range(2):
                        nc.scalar.activation(rstd[:, half * HALF:(half + 1) * HALF], banks[6 + half][:, 0:HALF],
                                             ACT.Sqrt, bias=eps[:, 0:1], scale=1.0 / D).then_inc(n_root2, 1)
                elif not split:
                    split_high(act, 0, 0, 0)
                    split_high(act, 0, 0, 1)
                if act_first is not None:
                    act_first(act)
                turns(act, turn)
                if following:
                    next_high(act, 0, 0, 0)
                    next_high(act, 0, 0, 1)

            @block.vector
            def _(dve):
                def turn(i, more):
                    for q in range(4):
                        slot, p = q // 2, q % 2
                        tl = tile_of(slot, p)
                        if silu is not None or whole or p:
                            dve.wait_ge(tile_full[tl], i + (full0[tl] + 1))
                        if silu is not None:
                            if p == 0:
                                dve.wait_ge(hid_split[slot], i + silu0)
                            else:
                                dve.wait_ge(silu_done[slot], i + silu0)
                            for half in range(2):
                                cols_ = slice(half * HALF, (half + 1) * HALF)
                                c = nc.vector.tensor_tensor(
                                    silu[:, slot, cols_], silu[:, slot, cols_] if p else rstd[:, cols_],
                                    banks[2 * tl + half][:, 0:HALF], ALU.mult)
                            c.then_inc(tile_free[tl], 1)
                        elif whole or p:
                            step, at = (4, first + q) if whole else (2, first + slot)
                            for half in range(2):
                                cols_ = slice(half * HALF, (half + 1) * HALF)
                                out = dst[:, bass.ds(i * step + at, 1), cols_].rearrange("p a t -> p (a t)")
                                if scale:
                                    c = nc.vector.tensor_tensor(out, banks[2 * tl + half][:, 0:HALF], rstd[:, cols_],
                                                                ALU.mult)
                                else:
                                    c = nc.vector.tensor_copy(out, banks[2 * tl + half][:, 0:HALF])
                            c.then_inc(tile_free[tl], 1)
                        if q < 2 or more:
                            split_low(dve, *two_on(i, q))
                        if q < 2 and not more and dve_last is not None:
                            dve_last[q](dve)

                if normed:
                    for half in range(2):
                        dve.wait_ge(n_root2, root0 + half + 1)
                        nc.vector.reciprocal(rstd[:, half * HALF:(half + 1) * HALF],
                                             rstd[:, half * HALF:(half + 1) * HALF])
                    nc.vector.drain()
                elif not split:
                    split_low(dve, 0, 0, 0)
                    split_low(dve, 0, 0, 1)
                if dve_first is not None:
                    dve_first(dve)
                turns(dve, turn)
                if dve_after is not None:
                    dve_after(dve)
                if following:
                    next_low(dve, 0, 0, 0)
                    next_low(dve, 0, 0, 1)

            @block.gpsimd
            def _(pool):
                if beside is not None:
                    beside(pool)
                if silu is None:
                    return
                with pool.Fori(0, iters) as i:
                    for slot in range(2):
                        pool.wait_ge(tile_free[2 * slot + 1], i + (free0[2 * slot + 1] + 1))
                        nc.gpsimd.tensor_tensor(silu[:, slot, :], silu[:, slot, :], rstd[:, :], ALU.mult)
                        nc.gpsimd.drain()
                        hh, hl = (a[:, bass.ds(i * 2 + slot, 1), :].rearrange("p a t -> p (a t)") for a in dst)
                        nc.gpsimd.tensor_copy(hh, silu[:, slot, :])
                        nc.gpsimd.drain()
                        nc.gpsimd.tensor_tensor(hl, silu[:, slot, :], hh.bitcast(F32),
                                                ALU.subtract).then_inc(hid_split[slot], 1)

    def put_pieces(stack, side="left"):
        return [place(stack, f"w_{x}", [128, 2, FC // 2 * 128], F32R, side) for x in ("high", "low")]

    def put_split(stack, name, chunks, side):
        return [place(stack, f"{name}_{x}", [128, chunks, T], F32R, side) for x in ("high", "low")]

    def warm(bank, times=4):
        for _ in range(times):
            nc.tensor.matmul(banks[bank], ones[:, :], ones[:, :].unsqueeze(1).to_broadcast([128, 4, 128]), start=True,
                             stop=True)

    tr_full, tr_free, tr_n = [sem("tr_full_v"), sem("tr_full_a")], [sem("tr_free_v"), sem("tr_free_a")], [0, 0]

    def transposes(jobs, sync=None):
        full, free, n0 = tr_full, tr_free, list(tr_n)
        with nc.Block() as block:
            if sync is not None:
                block.sync(sync)

            @block.tensor
            def _(pe):
                for j, (ins, _) in enumerate(jobs):
                    if j >= 8:
                        pe.wait_ge(free[j % 2], n0[j % 2] + (j - 8) // 2 + 1)
                    for src, col in ins:
                        k, m = src.shape[0], src.shape[-1]
                        last = nc.tensor.matmul(banks[j % 8][0:m, col:col + k], src, ident[0:k, 0:k],
                                                start=True, stop=True, is_transpose=True)
                    last.then_inc(full[j % 2], 1)

            @block.vector
            def _(dve):
                for j in range(0, len(jobs), 2):
                    dve.wait_ge(full[0], n0[0] + j // 2 + 1)
                    jobs[j][1](lambda d, s: nc.vector.tensor_copy(d, s), banks[j % 8]).then_inc(free[0], 1)

            @block.scalar
            def _(act):
                for j in range(1, len(jobs), 2):
                    act.wait_ge(full[1], n0[1] + j // 2 + 1)
                    jobs[j][1](lambda d, s: nc.scalar.copy(d, s), banks[j % 8]).then_inc(free[1], 1)

        tr_n[0] += (len(jobs) + 1) // 2
        tr_n[1] += len(jobs) // 2

    (n_sqa, n_sqp, n_pair, n_sum, n_root, n_y, n_h, n_high, n_sq) = (sem(x) for x in (
        "squares_by_scalar", "squares_by_gpsimd", "square_pairs", "sum_done", "root_done", "post_normed", "residual",
        "x_high", "h_squares"))
    n_root2 = sem("h_root_done")
    roots = [0]
    posts, pres = [0], [0]

    def sums_of_squares(pe, sq, chunks, ready, base, first_bank, done=None):
        for j in range(chunks):
            pe.wait_ge(ready, base + j + 1)
            for half in range(2):
                last = nc.tensor.matmul(banks[first_bank + half][:, 0:HALF], ones[:, :],
                                        sq[:, j, half * HALF:(half + 1) * HALF],
                                        start=(j == 0), stop=(j == chunks - 1))
                if done is not None and j == chunks - 1:
                    last.then_inc(done, 1)

    def norm(o, post, pre, sq, dst=None, upcoming=None, beside=None, pool_work=None):
        a, b = posts[0], pres[0]
        posts[0] += o is not None
        pres[0] += dst is not None
        with nc.Block() as block:
            if beside is not None:
                block.sync(beside)

            @block.scalar
            def _(act):
                if o is not None:
                    for k in range(4):
                        nc.scalar.activation(sq[:, k, :], o[:, k, :], ACT.Square).then_inc(n_sqa, 1)
                if upcoming is not None:
                    for p in range(2):
                        upcoming[0](act, 0, 0, p)
                if o is not None:
                    nc.scalar.activation(eps[:, 1:2], eps[:, 0:1], ACT.Sqrt)
                    for half in range(2):
                        act.wait_ge(n_sum, 2 * a + half + 1)
                        nc.scalar.activation(rstd[:, half * HALF:(half + 1) * HALF], banks[half][:, 0:HALF], ACT.Sqrt,
                                             bias=eps[:, 0:1], scale=1.0 / D).then_inc(n_root, 1)
                if dst is None:
                    return
                for k in range(KC):
                    if o is not None:
                        act.wait_ge(n_h, KC * a + k + 1)
                    nc.scalar.mul(dst[0][:, k, :], h[:, k, :], gain(*pre, k)).then_inc(n_high, 1)
                    nc.scalar.activation(sq[:, k, :], h[:, k, :], ACT.Square).then_inc(n_sq, 1)

            @block.tensor
            def _(pe):
                if o is not None:
                    warm(6, 4)
                    sums_of_squares(pe, sq, 4, n_pair, 4 * a, 0, n_sum)
                    if dst is not None:
                        warm(4, 8)
                if dst is not None:
                    sums_of_squares(pe, sq, KC, n_sq, KC * b, 6)

            @block.gpsimd
            def _(pool):
                if pool_work is not None:
                    pool_work(pool)
                if o is None:
                    return
                for k in (6, 7):
                    nc.gpsimd.tensor_tensor(sq[:, k, :], o[:, k, :], o[:, k, :], ALU.mult).then_inc(n_sqp, 1)
                for k in range(0, KC, 1 if dst is not None else 2):
                    pool.wait_ge(n_y, KC * a + k + 1)
                    nc.gpsimd.tensor_tensor(h[:, k, :], h[:, k, :], sq[:, k, :], ALU.add).then_inc(n_h, 1)

            @block.vector
            def _(dve):
                v = nc.vector
                if o is not None:
                    for k in (4, 5):
                        v.tensor_tensor(sq[:, k, :], o[:, k, :], o[:, k, :], ALU.mult)
                    v.drain()
                    for k in range(4):
                        dve.wait_ge(n_sqa, 4 * a + k + 1)
                        if k >= 2:
                            dve.wait_ge(n_sqp, 2 * a + k - 1)
                        v.tensor_tensor(sq[:, k, :], sq[:, k, :], sq[:, k + 4, :], ALU.add).then_inc(n_pair, 1)
                if upcoming is not None:
                    for p in range(2):
                        upcoming[1](dve, 0, 0, p)
                if o is not None:
                    for half in range(2):
                        dve.wait_ge(n_root, 2 * a + half + 1)
                        v.reciprocal(rstd[:, half * HALF:(half + 1) * HALF], rstd[:, half * HALF:(half + 1) * HALF])
                    v.drain()
                    for k in range(KC):
                        v.scalar_tensor_tensor(out=sq[:, k, :], in0=o[:, k, :], scalar=gain(*post, k), in1=rstd[:, :],
                                               op0=ALU.mult, op1=ALU.mult).then_inc(n_y, 1)
                if dst is None:
                    v.drain()
                    for k in range(1, KC, 2):
                        v.tensor_tensor(h[:, k, :], h[:, k, :], sq[:, k, :], ALU.add)
                if dst is not None:
                    for k in range(KC):
                        dve.wait_ge(n_high, KC * b + k + 1)
                        v.scalar_tensor_tensor(out=dst[1][:, k, :], in0=h[:, k, :], scalar=gain(*pre, k),
                                               in1=dst[0][:, k, :].bitcast(F32), op0=ALU.mult, op1=ALU.subtract)

    even_a, even_b = plain_unit(io["w_in_even"], 0), plain_unit(io["w_in_even"], 2048 + 8)
    out_even, odd = plain_unit(io["w_out_even"], 0), plain_unit(io["w_in_odd"], 0)
    out_odd = plain_unit(io["w_out_odd"], 0)
    up = [gate_up_unit(io["ffn_wg"][l], io["ffn_wu"][l]) for l in range(2)]
    down = [down_unit(io["ffn_wd"][l]) for l in range(2)]

    left = ExitStack()
    xt = place(left, "tokens_in", [128, 6, D])
    params = rstd[0:100, 0:128]
    s_in, s_const = sem("x_loaded"), sem("const_loaded")
    xp, xs = io["x_prompt"][0], io["x_sample"].rearrange("b t d -> (b t) d")
    with nc.Block() as block:
        @block.sync
        def _(sp):
            sp.dma_start(ident[:, :], io["c_ident"]).then_inc(s_const, 16)
            sp.dma_start(page_ids[:, :], io["page_table"].rearrange("(a b) p -> a (b p)", a=1)).then_inc(s_const, 16)
            sp.dma_start(xt[0:META, 0, :], io["meta_tokens"]).then_inc(s_in, 16)
            sp.dma_start(xt[META:128, 0, :], xp[0:128 - META]).then_inc(s_in, 16)
            for b in range(1, SB):
                t0, n = BLK[b]
                sp.dma_start(xt[0:n, b, :], xp[t0 - META:t0 - META + n]).then_inc(s_in, 16)
            sp.dma_start(xt[0:NS, SB, :], xs).then_inc(s_in, 16)
            prefetch(sp, even_a)
            sp.wait_ge(s_in, 16 * 7)

        @block.scalar
        def _(act):
            for dst, name in ((ones, "ones"), (tri_ts, "tri_ts"), (tri_st, "tri_st"), (swap, "swap"),
                              (small, "small"), (smask, "smask")):
                act.dma_start(dst[:, :], io["c_" + name]).then_inc(s_const, 16)
            act.dma_start(dsm[:, :, :], io["c_decay_small"]).then_inc(s_const, 16)
            for r0, n, src in ((0, 64, io["norm_g"].rearrange("l n (k p) -> (l n k) p", p=128)),
                               (CONVW, 16, io["conv_w"].rearrange("j (k p) -> (j k) p", p=128)),
                               (CONVB, 4, io["conv_b"].rearrange("(k p) -> k p", p=128)),
                               (LBA, 4, io["lru_ba"].rearrange("(k p) -> k p", p=128)),
                               (LBX, 4, io["lru_bx"].rearrange("(k p) -> k p", p=128)),
                               (LLAM, 4, io["lru_lambda"].rearrange("(k p) -> k p", p=128)),
                               (LNG, 4, io["ret_ln_g"])):
                act.dma_start(params[r0:r0 + n, :], src).then_inc(s_const, 16)
            act.wait_ge(s_const, 16 * 16)

    jobs = [([(params, 0)], lambda cp, bank: cp(cols[:, :], bank[:, 0:100]))]
    for b, (t0, n) in enumerate(BLK):
        for kk in range(0, KC, 4):
            jobs.append(([(xt[0:n, b, (kk + j) * 128:(kk + j + 1) * 128], j * 128) for j in range(4)],
                         lambda cp, bank, kk=kk, t0=t0, n=n: cp(
                             h[:, kk:kk + 4, t0:t0 + n],
                             bank[:, :].rearrange("p (j t) -> p j t", j=4)[:, :, 0:n])))
    transposes(jobs)

    lf_past = nc.dram_tensor("lf_past", (NB, FH, PAST), F32, kind="Internal").ap()
    lf_new = nc.dram_tensor("lf_new", (FH, NS), F32, kind="Internal").ap()

    def page_numbers(b, engine=mybir.EngineType.SP):
        _, pages = nc.values_load_multi_w_load_instructions(
            page_ids[0:1, bass.ds(b * PAGES, PAGES)], engines=[engine], min_val=0, max_val=NPHYS - 1)
        return pages

    left.close()
    left, right = ExitStack(), ExitStack()
    proj = place(right, "projected", [128, 7 * 4 * T], side="right")
    pieces = put_pieces(left)
    xn = put_split(left, "normed", KC, "left")
    lf_pages = place(left, "lf_pages", [NB * PAGES, PAGE * FH])
    lf_heads = place(left, "lf_heads", [NB * PAGES, PAGE * FH])
    lf_rows = nc.dram_tensor("lf_rows", (NB * PAGES, PAGE * FH), F32, kind="Internal").ap()
    s_lg, s_lf, s_lh, s_ls = sem("lf_gathered"), sem("lf_loaded"), sem("lf_by_head"), sem("lf_stored")

    def gather_lf(pool):
        with pool.Fori(0, NB) as b:
            for i, page in enumerate(page_numbers(b, mybir.EngineType.Pool)):
                pool.dma_start(lf_rows[bass.ds(b * PAGES + i, 1), :],
                               io["cache_fox_logf"].rearrange("n t h -> n (t h)")[bass.ds(page, 1), :]).then_inc(s_lg, 16)

    def reorder_lf(pool):
        pool.wait_ge(s_lg, 16 * NB * PAGES)
        pool.dma_start(lf_pages[:, :], lf_rows).then_inc(s_lf, 16)
        pool.wait_ge(s_lf, 16)
        nc.gpsimd.tensor_copy(lf_heads[:, :].rearrange("p (h t) -> p h t", h=FH),
                              lf_pages[:, :].rearrange("p (t h) -> p h t", h=FH)).then_inc(s_lh, 1)
        pool.wait_ge(s_lh, 1)
        for b in range(NB):
            pool.dma_start(lf_past[b].rearrange("h (p t) -> p h t", p=PAGES),
                           lf_heads[b * PAGES:(b + 1) * PAGES, :].rearrange("p (h t) -> p h t", h=FH)).then_inc(s_ls, 16)
        pool.wait_ge(s_ls, 16 * NB)

    keep = place(right, "gate_rows", [72, T], side="right")
    R, CS = keep[:, :], rstd[0:72, :]
    mrow = place(right, "m_rows", [4, 2, T], side="right")
    negM, expm = mrow[:, 0, :], mrow[:, 1, :]
    winter = place(right, "w_inter", [4, NS], side="right")
    st4 = place(right, "by_head_and_sequence", [4, 4 * NB], side="right")
    m0, dec4, mnew = st4[:, 0:NB], st4[:, NB:2 * NB], st4[:, 2 * NB:3 * NB]
    mnew_p = st4[:, 3 * NB:3 * NB + 1]
    gbias = place(right, "gate_bias", [128, 1], side="right")
    TR = place(right, "gate_columns", [128, 6, 72], side="right")
    row_ = place(left, "gate_scratch", [128, 6, T])
    row = [row_[:, i, :] for i in range(6)]
    wg = row_[:, 4:6, :].rearrange("p a t -> p (a t)")[:, 0:KC * 96].rearrange("p (k c) -> p k c", k=KC)
    wg_high, wg_low = (place(left, f"gate_w_{x}", [128, KC, 96], F32R) for x in ("high", "low"))
    s_gw, s_wz, s_gh, s_gl0, s_gp, s_ga, s_gv = (sem(x) for x in (
        "gate_w", "gate_w_zero", "gate_w_high", "gate_w_low", "gate_logits", "gate_act", "gate_vec"))

    def load_gate_weights(sp):
        sp.wait_ge(s_wz, 1)
        wv = w_view(io["w_in_even"])
        with nc.allow_non_contiguous_dma(reason="16 gate columns"):
            for dst, col, n in ((0, 2048, 4), (32, 2052, 4), (64, 3592, 8)):
                sp.dma_start(wg[:, :, dst:dst + n], wv[:, :, col:col + n]).then_inc(s_gw, 16)
            for dst, src in ((0, "b_mlstm_i"), (32, "b_mlstm_f"), (64, "b_fox_f")):
                n = io[src].shape[0]
                sp.dma_start(gbias[dst:dst + n, :], io[src].rearrange("(a b) -> a b", b=1)).then_inc(s_gw, 16)
            sp.dma_start(m0, io["state_mlstm_m"].rearrange("b h -> h b")).then_inc(s_gw, 16)
        sp.wait_ge(s_gw, 16 * 7)

    def zero_gate_weights(pool):
        nc.gpsimd.memset(wg, 0.0)
        nc.gpsimd.memset(gbias[:, :], 0.0)
        nc.gpsimd.drain()
        nc.gpsimd.memset(keep[:, :], 0.0).then_inc(s_wz, 1)

    def gate_weights_high(act):
        nc.scalar.copy(wg_high[:, :, :], wg).then_inc(s_gh, 1)

    def gate_weights_low(dve):
        dve.wait_ge(s_gh, 1)
        nc.vector.tensor_tensor(wg_low[:, :, :], wg, wg_high[:, :, :].bitcast(F32), ALU.subtract)

    def gate_products(pe):
        for k in range(KC):
            for n, (w, x) in enumerate(((wg_high, xn[0]), (wg_high, xn[1]), (wg_low, xn[0]))):
                for half in range(2):
                    last = nc.tensor.matmul(banks[6 + half][0:96, 0:HALF], w[:, k, :],
                                            x[:, k, half * HALF:(half + 1) * HALF],
                                            start=(k == 0 and n == 0), stop=(k == KC - 1 and n == 2))
        last.then_inc(s_gp, 1)

    x, ax, lf = row[0][0:96, :], row[1][0:96, :], row[2][0:96, :]

    cumul = ax[0:72, :]

    def log_sigmoid_by_scalar(act):
        nc.scalar.mul(mk[:, :, :], mk[:, :, :], QK_SCALE)
        act.wait_ge(s_gv, 1)
        nc.scalar.activation(ax, x, ACT.Abs)
        nc.scalar.drain()
        nc.scalar.activation(ax, ax, ACT.Exp, scale=-1.0).then_inc(s_ga, 1)
        act.wait_ge(s_gv, 2)
        nc.scalar.activation(ax, ax, ACT.Ln).then_inc(s_ga, 1)

    def gates_by_scalar(act):
        act.wait_ge(s_gv, 3)
        nc.scalar.activation(expm, expm, ACT.Exp)
        nc.scalar.activation(winter[:, :], winter[:, :], ACT.Exp)
        nc.scalar.activation(dec4, dec4, ACT.Exp)
        nc.scalar.activation(R[32:36, :], R[32:36, :], ACT.Exp)

    def gate_logits(dve):
        v = nc.vector
        dve.wait_ge(s_gp, 1)
        for half in range(2):
            c = slice(half * HALF, (half + 1) * HALF)
            v.tensor_tensor(x[:, c], banks[6 + half][0:96, 0:HALF], rstd[0:96, c], ALU.mult)
        v.drain()
        v.tensor_scalar(x, x, gbias[0:96, :], None, ALU.add).then_inc(s_gv, 1)

    def log_sigmoid_by_vector(dve):
        v = nc.vector
        v.memset(row[4][0:72, :], 1.0)
        v.drain()
        v.tensor_scalar(lf, x, 0.0, None, ALU.min)
        dve.wait_ge(s_ga, 1)
        v.tensor_scalar(ax, ax, 1.0, None, ALU.add).then_inc(s_gv, 1)
        dve.wait_ge(s_ga, 2)
        v.tensor_tensor(lf, lf, ax, ALU.subtract)
        v.drain()
        v.tensor_copy(R[64:72, :], lf[64:72, :])

    def gates_by_vector(dve):
        v = nc.vector
        v.tensor_tensor_scan(cumul[:, 0:TP], row[4][0:72, 0:TP], lf[0:72, 0:TP], 0.0, ALU.mult, ALU.add)
        cs, ls = (a[0:72, TP:T].rearrange("p (b t) -> p b t", t=TS) for a in (cumul, lf))
        v.tensor_copy(cs[:, :, 0], ls[:, :, 0])
        for t in range(1, TS):
            v.drain()
            v.tensor_tensor(cs[:, :, t], cs[:, :, t - 1], ls[:, :, t], ALU.add)
        v.drain()
        cf = row[5][0:4, :]
        v.tensor_copy(cf, cumul[32:36, :])
        v.drain()
        g, M = R[0:4, :], row[3][0:4, :]
        v.tensor_tensor(g, x[0:4, :], cf, ALU.subtract)
        v.drain()
        v.tensor_tensor_scan(M[:, 0:TP], g[:, 0:TP], g[:, 0:TP], 0.0, ALU.max, ALU.max)
        ms, gs = (a[:, TP:T].rearrange("p (b t) -> p b t", t=TS) for a in (M, g))
        v.tensor_tensor(ms[:, :, 0], gs[:, :, 0], m0, ALU.max)
        for t in range(1, TS):
            v.drain()
            v.tensor_tensor(ms[:, :, t], ms[:, :, t - 1], gs[:, :, t], ALU.max)
        v.drain()
        v.tensor_scalar(negM, M, -1.0, None, ALU.mult)
        v.tensor_tensor(expm, cf, M, ALU.add)
        cfs = cf[:, TP:T].rearrange("p (b t) -> p b t", t=TS)
        v.tensor_tensor(mnew, cfs[:, :, TS - 1], ms[:, :, TS - 1], ALU.add)
        v.tensor_tensor(mnew_p, cf[:, TP - 1:TP], M[:, TP - 1:TP], ALU.add)
        wi = winter[:, :].rearrange("p (b t) -> p b t", t=TS)
        for t in range(TS):
            v.tensor_tensor(wi[:, :, t], m0, ms[:, :, t], ALU.subtract)
        v.tensor_tensor(dec4, m0, ms[:, :, TS - 1], ALU.subtract)
        src = row[4][0:4, :]
        v.tensor_scalar(src[:, 0:TP], g[:, 0:TP], M[:, TP - 1:TP], None, ALU.subtract)
        ss = src[:, TP:T].rearrange("p (b t) -> p b t", t=TS)
        for t in range(TS):
            v.tensor_tensor(ss[:, :, t], gs[:, :, t], ms[:, :, TS - 1], ALU.subtract)
        v.drain()
        v.tensor_scalar(expm, expm, -1.0, None, ALU.mult)
        v.drain()
        v.tensor_copy(R[32:36, :], src).then_inc(s_gv, 1)

    def keep_cumulated(dve):
        nc.vector.drain()
        nc.vector.tensor_copy(CS, cumul)

    norm(None, None, (0, 0), proj[:, 0:KC * T].rearrange("p (k t) -> p k t", k=KC), xn, splitters(1, KC, pieces),
         load_gate_weights, zero_gate_weights)
    chunk = lambda a: lambda k: (a[0][:, k, :], a[1][:, k, :])
    Pt = proj[:, :].rearrange("p (k t) -> p k t", k=28)
    P = proj[:, :].rearrange("p (a k t) -> p a k t", a=7, k=4)
    mq, mk, mv, mo, fq, fk, fv = (P[:, a] for a in range(7))
    project(even_a, 1, 4, KC, chunk(xn), Pt, 0, pieces, then=even_b, beside=gather_lf, normed=True,
            following=(1, KC, False), act_first=gate_weights_high, dve_first=gate_weights_low)
    project(even_b, 1, 3, KC, chunk(xn), Pt, 16, pieces, beside=reorder_lf, scaled=True, split=True,
            pe_first=gate_products, dve_first=gate_logits, act_last=(log_sigmoid_by_scalar, gates_by_scalar),
            dve_last=(log_sigmoid_by_vector, gates_by_vector), dve_after=keep_cumulated, bank_free=(s_gv, 1))

    left.close()
    left = ExitStack()

    def place_mixer():
        out = place(left, "mixed", [128, KC, T])
        inner = ExitStack()
        states = place(inner, "states", [128, NB * MH * 128])
        v = place(inner, "token_major_v", [128, 6, FH, VW])
        top = ExitStack()
        return out, inner, states, v, top, place(top, "token_major", [128, 3, 6, 512])

    xn, inner, states, fox_v, inner_top, tok = place_mixer()
    fox_values = fox_v[:, :, :, 0:FD]
    TK = {"mk": tok[:, 0], "mv": tok[:, 1], "fk": tok[:, 2]}

    def token_major(pairs):
        jobs = []
        for dst, src in pairs:
            for b, (t0, n) in enumerate(BLK):
                jobs.append(([(src[:, c, t0:t0 + n], c * 128) for c in range(4)],
                             lambda cp, bank, dst=dst, b=b, n=n: cp(dst[0:n, b, :], bank[0:n, :])))
        return jobs

    jobs = token_major([(TK["mk"], mk), (TK["mv"], mv), (TK["fk"], fk)])
    for b, (t0, n) in enumerate(BLK):
        jobs.append(([(fv[:, c, t0:t0 + n], c * 128) for c in range(4)],
                     lambda cp, bank, b=b, n=n: cp(fox_values[0:n, b], bank[0:n, :].rearrange("p (h d) -> p h d", d=FD))))
    for b, (t0, n) in enumerate(BLK):
        jobs.append(([(R[:, t0:t0 + n], 0)],
                     lambda cp, bank, b=b, n=n: cp(TR[0:n, b, :], bank[0:n, 0:72])))
    Cst = states[:, :].rearrange("p (s v) -> p s v", v=128)
    cp = place(right, "cp", [128, MH, 129], side="right")
    nrow = cp[0:32, 0, 0:128]
    nst = place(right, "nst", [128, NB * MH], side="right")
    decs = place(right, "decs", [128, MH * NB], side="right")
    mwbuf = place(right, "mwbuf", [NS, 2, NB], side="right")
    nrows = place(right, "nrows", [32, 2, 128], side="right")
    s_state = sem("mlstm_state")

    def load_mlstm_state(sp):
        for b in range(NB):
            sp.dma_start(Cst[:, b * MH:(b + 1) * MH, :],
                         io["state_mlstm_C"][b].rearrange("h k v -> k h v")).then_inc(s_state, 16)
        sp.dma_start(nrow, io["state_mlstm_n"].rearrange("b h k -> (b h) k")).then_inc(s_state, 16)
        sp.wait_ge(s_state, 16 * 9)
    transposes(jobs, load_mlstm_state)

    s_kv = sem("kv_stored")

    def store_kv(sp):
        a = TK["fk"]
        p = io["p_fox_k"][0].rearrange("t h d -> t (h d)")
        sp.dma_start(p[0:512].rearrange("(b p) n -> p b n", p=128), a[:, 0:4, :]).then_inc(s_kv, 16)
        sp.dma_start(p[512:TP], a[0:16, 4, :]).then_inc(s_kv, 16)
        sp.dma_start(io["s_fox_k"].rearrange("b t h d -> (b t) (h d)"), a[0:NS, SB, :]).then_inc(s_kv, 16)
        p = io["p_fox_v"][0]
        for b in range(4):
            sp.dma_start(p[128 * b:128 * b + 128], fox_values[:, b]).then_inc(s_kv, 16)
        sp.dma_start(p[512:TP], fox_values[0:16, 4]).then_inc(s_kv, 16)
        sp.dma_start(io["s_fox_v"].rearrange("b t h d -> (b t) h d"), fox_values[0:NS, SB]).then_inc(s_kv, 16)
        p = io["p_fox_logf"][0]
        sp.dma_start(p[0:512].rearrange("(b p) n -> p b n", p=128), TR[:, 0:4, 64:72]).then_inc(s_kv, 16)
        sp.dma_start(p[512:TP], TR[0:16, 4, 64:72]).then_inc(s_kv, 16)
        sp.dma_start(io["s_fox_logf"].rearrange("b t h -> (b t) h"), TR[0:NS, SB, 64:72]).then_inc(s_kv, 16)
        with nc.allow_non_contiguous_dma(reason="36 numbers"):
            sp.dma_start(io["p_mlstm_m"].rearrange("b h -> h b"), mnew_p).then_inc(s_kv, 16)
            sp.dma_start(io["s_mlstm_m"].rearrange("b h -> h b"), mnew).then_inc(s_kv, 16)

    flat = lambda a: a.rearrange("p k t -> p (k t)")

    def scratch(x, y):
        return ([a[:, 0:1400] for a in (x, y)],
                [(x, y)[j % 2][:, 1400 + 304 * (j // 2):1704 + 304 * (j // 2)] for j in range(4)])

    qs = place(right, "qs", [128, MH, NS], side="right")
    nq = place(right, "nq", [128, MH, NS], side="right")
    TILES = [[(0, 0, 256), (1, 128, 128)],
             [(0, 256, 272), (1, 256, 272), (2, 256, 272), (3, 384, 144), (4, 512, 16), (SB, TP, NS)]]
    EOFF = [0, 528, 928, 1200, 1344, 1360]
    ALL = [(hd, r, tile) for hd in range(MH) for r in range(2) for tile in TILES[r]]

    d_bc, d_e, d_x = sem("m_rows"), sem("exponents"), sem("decays")
    d_s, d_w, d_wu, d_numc = (sem(x) for x in ("scores", "weights", "weights_used", "num_copied"))

    def decayed_attention(q, k, vt, state, bufs, mlstm, decay=None, decay_s=None, lam_steps=None, beside=None,
                          between=None, store=None):
        n_tiles = len(ALL)
        w0, c0_ = (0, 0) if mlstm else (len(ALL), 2 * MH)
        ebuf, wbuf = bufs

        with nc.Block() as block:
            @block.tensor
            def _(pe):
                def rows_of_max(hd):
                    if hd:
                        pe.wait_ge(d_e, hd)
                    for r, (c0, c1) in enumerate(RANGES):
                        at = banks[0][:, 256:512] if r == 0 else banks[1][:, 0:c1 - c0]
                        last = nc.tensor.matmul(at, head_row(4, hd), negM[:, c0:c1], start=True, stop=True)
                    last.then_inc(d_bc, 1)

                def score(i):
                    hd, r, (b, t0, w) = ALL[i]
                    if i >= 2:
                        pe.wait_ge(d_w, w0 + i - 1)
                    s0, n = BLK[b]
                    nc.tensor.matmul(banks[2 + i % 2][0:n, 0:w], k[:, hd, s0:s0 + n], q[:, hd, t0:t0 + w],
                                     start=True, stop=True).then_inc(d_s, 1)

                if mlstm:
                    rows_of_max(0)
                warm(3)
                score(0)
                for i, (hd, r, (b, t0, w)) in enumerate(ALL):
                    if i + 1 < n_tiles:
                        score(i + 1)
                    if mlstm and i % 8 == 0 and hd + 1 < MH:
                        rows_of_max(hd + 1)
                    n = BLK[b][1]
                    c0 = t0 - RANGES[r][0]
                    first = b == 0
                    final = b == (1 if r == 0 else SB)
                    if first and hd:
                        pe.wait_ge(d_numc, c0_ + (hd - 1) * 2 + r + 1)
                    pe.wait_ge(d_w, w0 + i + 1)
                    stop = final and b != SB
                    if mlstm:
                        nc.tensor.matmul(banks[6 + r][0:4, c0:c0 + w], onecol[0:n, hd, :], wbuf[i % 4][0:n, 0:w],
                                         start=(first and hd == 0), stop=(stop and hd == MH - 1), skip_group_check=True)
                    last = nc.tensor.matmul(banks[4 + r][:, c0:c0 + w], vt[0:n, b, hd * 128:(hd + 1) * 128],
                                            wbuf[i % 4][0:n, 0:w], start=first, stop=stop, skip_group_check=True)
                    if b != SB:
                        last.then_inc(d_wu, 1)
                        continue
                    if mlstm:
                        nc.tensor.matmul(banks[7][0:4, c0:c0 + w], onecol[:, hd, :], nq[:, hd, :],
                                         start=False, stop=(hd == MH - 1), skip_group_check=True)
                    for bb in range(NB):
                        last = nc.tensor.matmul(banks[5][:, c0 + bb * TS:c0 + (bb + 1) * TS],
                                                state[:, bb * MH + hd, :], qs[:, hd, bb * TS:(bb + 1) * TS],
                                                start=False, stop=(bb == NB - 1), skip_group_check=True)
                    last.then_inc(d_wu, 1)

            if beside is not None:
                block.gpsimd(beside)
            if store is not None:
                block.sync(store)

            @block.scalar
            def _(act):
                if lam_steps is not None:
                    lam_steps(act)
                for hd in range(MH):
                    if mlstm:
                        act.wait_ge(d_e, hd + 1)
                        nc.scalar.activation(ebuf[hd % 2][:, 0:1344], ebuf[hd % 2][:, 0:1344], ACT.Exp)
                        nc.scalar.activation(ebuf[hd % 2][0:16, 1344:1360], ebuf[hd % 2][0:16, 1344:1360], ACT.Exp)
                        nc.scalar.activation(ebuf[hd % 2][0:32, 1360:1392], ebuf[hd % 2][0:32, 1360:1392],
                                             ACT.Exp).then_inc(d_x, 1)
                    if hd:
                        for r, (c0, c1) in enumerate(RANGES):
                            act.wait_ge(d_wu, w0 + 8 * (hd - 1) + (2, 8)[r])
                            nc.scalar.copy(xn[:, hd - 1, c0:c1], banks[4 + r][:, 0:c1 - c0]).then_inc(d_numc, 1)
                for r, (c0, c1) in enumerate(RANGES):
                    act.wait_ge(d_wu, w0 + 8 * (MH - 1) + (2, 8)[r])
                    nc.scalar.copy(xn[:, MH - 1, c0:c1], banks[4 + r][:, 0:c1 - c0]).then_inc(d_numc, 1)

            @block.vector
            def _(dve):
                v = nc.vector

                def exponents(hd, b):
                    if b == 0:
                        dve.wait_ge(d_bc, hd + 1)
                        v.drain()
                    s0, n = BLK[b]
                    w = 528 - 128 * b if b < SB else NS
                    for lo, hi, bank, at in ((0, 256, 0, 256), (256, T, 1, -256)):
                        a, z = max(s0, lo), min(s0 + w, hi)
                        if a >= z:
                            continue
                        last = v.tensor_scalar(ebuf[hd % 2][0:n, EOFF[b] + a - s0:EOFF[b] + z - s0],
                                               banks[bank][0:n, a + at:z + at], TR[0:n, b, hd:hd + 1], 0.0,
                                               ALU.add, ALU.min)
                    if b == SB:
                        last.then_inc(d_e, 1)

                if mlstm:
                    for b in range(SB + 1):
                        exponents(0, b)
                for i, (hd, r, (b, t0, w)) in enumerate(ALL):
                    s0, n = BLK[b]
                    if mlstm and i % 8 == 0:
                        dve.wait_ge(d_x, hd + 1)
                    if mlstm:
                        dec = ebuf[hd % 2][0:n, EOFF[b] + t0 - s0:EOFF[b] + t0 - s0 + w]
                        diag = t0 == s0
                        if diag:
                            wd = min(w, n)
                            mask = smask[0:NS, 0:NS] if b == SB else tri_st[0:n, 0:wd]
                            v.tensor_tensor(dec[:, 0:wd], dec[:, 0:wd], mask, ALU.mult)
                            v.drain()
                    else:
                        dec = decay_s[0:n, hd, 0:NS] if b == SB else decay[0:n, hd, t0 - s0:t0 - s0 + w]
                    dve.wait_ge(d_s, w0 + i + 1)
                    if i >= 4:
                        dve.wait_ge(d_wu, w0 + i - 3)
                    v.tensor_tensor(wbuf[i % 4][0:n, 0:w], banks[2 + i % 2][0:n, 0:w], dec, ALU.mult).then_inc(d_w, 1)
                    if between is not None and i % 2:
                        between(dve, i // 2)
                    if mlstm and 1 <= i % 8 <= SB + 1 and hd + 1 < MH:
                        exponents(hd + 1, i % 8 - 1)

    s_prep = sem("state_rows")
    s_prep2 = sem("state_cols")
    with nc.Block() as block:
        @block.tensor
        def _(pe):
            for hd in range(MH):
                nc.tensor.matmul(banks[0][:, hd * NS:(hd + 1) * NS], head_row(4, hd), winter[:, :],
                                 start=True, stop=True)
            nc.tensor.matmul(banks[1][:, 0:32], nrow, ident[0:32, 0:32], start=True, stop=True,
                             is_transpose=True)
            for hd in range(MH):
                last = nc.tensor.matmul(banks[2][:, hd * NB:(hd + 1) * NB], head_row(4, hd), dec4,
                                        start=True, stop=True)
            last.then_inc(s_prep, 1)

        @block.vector
        def _(dve):
            v = nc.vector
            dve.wait_ge(s_prep, 1)
            v.tensor_copy(nst[:, :], banks[1][:, 0:32])
            v.tensor_copy(decs[:, :], banks[2][:, 0:32])
            for hd in range(MH):
                v.tensor_tensor(qs[:, hd, :], mq[:, hd, TP:T], banks[0][:, hd * NS:(hd + 1) * NS], ALU.mult)
            v.drain()
            for hd in range(MH):
                n = nst[:, :].rearrange("p (b h) -> p b h", h=MH)[:, :, hd:hd + 1].to_broadcast([128, NB, TS])
                v.tensor_tensor(nq[:, hd, :].rearrange("p (b t) -> p b t", t=TS),
                                qs[:, hd, :].rearrange("p (b t) -> p b t", t=TS), n, ALU.mult)

    bufs = scratch(flat(mv), flat(fv))
    decayed_attention(mq, mk, TK["mv"], Cst, bufs, True, store=store_kv)

    s_den, s_dbc, s_dbu, s_hm, s_sig = (sem(x) for x in ("den", "den_rows", "den_rows_used", "normalised", "sigmoid"))
    den = negM
    with nc.Block() as block:
        @block.vector
        def _(dve):
            v = nc.vector
            for r, (c0, c1) in enumerate(RANGES):
                v.tensor_copy(den[:, c0:c1], banks[6 + r][0:4, 0:c1 - c0])
            v.drain()
            v.scalar_tensor_tensor(out=den, in0=den, scalar=-1.0, in1=den, op0=ALU.mult, op1=ALU.max)
            v.drain()
            v.tensor_tensor(den, den, expm, ALU.max)
            v.drain()
            v.reciprocal(den, den).then_inc(s_den, 1)
            for i in range(2 * MH):
                hd, (c0, c1) = i // 2, RANGES[i % 2]
                dve.wait_ge(s_dbc, i + 1)
                v.tensor_tensor(xn[:, hd, c0:c1], xn[:, hd, c0:c1], banks[i % 4][:, 0:c1 - c0],
                                ALU.mult).then_inc(s_dbu, 1)

        @block.tensor
        def _(pe):
            pe.wait_ge(s_den, 1)
            for i in range(2 * MH):
                hd, (c0, c1) = i // 2, RANGES[i % 2]
                if i >= 4:
                    pe.wait_ge(s_dbu, i - 3)
                nc.tensor.matmul(banks[i % 4][:, 0:c1 - c0], head_row(4, hd), den[:, c0:c1],
                                 start=True, stop=True).then_inc(s_dbc, 1)

        @block.scalar
        def _(act):
            for hd in range(MH):
                nc.scalar.activation(mo[:, hd, :], mo[:, hd, :], ACT.Sigmoid).then_inc(s_sig, 1)

        @block.gpsimd
        def _(pool):
            for hd in range(MH):
                pool.wait_ge(s_sig, hd + 1)
                pool.wait_ge(s_dbu, 2 * hd + 2)
                nc.gpsimd.tensor_tensor(xn[:, hd, :], xn[:, hd, :], mo[:, hd, :], ALU.mult)

    u_v, u_u = sem("weighted_v"), sem("updates")

    def state_update(kt, vt, state, weight, decay, normaliser, bufs, between=None, beside={}, after=None):
        u0 = 0 if normaliser else MH
        ebuf, _ = bufs
        nv = 129 if normaliser else 128
        vw = [e[:, 0:5 * 129].rearrange("p (b v) -> p b v", b=5) for e in ebuf]
        vm = [e[0:NS, 0:1024].rearrange("p (b v) -> p b v", b=NB) for e in vmbuf]
        own = smask[:, 32:40]

        with nc.Block() as block:
            @block.vector
            def _(dve):
                v = nc.vector

                def sources(hd):
                    for b in range(SB):
                        n = BLK[b][1]
                        v.tensor_scalar(vw[hd % 2][0:n, b, 0:128], vt[0:n, b, hd * 128:(hd + 1) * 128],
                                        weight(n, b, hd), None, ALU.mult)
                        v.tensor_copy(vw[hd % 2][0:n, b, 128:129], weight(n, b, hd))
                    mw = mwbuf[:, hd % 2, :]
                    v.tensor_scalar(mw, own, weight(NS, SB, hd), None, ALU.mult)
                    v.drain()
                    for b in range(NB):
                        last = v.tensor_scalar(vm[hd % 2][:, b, :], vt[0:NS, SB, hd * 128:(hd + 1) * 128],
                                               mw[:, b:b + 1], None, ALU.mult)
                    last.then_inc(u_v, 1)

                sources(0)
                for hd in range(MH):
                    if hd + 1 < MH:
                        sources(hd + 1)
                    dve.wait_ge(u_u, u0 + hd + 1)
                    p = hd % 2
                    v.tensor_copy(cp[:, hd, 0:nv], banks[4 * p][:, 0:nv])
                    d = decay(hd)
                    for b in range(NB):
                        s = state[:, b * MH + hd, :]
                        v.scalar_tensor_tensor(out=s, in0=s, scalar=d if isinstance(d, float) else d[:, b:b + 1],
                                               in1=banks[4 * p + 1 + b // 4][:, (b % 4) * 128:(b % 4 + 1) * 128],
                                               op0=ALU.mult, op1=ALU.add)
                    if normaliser:
                        n = nst[:, :].rearrange("p (b h) -> p b h", h=MH)[:, :, hd]
                        v.tensor_tensor(n, n, d, ALU.mult)
                        v.drain()
                        v.tensor_tensor(n, n, banks[4 * p + 3][:, 0:NB], ALU.add)
                if after is not None:
                    after(dve)

            @block.tensor
            def _(pe):
                for hd in range(MH):
                    p = hd % 2
                    if between is not None:
                        between(pe, 2 * hd)
                    if hd == 0 and normaliser:
                        warm(6)
                    pe.wait_ge(u_v, u0 + hd + 1)
                    for b in range(SB):
                        n = BLK[b][1]
                        nc.tensor.matmul(banks[4 * p][:, 0:nv], kt[0:n, b, hd * 128:(hd + 1) * 128],
                                         vw[p][0:n, b, 0:nv], start=(b == 0), stop=(b == SB - 1))
                    ks = kt[0:NS, SB, hd * 128:(hd + 1) * 128]
                    for half in range(2):
                        last = nc.tensor.matmul(banks[4 * p + 1 + half][:, :], ks,
                                                vm[p][:, 4 * half:4 * half + 4, :].rearrange("p b v -> p (b v)"),
                                                start=True, stop=True)
                    if normaliser:
                        last = nc.tensor.matmul(banks[4 * p + 3][:, 0:NB], ks, mwbuf[:, p, :], start=True, stop=True)
                    last.then_inc(u_u, 1)
                    if between is not None:
                        between(pe, 2 * hd + 1)

            for name, work in beside.items():
                {"scalar": block.scalar, "gpsimd": block.gpsimd}[name](work)

    vmbuf = [flat(mk)[0:NS, 0:1024], flat(mk)[0:NS, 1024:2048]]
    decs_b = decs[:, :].rearrange("p (h b) -> p h b", h=MH)
    state_update(TK["mk"], TK["mv"], Cst, lambda n, b, hd: TR[0:n, b, 32 + hd:33 + hd],
                 lambda hd: decs_b[:, hd, :], True, bufs)

    s_st, s_nt, s_nr = sem("state_stored"), sem("norm_rows"), sem("norm_rows_copied")
    with nc.Block() as block:
        @block.tensor
        def _(pe):
            nc.tensor.matmul(banks[0][0:32, 0:128], nst[:, :], ident[:, :], start=True, stop=True, is_transpose=True)
            nc.tensor.matmul(banks[1][0:4, 0:128], cp[:, :, 128], ident[:, :], start=True, stop=True,
                             is_transpose=True).then_inc(s_nt, 1)

        @block.vector
        def _(dve):
            dve.wait_ge(s_nt, 1)
            nc.vector.tensor_copy(nrows[0:32, 0, :], banks[0][0:32, 0:128])
            nc.vector.tensor_copy(nrows[0:4, 1, :], banks[1][0:4, 0:128]).then_inc(s_nr, 1)

        @block.sync
        def _(sp):
            for b in range(NB):
                sp.dma_start(io["s_mlstm_C"][b].rearrange("h k v -> k h v"),
                             Cst[:, b * MH:(b + 1) * MH, :]).then_inc(s_st, 16)
            sp.dma_start(io["p_mlstm_C"][0].rearrange("h k v -> k h v"), cp[:, :, 0:128]).then_inc(s_st, 16)
            sp.wait_ge(s_nr, 1)
            sp.dma_start(io["s_mlstm_n"].rearrange("b h k -> (b h) k"), nrows[0:32, 0, :]).then_inc(s_st, 16)
            sp.dma_start(io["p_mlstm_n"][0], nrows[0:4, 1, :]).then_inc(s_st, 16)
            sp.wait_ge(s_kv, 16 * 14)

    cache_k = io["cache_fox_k"].rearrange("n t h d -> n t (h d)")
    cache_v = io["cache_fox_v"].rearrange("n t h d -> n t (h d)")
    k_full = [sem("k_full") for _ in range(PAGES)]
    v_full, v_used = [sem("v_full") for _ in range(4)], [sem("v_used") for _ in range(4)]

    def load_k(sp, b):
        for pg, page in enumerate(page_numbers(b)):
            sp.wait_ge(k_done[pg], b + 1)
            sp.dma_start(kpage[:, pg, :], cache_k[bass.ds(page, 1), :, :]
                         .rearrange("a t n -> (a t) n")).then_inc(k_full[pg], 16)

    def load_v(sp, b):
        slot = b % 4
        if b >= 4:
            sp.wait_ge(v_used[slot], 1)
        for pg, page in enumerate(page_numbers(b)):
            sp.dma_start(vpage[slot][:, pg * 512:(pg + 1) * 512],
                         cache_v[bass.ds(page, 1), :, :].rearrange("a t n -> (a t) n")).then_inc(v_full[slot], 16)

    inner_top.close()
    decode = ExitStack()
    kpage = proj[:, 0:4096].rearrange("p (g n) -> p g n", g=PAGES)
    vpage = [proj[:, 4096:8192], place(decode, "v_pages", [128, PAGES * 512]), None,
             ring[:, :, :].rearrange("p s n -> p (s n)")[:, 0:PAGES * 512]]
    fox = ExitStack()
    qh, kh = (place(fox, n, [128, 4, TP], F32R) for n in ("q_high", "k_high"))
    rows_h = place(fox, "rows_high", [FH, TP], F32R)
    idr, trir = (place(fox, n, [128, 128], F32R) for n in ("identity_r", "triangle_r"))
    fcol, mcol = (place(fox, n, [128, SB, FH]) for n in ("minus_F", "row_max"))
    fox_rows = place(fox, "fox_rows", [FH, TP])
    fst = place(right, "fst", [128, 4], side="right")
    UNITS = [(i, c, e) for i in range(SB - 1, -1, -1) for c in range(4) for e in range(2)]
    s_f8, s_fh, s_qk, s_kk, s_fc, s_fcc, s_s, s_m, s_mt, s_mn = (sem(x) for x in (
        "minus_F_rows", "F_high", "q_high", "k_high", "F_columns", "F_columns_copied", "max_scores", "row_max",
        "max_rows", "minus_max"))
    with nc.Block() as block:
        @block.scalar
        def _(act):
            nc.scalar.copy(idr[:, :], ident[:, :])
            nc.scalar.copy(trir[:, :], tri_ts[:, :])
            act.wait_ge(s_f8, 1)
            nc.scalar.copy(rows_h[:, :], fox_rows[:, :]).then_inc(s_fh, 1)
            for c in range(4):
                nc.scalar.copy(qh[:, c, :], fq[:, c, 0:TP]).then_inc(s_qk, 1)
            act.wait_ge(s_mn, 1)
            nc.scalar.copy(rows_h[:, :], fox_rows[:, :])

        @block.gpsimd
        def _(pool):
            nc.gpsimd.memset(fox_v[:, :, :, FD:], 0.0)
            nc.gpsimd.drain()
            for h_ in range(FH):
                nc.gpsimd.memset(fox_v[:, :, h_, FD + h_:FD + h_ + 1], 1.0)

        @block.tensor
        def _(pe):
            for b in range(SB):
                t0, n = BLK[b]
                last = nc.tensor.matmul(banks[4 + b // 3][0:n, (b % 3) * 128:(b % 3) * 128 + 72], CS[0:72, t0:t0 + n],
                                        ident[0:72, 0:72], start=True, stop=True, is_transpose=True)
            last.then_inc(s_fc, 1)
            pe.wait_ge(s_fh, 1)
            for n, (i, c, e) in enumerate(UNITS):
                t0, r = BLK[i]
                if n < 8 and e == 0:
                    pe.wait_ge(s_qk, c + 1)
                    pe.wait_ge(s_kk, c + 1)
                if n >= 2:
                    pe.wait_ge(s_m, n - 1)
                at, p = 1024 * (n % 2), slice(64 * e, 64 * e + 64)
                for s0, s1 in [(0, min(512, t0 + r))] + ([(512, TP)] if i == SB - 1 else []):
                    out, diag = psum[0:r, at + s0:at + s1], s1 > t0
                    nc.tensor.matmul(out, qh[p, c, t0:t0 + r], kh[p, c, s0:s1], start=True, stop=False)
                    own = idr[0:FH, 2 * c + e:2 * c + e + 1].to_broadcast([FH, r])
                    last = nc.tensor.matmul(out, own, rows_h[:, s0:s1], start=False, stop=not diag)
                    if diag:
                        last = nc.tensor.matmul(psum[0:r, at + t0:at + t0 + r], idr[0:r, 0:r], trir[0:r, 0:r],
                                                start=False, stop=True)
                last.then_inc(s_s, 1)
            pe.wait_ge(s_m, len(UNITS))
            for b in range(SB):
                t0, n = BLK[b]
                at = 3072 + t0 if b < 4 else 3584
                last = nc.tensor.matmul(psum[0:FH, at:at + n], mcol[0:n, b, :], ident[0:n, 0:n], start=True,
                                        stop=True, is_transpose=True)
            last.then_inc(s_mt, 1)

        @block.vector
        def _(dve):
            v = nc.vector
            v.tensor_scalar(fox_rows[:, :], CS[64:72, 0:TP], -1.0 / FOX_SCALE, None, ALU.mult).then_inc(s_f8, 1)
            for c in range(4):
                v.tensor_copy(kh[:, c, :], fk[:, c, 0:TP]).then_inc(s_kk, 1)
            dve.wait_ge(s_fc, 1)
            for b in range(SB):
                n = BLK[b][1]
                v.tensor_scalar(fcol[0:n, b, :], banks[4 + b // 3][0:n, (b % 3) * 128 + 64:(b % 3) * 128 + 72], -1.0,
                                None, ALU.mult)
            for n, (i, c, e) in enumerate(UNITS):
                r, w = BLK[i][1], BLK[i][0] + BLK[i][1]
                dve.wait_ge(s_s, n + 1)
                v.reduce_max(mcol[0:r, i, 2 * c + e:2 * c + e + 1], psum[0:r, 1024 * (n % 2):1024 * (n % 2) + w],
                             AX_X).then_inc(s_m, 1)
            dve.wait_ge(s_mt, 1)
            v.tensor_scalar(fox_rows[:, 0:512], psum[0:FH, 3072:3584], -1.0, None, ALU.mult)
            v.tensor_scalar(fox_rows[:, 512:TP], psum[0:FH, 3584:3600], -1.0, None, ALU.mult).then_inc(s_mn, 1)

        s_ln = sem("new_lf_stored")

        @block.sync
        def _(sp):
            sp.dma_start(lf_new, CS[64:72, TP:T]).then_inc(s_ln, 16)
            sp.wait_ge(s_ln, 16)
            sp.wait_ge(s_st, 16 * 11)

    FTILES = [[(0, 0, 256), (1, 128, 128)], [(0, 256, 272), (1, 256, 272), (2, 256, 272), (3, 384, 144), (4, 512, 16)]]
    FR = [(0, 256), (256, TP)]
    FALL = [(hd, r, tile) for hd in range(FH) for r in range(2) for tile in FTILES[r]]
    per_head = len(FALL) // FH
    pt = [flat(fv)[:, 272 * i:272 * (i + 1)] for i in range(4)]
    rden = fox_rows
    s_fs, s_fx, s_fp, s_fo, s_fd, s_fb, s_fn = (sem(x) for x in (
        "fox_scores", "fox_exps", "fox_products", "fox_out_copied", "fox_den", "fox_den_rows", "fox_scaled"))
    with nc.Block() as block:
        @block.tensor
        def _(pe):
            def score(i):
                hd, r, (b, t0, w) = FALL[i]
                c, p = hd // 2, slice(64 * (hd % 2), 64 * (hd % 2) + 64)
                s0, n = BLK[b]
                if i >= 2:
                    pe.wait_ge(s_fx, i - 1)
                out = banks[2 + i % 2][0:n, 0:w]
                own = idr[0:FH, hd:hd + 1].to_broadcast([FH, n])
                diag = t0 == s0
                nc.tensor.matmul(out, fk[p, c, s0:s0 + n], fq[p, c, t0:t0 + w], start=True, stop=False)
                last = nc.tensor.matmul(out, own, rows_h[:, t0:t0 + w], start=False, stop=not diag)
                if diag:
                    last = nc.tensor.matmul(banks[2 + i % 2][0:n, 0:n], trir[0:n, 0:n], idr[0:n, 0:n],
                                            start=False, stop=True)
                last.then_inc(s_fs, 1)

            warm(3)
            score(0)
            for i, (hd, r, (b, t0, w)) in enumerate(FALL):
                if i + 1 < len(FALL):
                    score(i + 1)
                n = BLK[b][1]
                first, final = b == 0, b == (1, SB - 1)[r]
                c0 = t0 - FR[r][0]
                if first and hd >= 2:
                    pe.wait_ge(s_fo, 2 * (hd - 2) + r + 1)
                pe.wait_ge(s_fx, i + 1)
                nc.tensor.matmul(banks[4 + 2 * (hd % 2) + r][0:VW, c0:c0 + w], fox_v[0:n, b, hd, :],
                                 pt[i % 4][0:n, 0:w], start=first, stop=final, skip_group_check=True).then_inc(s_fp, 1)
            pe.wait_ge(s_fd, 1)
            for i in range(8):
                c, (c0, c1) = i // 2, FR[i % 2]
                if i >= 4:
                    pe.wait_ge(s_fn, i - 3)
                for e in range(2):
                    last = nc.tensor.matmul(banks[i % 4][64 * e:64 * e + 64, 0:c1 - c0],
                                            ident[0:FH, 2 * c + e:2 * c + e + 1].to_broadcast([FH, 64]),
                                            rden[:, c0:c1], start=True, stop=True)
                last.then_inc(s_fb, 1)

        @block.scalar
        def _(act):
            for i, (hd, r, (b, t0, w)) in enumerate(FALL):
                n = BLK[b][1]
                act.wait_ge(s_fs, i + 1)
                if i >= 4:
                    act.wait_ge(s_fp, i - 3)
                nc.scalar.activation(pt[i % 4][0:n, 0:w], banks[2 + i % 2][0:n, 0:w], ACT.Exp,
                                     bias=fcol[0:n, b, hd:hd + 1], scale=FOX_SCALE).then_inc(s_fx, 1)

        @block.vector
        def _(dve):
            v = nc.vector
            v.memset(rden[:, :], 0.0)
            for hd in range(FH):
                e = hd % 2
                for r, (c0, c1) in enumerate(FR):
                    dve.wait_ge(s_fp, per_head * hd + (2, per_head)[r])
                    bank = banks[4 + 2 * e + r]
                    v.tensor_copy(xn[64 * e:64 * e + 64, 4 + hd // 2, c0:c1], bank[0:FD, 0:c1 - c0])
                    v.drain()
                    v.tensor_tensor(rden[:, c0:c1], rden[:, c0:c1], bank[FD:VW, 0:c1 - c0], ALU.add).then_inc(s_fo, 1)
            v.drain()
            v.reciprocal(rden[:, :], rden[:, :]).then_inc(s_fd, 1)
            for i in range(8):
                c, (c0, c1) = i // 2, FR[i % 2]
                dve.wait_ge(s_fb, i + 1)
                v.tensor_tensor(xn[:, 4 + c, c0:c1], xn[:, 4 + c, c0:c1], banks[i % 4][:, 0:c1 - c0],
                                ALU.mult).then_inc(s_fn, 1)

        @block.sync
        def _(sp):
            load_k(sp, 0)
            load_v(sp, 0)
            load_v(sp, 1)
            load_v(sp, 3)
    fox.close()

    vpage[2] = place(decode, "v_pages", [128, PAGES * 512])
    S = place(decode, "past_probs", [128, PAST + TS])[:, :]
    KT = states[:, :].rearrange("p (f c s) -> p f c s", f=2, c=4)
    Frow = flat(fv)[:, 0:PAST + TS]
    PT = flat(fv)[:, 1028:1028 + 9 * 128].rearrange("p (g n) -> p g n", g=9)
    Qbd = proj[:, 8192:8192 + 512].rearrange("p (c b n) -> p c b n", c=4, b=4)
    Pn = proj[:, 8704:8704 + 32]
    s_F, s_q0, s_q, s_sc = sem("F_loaded"), sem("q_zeroed"), sem("q_spread"), sem("past_scores")
    s_kc = [sem("kT_by_vector"), sem("kT_by_scalar")]

    s_m2, s_x2, s_p2, s_t2, s_t2c, s_o2, s_o2c = (sem(x) for x in (
        "past_max", "past_exps", "past_probs", "past_probs_T", "past_probs_T_copied", "past_out", "past_out_scaled"))
    for g in range(2):
        with nc.Block() as block:
            @block.sync
            def _(sp):
                with sp.Fori(1, 4) as b4:
                    load_k(sp, b4 + 4 * g)
                for b in (2,) if g == 0 else (5, 6, 7):
                    load_v(sp, b)

            @block.gpsimd
            def _(pool):
                nc.gpsimd.memset(proj[:, 8192:8192 + 512], 0.0).then_inc(s_q0, 1)
                for b4 in range(4):
                    b = 4 * g + b4
                    pool.dma_start(Frow[32 * b4:32 * b4 + 32, 0:PAST],
                                   lf_past[b].unsqueeze(1).to_broadcast([FH, TS, PAST])).then_inc(s_F, 16)
                    pool.dma_start(Frow[32 * b4:32 * b4 + 32, PAST:PAST + TS],
                                   lf_new[:, b * TS:(b + 1) * TS].unsqueeze(1).to_broadcast([FH, TS, TS])).then_inc(s_F, 16)

            @block.tensor
            def _(pe):
                def scores(b4, f):
                    for e in range(2):
                        pe.wait_ge(s_kc[e], g * 16 + (b4 * 8 + f * 4 + 4) // 2)
                    for c in range(4):
                        last = nc.tensor.matmul(psum[32 * b4:32 * b4 + 32, 512 * f:512 * f + 512], Qbd[:, c, b4, :],
                                                KT[:, f, c, :], start=(c == 0), stop=(c == 3))
                    last.then_inc(s_sc, 1)

                for j in range(4 * PAGES):
                    b4, pg = j // PAGES, j % PAGES
                    pe.wait_ge(k_full[pg], 16 * (4 * g + b4 + 1))
                    if j >= 4:
                        pe.wait_ge(s_kc[j % 2], g * 16 + (j - 4) // 2 + 1)
                    for c in range(4):
                        last = nc.tensor.matmul(banks[4 + j % 4][:, c * 128:(c + 1) * 128],
                                                kpage[:, pg, c * 128:(c + 1) * 128], ident[:, :],
                                                start=True, stop=True, is_transpose=True)
                    last.then_inc(k_done[pg], 1)
                    if j == 0:
                        pe.wait_ge(s_q, g + 1)
                    if j % 4 == 1 and j >= 4:
                        scores((j // 4 - 1) // 2, (j // 4 - 1) % 2)
                scores(3, 1)
                for b4 in range(4):
                    t0 = TP + (4 * g + b4) * TS
                    for c in range(4):
                        nc.tensor.matmul(banks[2][32 * b4:32 * b4 + 32, 0:TS], Qbd[:, c, b4, :], fk[:, c, t0:t0 + TS],
                                         start=(c == 0), stop=(c == 3))

            def kt_copy(eng, copy, e):
                for j in range(e, 4 * PAGES, 2):
                    b4, pg = j // PAGES, j % PAGES
                    f = pg // 4
                    eng.wait_ge(k_done[pg], 4 * g + b4 + 2)
                    if b4:
                        eng.wait_ge(s_sc, g * 8 + 2 * (b4 - 1) + f + 1)
                    copy(KT[:, f, :, (pg % 4) * 128:(pg % 4 + 1) * 128],
                         banks[4 + j % 4].rearrange("p (c s) -> p c s", c=4)).then_inc(s_kc[e], 1)

            @block.vector
            def _(dve):
                v = nc.vector
                dve.wait_ge(s_q0, g + 1)
                for c in range(4):
                    for e in range(2):
                        last = v.tensor_copy(Qbd[64 * e:64 * e + 64, c, :, (2 * c + e) * TS:(2 * c + e + 1) * TS],
                                             fq[64 * e:64 * e + 64, c, TP + 16 * g:TP + 16 * g + 16]
                                             .rearrange("p (b q) -> p b q", b=4))
                last.then_inc(s_q, 1)
                kt_copy(dve, lambda d, s: v.tensor_copy(d, s), 0)
                v.memset(S[:, 0:PAST], 1.0)
                dve.wait_ge(s_F, 128 * (g + 1))
                v.drain()
                v.tensor_tensor_scan(Frow[:, 0:PAST], S[:, 0:PAST], Frow[:, 0:PAST], 0.0, ALU.mult, ALU.add)
                v.drain()
                v.tensor_scalar(Frow[:, PAST:], Frow[:, PAST:], Frow[:, PAST - 1:PAST], None, ALU.add)

            @block.scalar
            def _(act):
                kt_copy(act, lambda d, s: nc.scalar.copy(d, s), 1)

        st = fst[:, :]
        with nc.Block() as block:
            @block.vector
            def _(dve):
                v = nc.vector
                v.scalar_tensor_tensor(out=S, in0=psum[:, 0:PAST + TS], scalar=FOX_SCALE, in1=Frow,
                                       op0=ALU.mult, op1=ALU.subtract)
                v.drain()
                v.tensor_tensor(S[:, PAST:], S[:, PAST:], newmask, ALU.add)
                v.drain()
                v.reduce_max(st[:, 0:1], S, AX_X)
                v.drain()
                v.tensor_scalar(st[:, 1:2], st[:, 0:1], -1.0, None, ALU.mult).then_inc(s_m2, 1)
                dve.wait_ge(s_x2, g + 1)
                v.reciprocal(st[:, 3:4], st[:, 2:3])
                v.tensor_tensor(Pn.rearrange("p (b t) -> p b t", b=NB),
                                S[:, PAST:].unsqueeze(1).to_broadcast([128, NB, TS]),
                                bmask[:, g, :].rearrange("p (b t) -> p b t", b=NB), ALU.mult).then_inc(s_p2, 1)
                for i in range(2):
                    dve.wait_ge(s_t2, 3 * g + i + 1)
                    v.tensor_copy(PT[:, 4 * i:4 * i + 4, :], banks[4 + i].rearrange("p (g n) -> p g n", g=4))
                dve.wait_ge(s_t2, 3 * g + 3)
                v.tensor_copy(PT[0:NS, 8, :], banks[6][0:NS, 0:128]).then_inc(s_t2c, 1)
                dve.wait_ge(v_used[3], g + 1)
                v.tensor_scalar(S[:, 0:512], banks[3], st[:, 3:4], None, ALU.mult).then_inc(s_o2c, 1)
                dve.wait_ge(s_o2, g + 1)
                acc = banks[7].rearrange("p (c b n) -> p c b n", b=4, c=4)
                for c in range(4):
                    for e in range(2):
                        v.tensor_copy(xn[64 * e:64 * e + 64, 4 + c, TP + 16 * g:TP + 16 * g + 16]
                                      .rearrange("p (b q) -> p b q", b=4),
                                      acc[64 * e:64 * e + 64, c, :, (2 * c + e) * TS:(2 * c + e + 1) * TS])

            @block.scalar
            def _(act):
                act.wait_ge(s_m2, g + 1)
                nc.scalar.activation(S, S, ACT.Exp, bias=st[:, 1:2], scale=1.0, accum_out=st[:, 2:3]).then_inc(s_x2, 1)

            @block.tensor
            def _(pe):
                warm(7, 4)
                pe.wait_ge(s_p2, g + 1)
                for i in range(2):
                    for j in range(4):
                        last = nc.tensor.matmul(banks[4 + i][:, j * 128:(j + 1) * 128],
                                                S[:, (4 * i + j) * 128:(4 * i + j + 1) * 128], ident[:, :],
                                                start=True, stop=True, is_transpose=True)
                    last.then_inc(s_t2, 1)
                nc.tensor.matmul(banks[6][0:NS, 0:128], Pn, ident[:, :], start=True, stop=True,
                                 is_transpose=True).then_inc(s_t2, 1)
                pe.wait_ge(s_t2c, g + 1)
                for b4 in range(4):
                    slot, use = b4, g
                    pe.wait_ge(v_full[slot], 128 * (use + 1))
                    at, own = banks[3][32 * b4:32 * b4 + 32, :], slice(b4 * 32, b4 * 32 + 32)
                    for pg in range(PAGES):
                        nc.tensor.matmul(at, PT[:, pg, own], vpage[slot][:, pg * 512:(pg + 1) * 512],
                                         start=(pg == 0), stop=False)
                    nc.tensor.matmul(at, PT[0:NS, 8, own], fox_values[0:NS, SB],
                                     start=False, stop=True).then_inc(v_used[slot], 1)
                pe.wait_ge(s_o2c, g + 1)
                for c in range(4):
                    last = nc.tensor.matmul(banks[7][:, c * 128:(c + 1) * 128], S[:, c * 128:(c + 1) * 128], ident[:, :],
                                            start=True, stop=True, is_transpose=True)
                last.then_inc(s_o2, 1)

            @block.sync
            def _(sp):
                if g == 0:
                    load_k(sp, 4)
                    load_v(sp, 4)
    decode.close()

    s_mh = sem("mixed_high")
    closed = [0]
    ffn_out = None

    def close_layer(layer, units, load_first=False):
        nonlocal left, right, pieces, ffn_out
        m, closed[0] = closed[0], closed[0] + 1
        inner.close()
        right.close()
        right = ExitStack()
        pieces = put_pieces(right, "right")
        above = ExitStack()
        x = put_split(above, "mixed", KC, "right")
        high, low, _ = splitters(1, KC, pieces)
        with nc.Block() as block:
            @block.sync
            def _(sp):
                if load_first:
                    prefetch(sp, units[0])

            @block.scalar
            def _(act):
                for k in range(KC):
                    nc.scalar.copy(x[0][:, k, :], xn[:, k, :]).then_inc(s_mh, 1)
                    if k == 5:
                        high(act, 0, 0, 0)
                high(act, 0, 0, 1)

            def split_x(eng, ne, k):
                eng.wait_ge(s_mh, KC * m + k + 1)
                ne.tensor_tensor(x[1][:, k, :], xn[:, k, :], x[0][:, k, :].bitcast(F32), ALU.subtract)

            @block.vector
            def _(dve):
                for k in (0, 2, 3, 5, 6):
                    split_x(dve, nc.vector, k)
                for p in range(2):
                    low(dve, 0, 0, p)

            @block.gpsimd
            def _(pool):
                for k in (1, 4, 7):
                    split_x(pool, nc.gpsimd, k)
        left.close()
        left = ExitStack()
        inner_ = ExitStack()
        o = place(inner_, "projected_out", [128, KC, T])
        squares = place(inner_, "squares", [128, KC, T])
        project(units[0], 1, 2, KC, chunk(x), o, 0, pieces, then=up[layer], split=True)
        norm(o, (layer, 1), (layer, 2), squares, x, splitters(2, KC, pieces, True))
        inner_.close()
        inner_ = ExitStack()
        hid = put_split(inner_, "hidden", FC, "left")
        silu = ExitStack()
        project(up[layer], 2, FC // 2, KC, chunk(x), hid, 0, pieces, then=down[layer],
                silu=place(silu, "silu", [128, 2, T]), normed=True, following=(1, FC, False))
        silu.close()
        above.close()
        ffn_out = place(right, "ffn_out", [128, KC, T], side="right")
        project(down[layer], 1, 4, FC, chunk(hid), ffn_out, 0, pieces, then=units[1], split=True)
        inner_.close()

    close_layer(0, (out_even, odd), True)

    s_odd, s_rope = sem("odd_constants"), sem("rope_loaded")
    pieces = put_pieces(left)
    xn = put_split(left, "normed", KC, "left")
    with ExitStack() as scratch_:
        norm(ffn_out, (0, 3), (1, 0), place(scratch_, "squares", [128, KC, T]), xn, splitters(1, KC, pieces))
    right.close()
    right = ExitStack()
    proj = place(right, "projected", [128, 7 * 4 * T], side="right")
    cp, mwbuf, qs, lam, fin = (place(right, n, shape, side="right") for n, shape in (
        ("cp", [128, MH, 129]), ("mwbuf", [NS, 2, NB]), ("qs", [128, MH, NS]), ("lam", [128, 4, 4]),
        ("fin", [128, 2, 32])))
    rope = proj[:, 6 * 4 * T:6 * 4 * T + 2 * T].rearrange("p (a t) -> p a t", a=2)

    Pt = proj[:, :].rearrange("p (k t) -> p k t", k=28)
    P = proj[:, :].rearrange("p (a k t) -> p a k t", a=7, k=4)
    project(odd, 1, 6, KC, chunk(xn), Pt, 0, pieces, then=out_odd, normed=True)
    rq, rk, rv, rg, lx, lgate = (P[:, a] for a in range(6))
    left.close()
    left = ExitStack()
    xn, inner, states, spare, inner_top, tok = place_mixer()
    tokf = tok[:, :, :, :].rearrange("p a b c -> p (a b c)")
    TK = {"mk": tok[:, 0], "mv": tok[:, 1]}
    Cst = states[:, :].rearrange("p (s v) -> p s v", v=128)
    sparef = spare[:, :, :, :].rearrange("p b h n -> p (b h n)")
    xc = place(right, "convolved", [128, 4, T], side="right")
    lru_s = place(right, "lru_samples", [128, 256], side="right")
    us = lru_s[:, 0:224].rearrange("p (c b u) -> p c b u", c=4, b=NB)
    h0 = lru_s[:, 224:256]
    conv_in, h0_in = sparef[0:24, 2816:3328], sparef[0:32, 3328:3456]
    wab = proj[:, 6 * 4 * T + 2 * T:6 * 4 * T + 2 * T + 1024].rearrange("p (a c j) -> p a c j", a=2, c=4)
    s_li, s_lz = sem("lru_loaded"), sem("lru_zeroed")
    dtab = tokf[:, 6144:6144 + MH * TP].rearrange("p (h t) -> p h t", h=MH)

    s_ks, s_sw, s_xc, s_xs = sem("k_scaled"), sem("swapped"), sem("times_cos"), sem("times_sin")
    s_st2, s_ro = sem("ret_state"), sem("rotated")
    rtmp = [tokf[:, T * i:T * (i + 1)] for i in range(2)]
    RX = [a[:, hd, :] for a in (rq, rk) for hd in range(MH)]
    with nc.Block() as block:
        @block.sync
        def _(sp):
            sp.dma_start(rope, io["c_rope"]).then_inc(s_rope, 16)
            for b in range(NB):
                sp.dma_start(Cst[:, b * MH:(b + 1) * MH, :],
                             io["state_ret_S"][b].rearrange("h k v -> k h v")).then_inc(s_st2, 16)
            sp.dma_start(dtab, io["c_decay"]).then_inc(s_odd, 16)
            sp.dma_start(conv_in, io["state_lru_conv"].rearrange("b j n -> (b j) n")).then_inc(s_li, 16)
            sp.dma_start(h0_in, io["state_lru_h"].rearrange("b (k p) -> (b k) p", p=128)).then_inc(s_li, 16)
            sp.wait_ge(s_lz, 1)
            for a, name in enumerate(("lru_wa", "lru_wx")):
                for e in range(2):
                    sp.dma_start(wab[64 * e:64 * e + 64, a, :, 64 * e:64 * e + 64],
                                 io[name].rearrange("(c e) i j -> e i c j", e=2)[e]).then_inc(s_li, 16)
            sp.wait_ge(s_li, 16 * 6)
            sp.wait_ge(s_odd, 16)
            sp.wait_ge(s_st2, 16 * 8)

        @block.scalar
        def _(act):
            nc.scalar.mul(rk[:, :, :], rk[:, :, :], QK_SCALE).then_inc(s_ks, 1)

        @block.tensor
        def _(pe):
            for i, x in enumerate(RX):
                if i == MH:
                    pe.wait_ge(s_ks, 1)
                if i >= 4:
                    pe.wait_ge(s_xs, i - 3)
                for half in range(2):
                    last = nc.tensor.matmul(banks[2 * (i % 4) + half][:, 0:HALF], swap[:, :],
                                            x[:, half * HALF:(half + 1) * HALF], start=True, stop=True)
                last.then_inc(s_sw, 1)

        @block.gpsimd
        def _(pool):
            nc.gpsimd.memset(wab[:, :, :, :], 0.0).then_inc(s_lz, 1)
            for i, x in enumerate(RX):
                pool.wait_ge(s_sw, i + 1)
                if i == 0:
                    pool.wait_ge(s_rope, 16)
                nc.gpsimd.tensor_tensor(x, x, rope[:, 0, :], ALU.mult).then_inc(s_xc, 1)

        @block.vector
        def _(dve):
            for i, x in enumerate(RX):
                dve.wait_ge(s_sw, i + 1)
                if i == 0:
                    dve.wait_ge(s_rope, 16)
                nc.vector.drain()
                for half in range(2):
                    last = nc.vector.tensor_tensor(rtmp[i % 2][:, half * HALF:(half + 1) * HALF],
                                                   banks[2 * (i % 4) + half][:, 0:HALF],
                                                   rope[:, 1, half * HALF:(half + 1) * HALF], ALU.mult)
                last.then_inc(s_xs, 1)
                nc.vector.drain()
                dve.wait_ge(s_xc, i + 1)
                nc.vector.tensor_tensor(x, x, rtmp[i % 2], ALU.add)
            for hd in range(MH):
                nc.vector.tensor_tensor(qs[:, hd, :], rq[:, hd, TP:T], dsm[:, hd, NS:2 * NS], ALU.mult)

    jobs = token_major([(TK["mk"], rk), (TK["mv"], rv)])
    jobs += [([(conv_in[:, c * 128:(c + 1) * 128], 0)],
              lambda cp_, bank, c=c: cp_(us[:, c, :, 0:3], bank[:, 0:24].rearrange("p (b j) -> p b j", j=3)))
             for c in range(4)]
    jobs.append(([(h0_in, 0)], lambda cp_, bank: cp_(h0, bank[:, 0:32])))
    transposes(jobs)

    s_us, s_gl, s_gs, s_lm, s_ln2, s_a, s_r = (sem(x) for x in (
        "new_inputs", "gate_logits", "gates", "lambda_by_scalar", "lambda_by_gpsimd", "decay_done",
        "root_done"))
    ga = tokf[:, 6144:6144 + 4 * T].rearrange("p (c t) -> p c t", c=4)
    gi = sparef[:, 1216:1216 + 4 * T].rearrange("p (c t) -> p c t", c=4)
    gt = rq
    a2 = [flat(rv)[:, 700:700 + T], flat(rv)[:, 1300:1300 + T]] + [proj[:, 6 * 4 * T + T * i:6 * 4 * T + T * (i + 1)]
                                                                  for i in range(2)]

    def lambda_by_scalar(act):
        nc.scalar.activation(lam[:, 0, :], cols[:, LLAM:LLAM + 4], ACT.Abs)
        nc.scalar.drain()
        nc.scalar.activation(lam[:, 1, :], lam[:, 0, :], ACT.Exp, scale=-1.0).then_inc(s_lm, 1)
        act.wait_ge(s_ln2, 1)
        nc.scalar.activation(lam[:, 1, :], lam[:, 1, :], ACT.Ln).then_inc(s_lm, 1)
        nc.scalar.activation(rg[:, :, :], rg[:, :, :], ACT.Silu)
        nc.scalar.activation(lgate[:, :, :], lgate[:, :, :], ACT.Gelu_apprx_tanh)

    def lambda_by_gpsimd(pool):
        g = nc.gpsimd
        pool.wait_ge(s_lm, 1)
        g.tensor_scalar(lam[:, 1, :], lam[:, 1, :], 1.0, None, ALU.add).then_inc(s_ln2, 1)
        g.tensor_scalar(lam[:, 2, :], cols[:, LLAM:LLAM + 4], -1.0, 0.0, ALU.mult, ALU.max)
        g.drain()
        pool.wait_ge(s_lm, 2)
        g.tensor_tensor(lam[:, 1, :], lam[:, 1, :], lam[:, 2, :], ALU.add)
        g.drain()
        g.tensor_scalar(lam[:, 2, :], lam[:, 1, :], 8.0, None, ALU.mult)
        g.tensor_scalar(lam[:, 3, :], lam[:, 1, :], -8.0, None, ALU.mult)
        g.tensor_scalar(lam[:, 0, :], lam[:, 1, :], -16.0, None, ALU.mult)
        for c in range(4):
            g.tensor_copy(us[:, c, :, 3:7], lx[:, c, TP:T].rearrange("p (b t) -> p b t", t=TS)).then_inc(s_us, 1)

    def convolution(dve, i):
        v = nc.vector
        if i < 4:
            dve.wait_ge(s_us, 4)
        j, c = (3, 0, 1, 2)[i // 4], i % 4
        w, bias, d = cols[:, CONVW + 4 * j + c:CONVW + 4 * j + c + 1], cols[:, CONVB + c:CONVB + c + 1], 3 - j
        new, old = xc[:, c, TP:T].rearrange("p (b t) -> p b t", t=TS), us[:, c, :, j:j + 4]
        if j == 3:
            v.tensor_scalar(xc[:, c, 0:TP], lx[:, c, 0:TP], w, bias, ALU.mult, ALU.add)
            v.tensor_scalar(new, old, w, bias, ALU.mult, ALU.add)
            return
        v.drain()
        v.scalar_tensor_tensor(out=xc[:, c, d:TP], in0=lx[:, c, 0:TP - d], scalar=w, in1=xc[:, c, d:TP],
                               op0=ALU.mult, op1=ALU.add)
        v.scalar_tensor_tensor(out=new, in0=old, scalar=w, in1=new, op0=ALU.mult, op1=ALU.add)

    def gate_banks(i):
        return (banks[4], banks[5]) if i in (1, 3, 5) else (banks[3], banks[7])

    def lru_gate(pe, i):
        c, a = i // 2, i % 2
        if i >= 2:
            pe.wait_ge(s_gs, i if i == 7 else i - 1)
        for half in range(2):
            last = nc.tensor.matmul(gate_banks(i)[half][:, 0:HALF], wab[:, a, c, :],
                                    xc[:, c, half * HALF:(half + 1) * HALF], start=True, stop=True)
        last.then_inc(s_gl, 1)

    def lru_gates(pe, at):
        for i in ((0, 1, 2, 3), (4, 5), (), (6, 7), (), (), (), ())[at]:
            lru_gate(pe, i)
        if at == 2:
            pe.wait_ge(s_gs, 6)

    def lru_by_scalar(act):
        for i in range(8):
            c, a = i // 2, i % 2
            bias = cols[:, (LBA, LBX)[a] + c:(LBA, LBX)[a] + c + 1]
            act.wait_ge(s_gl, i + 1)
            for half in range(2):
                last = nc.scalar.activation((ga, gi)[a][:, c, half * HALF:(half + 1) * HALF],
                                            gate_banks(i)[half][:, 0:HALF], ACT.Sigmoid, bias=bias)
            last.then_inc(s_gs, 1)
        nc.scalar.drain()
        for c in range(4):
            nc.scalar.activation(gt[:, c, :], ga[:, c, :], ACT.Tanh, scale=lam[:, 2, c:c + 1])
        nc.scalar.drain()
        for c in range(4):
            nc.scalar.activation(a2[c], ga[:, c, :], ACT.Exp, scale=lam[:, 0, c:c + 1]).then_inc(s_a, 1)

    def lru_by_gpsimd(pool):
        g = nc.gpsimd
        for c in range(4):
            pool.wait_ge(s_gs, 2 * c + 2)
            g.tensor_tensor(gi[:, c, :], gi[:, c, :], xc[:, c, :], ALU.mult)

    def one_minus_a2(dve):
        for c in range(4):
            dve.wait_ge(s_a, c + 1)
            nc.vector.scalar_tensor_tensor(out=gt[:, c, :], in0=a2[c], scalar=1.0, in1=gt[:, c, :],
                                           op0=ALU.add, op1=ALU.mult)

    bufs = scratch(flat(rv), sparef)
    decayed_attention(rq, rk, TK["mv"], Cst, bufs, False, dtab, dsm[:, :, 0:NS],
                      lambda_by_scalar, lambda_by_gpsimd, convolution)
    vmbuf = [flat(rk)[0:NS, 0:1024], flat(rk)[0:NS, 1024:2048]]
    state_update(TK["mk"], TK["mv"], Cst, lambda n, b, hd: dsm[0:n, hd, 2 * NS + b:2 * NS + b + 1],
                 lambda hd: GAMMA4[hd], False, bufs, lru_gates, {"scalar": lru_by_scalar, "gpsimd": lru_by_gpsimd},
                 one_minus_a2)

    s_mu, s_hc, s_sq, s_var, s_iv, s_sd, s_bc, s_hn = (sem(x) for x in (
        "head_sum", "centred", "head_sq", "head_var", "inv_var_rows", "rstd_rows", "rstd_bc", "head_normed"))
    s_rs, s_h = sem("ret_stored"), sem("recurrence")
    hs = tokf[:, 0:4 * T].rearrange("p (c t) -> p c t", c=4)
    fin2 = flat(rv)[:, 1400:1400 + 4 * 27].rearrange("p (c n) -> p c n", c=4)
    vrow = rstd[0:4, :]
    sqh = [flat(rk)[:, T * i:T * (i + 1)] for i in range(4)]

    def recurrence_inputs(dve, v):
        for c in range(4):
            dve.wait_ge(s_r, c + 1)
            v.tensor_tensor(gi[:, c, :], gi[:, c, :], gt[:, c, :], ALU.mult)
        v.drain()
        dve.wait_ge(s_a, 8)
        a_, b_, h_ = (t[:, :, TP:T].rearrange("p c (b t) -> p c b t", t=TS) for t in (ga, gi, hs))
        prev = h0.rearrange("p (b k) -> p k b", k=4)
        for t in range(TS):
            v.tensor_tensor(h_[:, :, :, t], a_[:, :, :, t], prev, ALU.mult)
            v.drain()
            v.tensor_tensor(h_[:, :, :, t], h_[:, :, :, t], b_[:, :, :, t], ALU.add)
            v.drain()
            prev = h_[:, :, :, t]

    def recurrence(v, c):
        v.tensor_tensor_scan(hs[:, c, 0:TP], ga[:, c, 0:TP], gi[:, c, 0:TP], 0.0, ALU.mult, ALU.add).then_inc(s_h, 1)

    with nc.Block() as block:
        @block.sync
        def _(sp):
            for b in range(NB):
                sp.dma_start(io["s_ret_S"][b].rearrange("h k v -> k h v"),
                             Cst[:, b * MH:(b + 1) * MH, :]).then_inc(s_rs, 16)
            sp.dma_start(io["p_ret_S"][0].rearrange("h k v -> k h v"), cp[:, :, 0:128]).then_inc(s_rs, 16)
            sp.wait_ge(s_rs, 16 * 9)

        @block.tensor
        def _(pe):
            def variance(hd):
                pe.wait_ge(s_sq, hd + 1)
                for half in range(2):
                    last = nc.tensor.matmul(banks[4 + half][0:4, 0:HALF], onecol[:, hd, :],
                                            sqh[hd][:, half * HALF:(half + 1) * HALF],
                                            start=(hd == 0), stop=(hd == MH - 1))
                return last

            for hd in range(MH):
                if hd >= 2:
                    pe.wait_ge(s_hc, hd - 1)
                for half in range(2):
                    last = nc.tensor.matmul(banks[2 * (hd % 2) + half][:, 0:HALF], ones[:, :],
                                            xn[:, hd, half * HALF:(half + 1) * HALF], start=True, stop=True)
                last.then_inc(s_mu, 1)
                if hd:
                    variance(hd - 1)
            variance(MH - 1).then_inc(s_var, 1)
            pe.wait_ge(s_sd, 1)
            for hd in range(MH):
                if hd >= 2:
                    pe.wait_ge(s_hn, hd - 1)
                for half in range(2):
                    last = nc.tensor.matmul(banks[2 * (hd % 2) + half][:, 0:HALF], head_row(4, hd),
                                            vrow[:, half * HALF:(half + 1) * HALF], start=True, stop=True)
                last.then_inc(s_bc, 1)

        @block.vector
        def _(dve):
            v = nc.vector
            for hd in range(MH):
                dve.wait_ge(s_mu, hd + 1)
                for half in range(2):
                    c = slice(half * HALF, (half + 1) * HALF)
                    last = v.scalar_tensor_tensor(out=xn[:, hd, c], in0=banks[2 * (hd % 2) + half][:, 0:HALF],
                                                  scalar=-1.0 / 128, in1=xn[:, hd, c], op0=ALU.mult, op1=ALU.add)
                last.then_inc(s_hc, 1)
            dve.wait_ge(s_var, 1)
            for half in range(2):
                v.tensor_scalar(vrow[:, half * HALF:(half + 1) * HALF], banks[4 + half][0:4, 0:HALF],
                                1.0 / 128, EPS, ALU.mult, ALU.add)
            v.drain()
            v.reciprocal(vrow, vrow).then_inc(s_iv, 1)
            recurrence_inputs(dve, v)
            for c in range(4):
                recurrence(v, c)
            for hd in range(MH):
                dve.wait_ge(s_bc, hd + 1)
                for half in range(2):
                    c = slice(half * HALF, (half + 1) * HALF)
                    last = v.scalar_tensor_tensor(out=xn[:, hd, c], in0=xn[:, hd, c], scalar=cols[:, LNG + hd:LNG + hd + 1],
                                                  in1=banks[2 * (hd % 2) + half][:, 0:HALF], op0=ALU.mult, op1=ALU.mult)
                last.then_inc(s_hn, 1)
            v.drain()
            v.tensor_copy(fin[:, 0, 0:4], hs[:, :, TP - 1])
            for c in range(4):
                v.tensor_copy(fin[:, 1, c * NB:(c + 1) * NB], hs[:, c, TP:T].rearrange("p (b t) -> p b t", t=TS)[:, :, TS - 1])
                v.tensor_copy(fin2[:, c, 0:3], lx[:, c, TP - 3:TP])
                v.tensor_copy(fin2[:, c, 3:27].rearrange("p (b j) -> p b j", j=3), us[:, c, :, 4:7])

        @block.scalar
        def _(act):
            for c in range(4):
                nc.scalar.activation(ga[:, c, :], ga[:, c, :], ACT.Exp, scale=lam[:, 3, c:c + 1]).then_inc(s_a, 1)
            for hd in range(MH):
                act.wait_ge(s_hc, hd + 1)
                nc.scalar.activation(sqh[hd], xn[:, hd, :], ACT.Square).then_inc(s_sq, 1)
            for c in range(4):
                nc.scalar.activation(gt[:, c, :], gt[:, c, :], ACT.Sqrt).then_inc(s_r, 1)
            act.wait_ge(s_iv, 1)
            nc.scalar.activation(vrow, vrow, ACT.Sqrt).then_inc(s_sd, 1)

        @block.gpsimd
        def _(pool):
            for c in range(4):
                pool.wait_ge(s_h, c + 1)
                nc.gpsimd.tensor_tensor(xn[:, 4 + c, :], hs[:, c, :], lgate[:, c, :], ALU.mult)
            for hd in range(MH):
                pool.wait_ge(s_hn, hd + 1)
                nc.gpsimd.tensor_tensor(xn[:, hd, :], xn[:, hd, :], rg[:, hd, :], ALU.mult)

    orow = flat(rv)[0:32, 0:2 * 128]
    crow = [flat(rv)[0:24, 256 + 512 * i:256 + 512 * (i + 1)] for i in range(2)]
    jobs = [([(fin[:, 0, 0:4], 0)], lambda cp_, bank: cp_(orow[0:4, 0:128], bank[0:4, 0:128])),
            ([(fin[:, 1, :], 0)], lambda cp_, bank: cp_(orow[0:32, 128:256], bank[0:32, 0:128])),
            ([(fin2[:, c, 0:3], c * 128) for c in range(4)], lambda cp_, bank: cp_(crow[0][0:3, :], bank[0:3, :])),
            ([(fin2[:, c, 3:27], c * 128) for c in range(4)], lambda cp_, bank: cp_(crow[1][0:24, :], bank[0:24, :]))]
    s_lo = sem("lru_stored")
    before = list(tr_n)

    def store_lru(sp):
        for e in range(2):
            sp.wait_ge(tr_free[e], before[e] + 2)
        sp.dma_start(io["p_lru_h"].rearrange("b (k p) -> (b k) p", p=128), orow[0:4, 0:128]).then_inc(s_lo, 16)
        for c in range(4):
            sp.dma_start(io["s_lru_h"][:, c * 128:(c + 1) * 128], orow[c * NB:(c + 1) * NB, 128:256]).then_inc(s_lo, 16)
        sp.dma_start(io["p_lru_conv"][0], crow[0][0:3, :]).then_inc(s_lo, 16)
        sp.dma_start(io["s_lru_conv"].rearrange("b j n -> (b j) n"), crow[1][0:24, :]).then_inc(s_lo, 16)
        sp.wait_ge(s_lo, 16 * 7)
    transposes(jobs, store_lru)

    inner_top.close()
    close_layer(1, (out_odd, None))

    with ExitStack() as scratch_:
        norm(ffn_out, (1, 3), None, place(scratch_, "squares", [128, KC, T]))
    right.close()

    yt = place(left, "tokens_out", [128, 6, D])
    jobs = []
    for b, (t0, n) in enumerate(BLK):
        for kk in range(0, KC, 4):
            jobs.append(([(h[:, kk + j, t0:t0 + n], j * 128) for j in range(4)],
                         lambda cp_, bank, kk=kk, b=b, n=n: cp_(yt[0:n, b, kk * 128:(kk + 4) * 128], bank[0:n, :])))
    s_y = sem("y_stored")
    yn = list(tr_n)

    def store_y(sp):
        yp = io["y_prompt"][0]
        for b, (t0, n) in enumerate(BLK):
            for e in range(2):
                sp.wait_ge(tr_free[e], yn[e] + b + 1)
            if b == SB:
                out = io["y_sample"].rearrange("b t d -> (b t) d")
            else:
                out = yp[max(t0 - META, 0):t0 + n - META]
            sp.dma_start(out, yt[META if b == 0 else 0:n, b, :]).then_inc(s_y, 16)
        sp.wait_ge(s_y, 16 * len(BLK))
    transposes(jobs, store_y)

    left.close()
    ctx.close()


_OUTS = [("y_prompt", (1, SEQ, D)), ("y_sample", (NB, TS, D)),
         ("p_fox_k", (1, TP, FH, FD)), ("p_fox_v", (1, TP, FH, FD)), ("p_fox_logf", (1, TP, FH)),
         ("s_fox_k", (NB, TS, FH, FD)), ("s_fox_v", (NB, TS, FH, FD)), ("s_fox_logf", (NB, TS, FH)),
         ("p_mlstm_C", (1, MH, 128, 128)), ("p_mlstm_n", (1, MH, 128)), ("p_mlstm_m", (1, MH)),
         ("s_mlstm_C", (NB, MH, 128, 128)), ("s_mlstm_n", (NB, MH, 128)), ("s_mlstm_m", (NB, MH)),
         ("p_ret_S", (1, MH, 128, 128)), ("s_ret_S", (NB, MH, 128, 128)),
         ("p_lru_h", (1, LW)), ("s_lru_h", (NB, LW)), ("p_lru_conv", (1, 3, LW)), ("s_lru_conv", (NB, 3, LW))]


def kernel(**inputs):
    import concourse.bacc as bacc
    from concourse.bass_utils import run_bass_kernel_spmd

    nc = bacc.Bacc("TRN2", target_bir_lowering=False, num_devices=1)
    arrays, io = {}, {}
    for name, a in list(inputs.items()) + [("c_" + k, v) for k, v in constants().items()]:
        a = np.ascontiguousarray(a)
        arrays["in_" + name] = a
        io[name] = nc.dram_tensor("in_" + name, a.shape, mybir.dt.from_np(a.dtype), kind="ExternalInput").ap()
    for name, shape in _OUTS:
        io[name] = nc.dram_tensor("out_" + name, shape, F32, kind="ExternalOutput").ap()
    hybrid_decoder(nc, io)
    r = run_bass_kernel_spmd(nc, [arrays], core_ids=[0])
    return tuple(r.results[0]["out_" + name] for name, _ in _OUTS)
```
